# Optimizing a Trainium2 kernel written in Bass

```python
import jax, jax.numpy as jnp
from jax import lax
import numpy as np

D_MODEL = 1024
BATCH = 1
SEQ = 128
DEPTH = 2
DEC_BATCH = 1
DEC_SEQ = 512
PAST_LEN = 256

GRID_W = 64
GLA_HEADS = 4
GLA_DV = D_MODEL // 8
GLA_DK = GLA_DV // 2
GLA_RANK = 16
GLA_TAU = 16.0
GLA_CHUNK = 32
GMLP_CHUNK = 128
GMLP_CH = 128
GMLP_GROUPS = (D_MODEL // 2) // GMLP_CH
ATTN_HEADS = 8
ATTN_KV_HEADS = 2
ATTN_HEAD_DIM = 64
ATTN_GROUP = ATTN_HEADS // ATTN_KV_HEADS
WINDOW = 128
ATTN_BLOCK = 128
ROPE_BASE = 10000.0
BRANCH_W = D_MODEL // 2
N_BRANCH = 3
N_GROUPS = 4
EXPERTS_PER_GROUP = 4
N_EXPERTS = N_GROUPS * EXPERTS_PER_GROUP
TOP_K_IN_GROUP = 2
EXPERT_FF = D_MODEL // 4
LN_EPS = 1e-5
IN_WIDTHS = (GLA_HEADS * GLA_DK, GLA_HEADS * GLA_DK, GLA_HEADS * GLA_DV, GLA_HEADS * GLA_DV,
             GLA_RANK, GLA_RANK, 2 * GMLP_GROUPS * GMLP_CH,
             ATTN_HEADS * ATTN_HEAD_DIM, ATTN_KV_HEADS * ATTN_HEAD_DIM, ATTN_KV_HEADS * ATTN_HEAD_DIM,
             N_BRANCH * D_MODEL)
IN_COLS = sum(IN_WIDTHS)

kernel_name = "hybrid_gla_gmlp_swa_hmoe_diffusion_step"

F32 = jnp.float32

def split_cols(x, widths):
    out, start = [], 0
    for w in widths:
        out.append(x[..., start:start + w])
        start += w
    return out

def layer_norm(x, g, b):
    xf = x.astype(F32)
    mu = jnp.mean(xf, axis=-1, keepdims=True)
    xc = xf - mu
    var = jnp.mean(xc * xc, axis=-1, keepdims=True)
    return (xc * lax.rsqrt(var + LN_EPS) * g.astype(F32) + b.astype(F32)).astype(x.dtype)

def axial_rope(x, row_pos, col_pos):
    half = x.shape[-1] // 2
    quarter = half // 2
    inv_freq = jnp.power(ROPE_BASE, -jnp.arange(quarter, dtype=F32) / quarter)

    def rotate(xh, pos):
        ang = pos[:, None] * inv_freq[None, :]
        cos = jnp.cos(ang)[None, :, None, :].astype(x.dtype)
        sin = jnp.sin(ang)[None, :, None, :].astype(x.dtype)
        x1, x2 = xh[..., :quarter], xh[..., quarter:]
        return jnp.concatenate([x1 * cos - x2 * sin, x1 * sin + x2 * cos], axis=-1)

    return jnp.concatenate([rotate(x[..., :half], row_pos), rotate(x[..., half:], col_pos)], axis=-1)

def gla_log_decay(lr, w2, b2):
    B, L, _ = lr.shape
    z = (lr @ w2 + b2).astype(F32)
    return (jax.nn.log_sigmoid(z) / GLA_TAU).reshape(B, L, GLA_HEADS, GLA_DK)

def gla_chunked(q, k, v, log_a, s0):
    B, L, H, DK = q.shape
    DV = v.shape[-1]
    C = GLA_CHUNK
    N = L // C
    q = q.astype(F32).reshape(B, N, C, H, DK) * (DK ** -0.5)
    k = k.astype(F32).reshape(B, N, C, H, DK)
    v = v.astype(F32).reshape(B, N, C, H, DV)
    b = jnp.cumsum(log_a.reshape(B, N, C, H, DK), axis=2)
    tri = jnp.tril(jnp.ones((C, C), dtype=bool))
    diff = b[:, :, :, None] - b[:, :, None, :]
    decay = jnp.exp(jnp.where(tri[None, None, :, :, None, None], diff, -jnp.inf))
    scores = jnp.einsum('bnthd,bnshd,bntshd->bnhts', q, k, decay)
    intra = jnp.einsum('bnhts,bnshv->bnthv', scores, v)
    b_last = b[:, :, -1]
    kv_chunk = jnp.einsum('bnshd,bnshv->bnhdv', k * jnp.exp(b_last[:, :, None] - b), v)

    def step(S, inp):
        g, kv = inp
        return jnp.exp(g)[..., None] * S + kv, S

    s_fin, s_in = lax.scan(step, s0.astype(F32),
                           (jnp.moveaxis(b_last, 1, 0), jnp.moveaxis(kv_chunk, 1, 0)))
    s_in = jnp.moveaxis(s_in, 0, 1)
    inter = jnp.einsum('bnthd,bnhdv->bnthv', q * jnp.exp(b), s_in)
    return (intra + inter).reshape(B, L, H, DV), s_fin

def chunk_gmlp(z, ln_g, ln_b, w_s, b_s):
    B, L, _ = z.shape
    u, v = jnp.split(z, 2, axis=-1)
    v = layer_norm(v, ln_g, ln_b)
    v = v.reshape(B, L // GMLP_CHUNK, GMLP_CHUNK, GMLP_GROUPS, GMLP_CH)
    s = jnp.einsum('gts,bnsgc->bntgc', w_s, v) + b_s.T[None, None, :, :, None]
    return u * s.reshape(B, L, GMLP_GROUPS * GMLP_CH)

def context_attention(q, k, v, sink):
    B, S = q.shape[0], q.shape[1]
    nb = S // ATTN_BLOCK
    scale = ATTN_HEAD_DIM ** -0.5
    qb = q.reshape(B, nb, ATTN_BLOCK, ATTN_KV_HEADS, ATTN_GROUP, ATTN_HEAD_DIM).transpose(1, 0, 2, 3, 4, 5)
    sink_col = sink.astype(F32).reshape(ATTN_KV_HEADS, ATTN_GROUP)[None, :, :, None, None]

    def block(qi):
        s = jnp.einsum('bqkgd,bskd->bkgqs', qi, k).astype(F32) * scale
        sink_b = jnp.broadcast_to(sink_col, s.shape[:-1] + (1,))
        p = jax.nn.softmax(jnp.concatenate([s, sink_b], axis=-1), axis=-1)[..., :-1]
        return jnp.einsum('bkgqs,bskd->bqkgd', p.astype(v.dtype), v)

    o = lax.map(block, qb)
    return o.transpose(1, 0, 2, 3, 4, 5).reshape(B, S, ATTN_HEADS * ATTN_HEAD_DIM)

def latent_window_attention(q, k, v, k_ctx, v_ctx, sink):
    B, L = q.shape[0], q.shape[1]
    wb = ATTN_BLOCK
    nb = L // wb
    scale = ATTN_HEAD_DIM ** -0.5
    qb = q.reshape(B, nb, wb, ATTN_KV_HEADS, ATTN_GROUP, ATTN_HEAD_DIM)

    def neighbours(t):
        tb = jnp.pad(t, ((0, 0), (wb, wb), (0, 0), (0, 0))).reshape(
            B, nb + 2, wb, ATTN_KV_HEADS, ATTN_HEAD_DIM)
        return jnp.concatenate([tb[:, :-2], tb[:, 1:-1], tb[:, 2:]], axis=2)

    kn, vn = neighbours(k), neighbours(v)
    s_loc = jnp.einsum('bnqkgd,bnskd->bnkgqs', qb, kn).astype(F32) * scale
    s_ctx = jnp.einsum('bnqkgd,bskd->bnkgqs', qb, k_ctx).astype(F32) * scale
    blk = jnp.arange(nb)[:, None, None]
    q_pos = blk * wb + jnp.arange(wb)[None, :, None]
    k_pos = (blk - 1) * wb + jnp.arange(3 * wb)[None, None, :]
    valid = (jnp.abs(k_pos - q_pos) <= WINDOW) & (k_pos >= 0) & (k_pos < L)
    s_loc = jnp.where(valid[None, :, None, None], s_loc, -jnp.inf)
    sink_col = jnp.broadcast_to(
        sink.astype(F32).reshape(ATTN_KV_HEADS, ATTN_GROUP)[None, None, :, :, None, None],
        s_loc.shape[:-1] + (1,))
    p = jax.nn.softmax(jnp.concatenate([s_loc, s_ctx, sink_col], axis=-1), axis=-1).astype(v.dtype)
    n_loc = 3 * wb
    n_ctx = k_ctx.shape[1]
    o = (jnp.einsum('bnkgqs,bnskd->bnqkgd', p[..., :n_loc], vn)
         + jnp.einsum('bnkgqs,bskd->bnqkgd', p[..., n_loc:n_loc + n_ctx], v_ctx))
    return o.reshape(B, L, ATTN_HEADS * ATTN_HEAD_DIM)

def hier_moe(h, rg_w, rg_b, re_w, re_b, w_gate, w_up, w_down):
    B, L, D = h.shape
    T = B * L
    t = h.reshape(T, D)
    rows = jnp.arange(T)
    g_prob = jax.nn.softmax((t @ rg_w + rg_b).astype(F32), axis=-1)
    g_p, g_i = lax.top_k(g_prob, 1)
    e_logits = (t @ re_w + re_b).astype(F32).reshape(T, N_GROUPS, EXPERTS_PER_GROUP)
    e_prob = jax.nn.softmax(e_logits[rows, g_i[:, 0]], axis=-1)
    e_p, e_i = lax.top_k(e_prob, TOP_K_IN_GROUP)
    w = g_p * e_p / jnp.sum(e_p, axis=-1, keepdims=True)
    ids = g_i * EXPERTS_PER_GROUP + e_i
    combine = jnp.zeros((T, N_EXPERTS), F32).at[rows[:, None], ids].add(w).astype(h.dtype)
    hid = jax.nn.silu(jnp.einsum('td,edf->tef', t, w_gate)) * jnp.einsum('td,edf->tef', t, w_up)
    y = jnp.einsum('tef,efd->td', hid * combine[:, :, None], w_down)
    return y.reshape(B, L, D)

def trunk_layer(x, cond, lp, alpha, ctx):
    B, L, _ = x.shape
    mod = (jax.nn.silu(cond) @ lp["ada_w"] + lp["ada_b"])[:, None, :]
    sh_a, sc_a, gt_a, sh_m, sc_m, gt_m = jnp.split(mod, 6, axis=-1)
    h = x * (1 + sc_a) + sh_a
    aq, ak, av, ag, alr_f, alr_b, bz, cq, ck, cv, mg = split_cols(h @ lp["w_in"], IN_WIDTHS)

    aq = aq.reshape(B, L, GLA_HEADS, GLA_DK)
    ak = ak.reshape(B, L, GLA_HEADS, GLA_DK)
    av = av.reshape(B, L, GLA_HEADS, GLA_DV)
    log_f = gla_log_decay(alr_f, lp["gla_gate_w"][0], lp["gla_gate_b"][0])
    log_b = gla_log_decay(alr_b, lp["gla_gate_w"][1], lp["gla_gate_b"][1])
    if ctx is None:
        s0_f = jnp.zeros((B, GLA_HEADS, GLA_DK, GLA_DV), F32)
        s0_b = s0_f
    else:
        s0_f, s0_b, k_ctx, v_ctx = ctx
    o_f, s_f = gla_chunked(aq, ak, av, log_f, s0_f)
    o_b, s_b = gla_chunked(aq[:, ::-1], ak[:, ::-1], av[:, ::-1], log_b[:, ::-1], s0_b)
    o = o_f + o_b[:, ::-1]
    o = o * lax.rsqrt(jnp.mean(o * o, axis=-1, keepdims=True) + LN_EPS) \
        * lp["gla_norm_g"].astype(F32).reshape(GLA_HEADS, GLA_DV)
    br_a = o.reshape(B, L, GLA_HEADS * GLA_DV).astype(x.dtype) * jax.nn.silu(ag)

    br_b = chunk_gmlp(jax.nn.gelu(bz), lp["gmlp_ln_g"], lp["gmlp_ln_b"], lp["gmlp_ws"], lp["gmlp_bs"])

    cq = cq.reshape(B, L, ATTN_HEADS, ATTN_HEAD_DIM)
    ck = ck.reshape(B, L, ATTN_KV_HEADS, ATTN_HEAD_DIM)
    cv = cv.reshape(B, L, ATTN_KV_HEADS, ATTN_HEAD_DIM)
    if ctx is None:
        br_c = context_attention(cq, ck, cv, lp["attn_sink"])
    else:
        n_rows = L // GRID_W
        row_pos = jnp.repeat(jnp.arange(n_rows, dtype=F32), GRID_W)
        col_pos = (jnp.arange(n_rows * GRID_W) % GRID_W).astype(F32)
        br_c = latent_window_attention(axial_rope(cq, row_pos, col_pos), axial_rope(ck, row_pos, col_pos),
                                       cv, k_ctx, v_ctx, lp["attn_sink"])

    branches = jnp.stack([br_a, br_b, br_c], axis=2)
    proj = jnp.einsum('blnc,ncd->blnd', branches, lp["w_branch"])
    gates = jax.nn.sigmoid(mg).reshape(B, L, N_BRANCH, D_MODEL)
    y = jnp.sum(gates * proj, axis=2) @ lp["w_out"]
    x = layer_norm(alpha * x + gt_a * y, lp["ln1_g"], lp["ln1_b"])

    h2 = x * (1 + sc_m) + sh_m
    y2 = hier_moe(h2, lp["router_group_w"], lp["router_group_b"], lp["router_expert_w"],
                  lp["router_expert_b"], lp["expert_w_gate"], lp["expert_w_up"], lp["expert_w_down"])
    x = layer_norm(alpha * x + gt_m * y2, lp["ln2_g"], lp["ln2_b"])
    if ctx is None:
        return x, (s_f.astype(x.dtype), s_b.astype(x.dtype), ck, cv)
    return x, None

def setup_inputs(seed: int = 0) -> dict:
    key = jax.random.key(seed)
    ks = jax.random.split(key, 40)
    D = D_MODEL
    beta = (8.0 * DEPTH) ** -0.25

    def nrm(k, shape, scale):
        return jax.random.normal(k, shape, F32) * scale

    return {
        "x_prompt": nrm(ks[0], (BATCH, SEQ, D), 1.0),
        "x_sample": nrm(ks[1], (DEC_BATCH, DEC_SEQ, D), 1.0),
        "state_gla": nrm(ks[2], (DEC_BATCH, DEPTH, 2, GLA_HEADS, GLA_DK, GLA_DV), 1.0),
        "cache_k": nrm(ks[3], (DEC_BATCH, DEPTH, PAST_LEN, ATTN_KV_HEADS, ATTN_HEAD_DIM), 1.0),
        "cache_v": nrm(ks[4], (DEC_BATCH, DEPTH, PAST_LEN, ATTN_KV_HEADS, ATTN_HEAD_DIM), 1.0),
        "c": nrm(ks[5], (DEC_BATCH, D), 1.0),
        "c_ctx": nrm(ks[6], (D,), 1.0),
        "ada_w": nrm(ks[7], (DEPTH, D, 6 * D), D ** -0.5),
        "ada_b": nrm(ks[8], (DEPTH, 6 * D), 0.02),
        "w_in": nrm(ks[9], (DEPTH, D, IN_COLS), D ** -0.5),
        "gla_gate_w": nrm(ks[10], (DEPTH, 2, GLA_RANK, GLA_HEADS * GLA_DK), GLA_RANK ** -0.5),
        "gla_gate_b": nrm(ks[11], (DEPTH, 2, GLA_HEADS * GLA_DK), 0.1),
        "gla_norm_g": 1.0 + nrm(ks[12], (DEPTH, GLA_HEADS * GLA_DV), 0.02),
        "gmlp_ln_g": 1.0 + nrm(ks[13], (DEPTH, GMLP_GROUPS * GMLP_CH), 0.02),
        "gmlp_ln_b": nrm(ks[14], (DEPTH, GMLP_GROUPS * GMLP_CH), 0.02),
        "gmlp_ws": nrm(ks[15], (DEPTH, GMLP_GROUPS, GMLP_CHUNK, GMLP_CHUNK), GMLP_CHUNK ** -0.5),
        "gmlp_bs": 1.0 + nrm(ks[16], (DEPTH, GMLP_GROUPS, GMLP_CHUNK), 0.02),
        "attn_sink": nrm(ks[17], (DEPTH, ATTN_HEADS), 1.0),
        "w_branch": nrm(ks[18], (DEPTH, N_BRANCH, BRANCH_W, D), BRANCH_W ** -0.5 * beta),
        "w_out": nrm(ks[19], (DEPTH, D, D), D ** -0.5 * beta),
        "ln1_g": 1.0 + nrm(ks[20], (DEPTH, D), 0.02),
        "ln1_b": nrm(ks[21], (DEPTH, D), 0.02),
        "ln2_g": 1.0 + nrm(ks[22], (DEPTH, D), 0.02),
        "ln2_b": nrm(ks[23], (DEPTH, D), 0.02),
        "router_group_w": nrm(ks[24], (DEPTH, D, N_GROUPS), D ** -0.5),
        "router_group_b": nrm(ks[25], (DEPTH, N_GROUPS), 0.01),
        "router_expert_w": nrm(ks[26], (DEPTH, D, N_EXPERTS), D ** -0.5),
        "router_expert_b": nrm(ks[27], (DEPTH, N_EXPERTS), 0.01),
        "expert_w_gate": nrm(ks[28], (DEPTH, N_EXPERTS, D, EXPERT_FF), D ** -0.5),
        "expert_w_up": nrm(ks[29], (DEPTH, N_EXPERTS, D, EXPERT_FF), D ** -0.5 * beta),
        "expert_w_down": nrm(ks[30], (DEPTH, N_EXPERTS, EXPERT_FF, D), EXPERT_FF ** -0.5 * beta),
    }

def reference(x_prompt, x_sample, state_gla, cache_k, cache_v, c, c_ctx, ada_w, ada_b, w_in,
              gla_gate_w, gla_gate_b, gla_norm_g, gmlp_ln_g, gmlp_ln_b, gmlp_ws, gmlp_bs, attn_sink,
              w_branch, w_out, ln1_g, ln1_b, ln2_g, ln2_b, router_group_w, router_group_b,
              router_expert_w, router_expert_b, expert_w_gate, expert_w_up, expert_w_down):
    alpha = (2.0 * DEPTH) ** 0.25
    xp, xs = x_prompt, x_sample
    states, keys, values = [], [], []
    for l in range(DEPTH):
        lp = {
            "ada_w": ada_w[l], "ada_b": ada_b[l], "w_in": w_in[l],
            "gla_gate_w": gla_gate_w[l], "gla_gate_b": gla_gate_b[l], "gla_norm_g": gla_norm_g[l],
            "gmlp_ln_g": gmlp_ln_g[l], "gmlp_ln_b": gmlp_ln_b[l], "gmlp_ws": gmlp_ws[l],
            "gmlp_bs": gmlp_bs[l], "attn_sink": attn_sink[l], "w_branch": w_branch[l],
            "w_out": w_out[l], "ln1_g": ln1_g[l], "ln1_b": ln1_b[l], "ln2_g": ln2_g[l],
            "ln2_b": ln2_b[l], "router_group_w": router_group_w[l], "router_group_b": router_group_b[l],
            "router_expert_w": router_expert_w[l], "router_expert_b": router_expert_b[l],
            "expert_w_gate": expert_w_gate[l], "expert_w_up": expert_w_up[l],
            "expert_w_down": expert_w_down[l],
        }
        xp, (s_f, s_b, k_l, v_l) = trunk_layer(xp, c_ctx[None, :], lp, alpha, None)
        states.append(jnp.stack([s_f, s_b], axis=1))
        keys.append(k_l)
        values.append(v_l)
        xs, _ = trunk_layer(xs, c, lp, alpha,
                            (state_gla[:, l, 0], state_gla[:, l, 1], cache_k[:, l], cache_v[:, l]))
    new_state_gla = jnp.stack(states, axis=1)
    new_cache_k = jnp.stack(keys, axis=1)
    new_cache_v = jnp.stack(values, axis=1)
    return (xp, xs, new_state_gla, new_cache_k, new_cache_v)


_drawn_inputs = setup_inputs


def setup_inputs(seed=0):
    import zlib

    import numpy as np

    out = dict(_drawn_inputs(seed))
    spreads = {}
    factors = {'state_gla': 8.0,
     'cache_k': 8.0,
     'cache_v': 8.0,
     'gla_norm_g': 35.618,
     'gmlp_ln_g': 30.39,
     'gmlp_ln_b': 33.368,
     'gmlp_bs': 34.551,
     'attn_sink': 8.0,
     'router_group_b': 28.279,
     'router_expert_b': 31.667}
    for name, (base, spread) in spreads.items():
        noise = np.random.default_rng([zlib.crc32(name.encode()), seed]).standard_normal(out[name].shape)
        drawn = base * np.exp(spread * noise) if base else spread * noise
        out[name] = __import__('jax').numpy.asarray(drawn.astype(out[name].dtype))
    for name, factor in factors.items():
        out[name] = (out[name] * factor).astype(out[name].dtype)
    return out
```

```python
from contextlib import ExitStack

import numpy as np
import concourse.bass as bass
from concourse import mybir

F32, I32 = mybir.dt.float32, mybir.dt.int32
ALU, ACT, AXL = mybir.AluOpType, mybir.ActivationFunctionType, mybir.AxisListType

P = 128
D = 1024
KD = D // P
DEPTH = 2
T = 5
TOK = T * P
HALF = TOK // 2
CTX = 256
GRID_W = 64
GLA_H, DK, DV, RANK = 4, 64, 128, 16
PAIRS = GLA_H // 2
GLA_TAU = 16.0
HEADS, KV_HEADS, HD = 8, 2, 64
EPS = 1e-5
ALPHA = (2.0 * DEPTH) ** 0.25
NG, EG = 4, 4
NE = NG * EG
FF = D // 4
LOGITS = NG + NE
TILES = 26
BIG = 1e30

C_AQ, C_AK, C_AV, C_AG, C_LR, C_U, C_V, C_CQ, C_CK, C_MG = 0, 256, 512, 1024, 1536, 1568, 2080, 2592, 3104, 3360
V_ADA, V_NORM, V_GB, V_ROWS = 0, 48, 52, 56

UNITS = T * HEADS
RING = 6
BLK = 2048


def build_tables():
    jobs, blocks = [], []

    def job(eng, *key):
        jobs.append((key, eng))

    def block(name, last):
        blocks.append((name, last))

    job("D", "vec")
    for b in range(24):
        job("D", "mod", b)
        block(("ada", b), ("mod", b))
    for k in range(KD):
        job("A" if k % 2 else "D", "hT", k)
    job("A", "lr")
    block(("win", C_LR, 32), ("lr",))
    for c in range(2):
        job("A", "aq", c)
    block(("win", C_AQ, 256), ("aq", 1))
    for c in range(2):
        job("D", "ak", c)
    block(("win", C_AK, 256), ("ak", 1))
    for c in range(4):
        job("D", "z", c)
        name, col = ("vtok", C_V) if c < 2 else ("av", C_AV)
        for t in range(T):
            job("A", name, c % 2, t)
        block(("win", col + 256 * (c % 2), 256), (name, c % 2, T - 1))
    for c in range(4):
        job("A", "ag", c)
        if c % 2:
            block(("win", C_AG + 128 * (c - 1), 256), ("ag", c))
    for c in range(4):
        job("A", "u", c)
        if c % 2:
            block(("win", C_U + 128 * (c - 1), 256), ("u", c))
    for c in range(4):
        job("D", "cq", c)
        if c % 2:
            block(("win", C_CQ + 128 * (c - 1), 256), ("cq", c))
    for t in range(T):
        job("D", "ckv", t)
    block(("win", C_CK, 256), ("ckv", T - 1))
    job("A", "wsT")
    job("A", "kcT")
    for g in range(KV_HEADS):
        job("D", "kT", g)
    for c in range(4 + KV_HEADS):
        job("D", "rot", c)
    for g in range(4):
        job("D", "mix", g)
    for c in range(5):
        if c < 4:
            job("A", "ktok", c)
        if c:
            job("D", "kv", c - 1)
    for p in range(PAIRS):
        for t in range(T + 1):
            if t < T:
                job("D", "gs", p, t)
            if t:
                job("A", "o", p, t - 1)
    for h in range(GLA_H):
        job("A", "ms", h)
    for i in range(UNITS + 3):
        if i < UNITS:
            job("A", "s", i)
        if 1 <= i <= UNITS:
            job("A", "pT", i - 1)
        if i >= 3 and i % 2:
            job("D", "pv", (i - 3) // 2)
    for half in range(2):
        for n in range(3):
            for q in range(4):
                job("A", "gate", half, n, q)
                job("D", "proj", half, n, q)
            block(("wb", half, n), ("proj", half, n, 3))
            block(("mg", half, n, 0), ("gate", half, n, 1))
            block(("mg", half, n, 1), ("gate", half, n, 3))
    for v in range(6):
        job("A", "row", v)
    for cb in range(4):
        for t in range(T):
            job("D", "y", cb, t)
        block(("wout", cb), ("y", cb, T - 1))
    for k in range(KD):
        job("A", "h2T", k)
    job("D", "logit")
    job("D", "rank")
    for v in range(6, 8):
        job("A", "row", v)
    job("D", "xg", 0)
    assert len(blocks) % RING == 0
    moe_job, moe_block = len(jobs), len(blocks)
    for j in range(TILES):
        job("D", "gu", j)
        job("D", "xg", j + 1)
        job("A", "ht", j)
        job("A", "dn", j)
        block(("gate", j), ("gu", j))
        block(("up", j), ("gu", j))
        block(("down", j), ("dn", j))
    number = {}
    moved = {}
    count = {"A": 0, "D": 0}
    for n, (key, eng) in enumerate(jobs):
        count[eng] += 1
        number[key] = n
        moved[key] = (eng, count[eng])
    assert len(blocks) % RING == 0
    return jobs, number, moved, count, blocks, moe_job, moe_block


JOBS, NUMBER, MOVED, TOTAL, BLOCKS, MOE_JOB, MOE_BLOCK = build_tables()
NJ, NB = len(JOBS), len(BLOCKS)
BLOCK_NO = {name: n for n, (name, _) in enumerate(BLOCKS)}
PER_TILE = (NJ - MOE_JOB) // TILES

CONST, _at = {}, 0
for _name, _width in (("ident", P), ("ones", P), ("before", P), ("gla_mask", 2 * P), ("att_mask", 2 * P), ("swap", P),
                      ("cos", 4 * P), ("sin", 4 * P), ("run", TOK), ("eps", 1), ("over", 5), ("first", 4),
                      ("tile", TILES)):
    CONST[_name] = (_at, _width)
    _at += _width
CONST_W = _at


def const_tile():
    c = np.zeros((P, CONST_W), np.float32)
    r, q = np.arange(P)[:, None], np.arange(P)[None, :]

    def put(name, values):
        at, width = CONST[name]
        c[:, at:at + width] = values

    put("ident", r == q)
    put("ones", 1.0)
    put("before", r < q)
    put("gla_mask", np.concatenate([r <= q, r >= q], 1))
    put("att_mask", np.where(np.concatenate([q >= r, q <= r], 1), 0.0, -BIG))
    quarter = HD // 4
    swap = np.zeros((P, P), np.float32)
    for base in range(0, P, 2 * quarter):
        for i in range(quarter):
            swap[base + quarter + i, base + i] = -1.0
            swap[base + i, base + quarter + i] = 1.0
    put("swap", swap)
    freq = np.power(np.float32(10000.0), -np.arange(quarter, dtype=np.float32) / np.float32(quarter)).astype(np.float32)
    tok = np.arange(4 * P)
    row, col = (tok // GRID_W).astype(np.float32), (tok % GRID_W).astype(np.float32)
    ang = np.stack([(row if d % HD < HD // 2 else col) * freq[d % quarter] for d in range(P)]).astype(np.float32)
    put("cos", np.cos(ang))
    put("sin", np.sin(ang))
    put("run", np.broadcast_to((np.arange(TOK) % P != 0), (P, TOK)))
    put("eps", EPS)
    put("over", P * np.arange(5.0)[None, :])
    put("first", np.arange(4.0, 0.0, -1.0)[None, :])
    put("tile", np.arange(float(TILES))[None, :])
    return c


_INS = ["x_prompt", "x_sample", "state_gla", "cache_k", "cache_v", "c", "c_ctx", "ada_w", "ada_b", "w_in",
        "gla_gate_w", "gla_gate_b", "gla_norm_g", "gmlp_ln_g", "gmlp_ln_b", "gmlp_ws", "gmlp_bs", "attn_sink",
        "w_branch", "w_out", "ln1_g", "ln1_b", "ln2_g", "ln2_b", "router_group_w", "router_group_b",
        "router_expert_w", "router_expert_b", "expert_w_gate", "expert_w_up", "expert_w_down"]
_OUTS = [("y", (TOK, D)), ("new_state", (DEPTH, 2, GLA_H, DK, DV)), ("new_k", (DEPTH, P, P)), ("new_v", (DEPTH, P, P))]



def build_program(nc, A):
    with ExitStack() as ctx:
        def sb(name, width, dt=F32, parts=P):
            return ctx.enter_context(nc.sbuf_tensor(name, [parts, width], dt))

        per_layer = []

        def sem(name):
            per_layer.append(ctx.enter_context(nc.semaphore(name)))
            return per_layer[-1]

        const = sb("const", CONST_W)
        hT = sb("hT", KD * TOK)
        ring = sb("ring", RING * BLK)
        br = sb("br", 12 * TOK)
        mg = sb("mg", KD * TOK)
        xr = sb("xr", T * D)
        ar = sb("ar", 11904)
        vst = sb("vst", P)
        vec = sb("vec", 72)
        mod = sb("mod", 96)
        cs = sb("cs", 16)
        w2 = sb("w2", 512, parts=32)
        wsT = sb("wsT", 4 * P)
        bsb = sb("bsb", 4 * P)
        sink = sb("sink", 2 * HEADS)
        rw = sb("rw", KD * LOGITS)
        rb = sb("rb", LOGITS)
        st = sb("st", 64)
        er = sb("er", 4 * 15)
        sm = sb("sm", 16)

        def cst(name, parts=P):
            at, width = CONST[name]
            return const[0:parts, at:at + width]

        ident = cst("ident")
        eps = cst("eps")
        h3 = hT[:, :].rearrange("p (k t) -> p k t", k=KD)
        br3 = br[:, :].rearrange("p (k t) -> p k t", k=12)
        mg3 = mg[:, :].rearrange("p (k t) -> p k t", k=KD)
        x3 = xr[:, :].rearrange("p (t d) -> p t d", t=T)
        av = xr[:, 0:2560].rearrange("p (t c) -> p t c", t=T)
        vtok = xr[:, 2560:5120].rearrange("p (t c) -> p t c", t=T)
        oT = xr[:, 2560:5120].rearrange("p (h t) -> p h t", h=GLA_H)
        mod3 = mod[:, :].rearrange("p (f c) -> p f c", c=2)
        lng = br[:, 5120:5632]
        lnb = br[:, 5632:6144]
        zero = br[:, 0:D]
        aqk = ar[:, 0:2560].rearrange("p (c t) -> p c t", c=4)
        t1 = ar[:, 0:2560].rearrange("p (c t v) -> p c t v", c=4, t=T)
        pbuf = [ar[:, 640 * i:640 * (i + 1)] for i in range(2)]
        pTbuf = [ar[:, 1280 + 640 * i:1920 + 640 * i] for i in range(3)]
        bufA, bufM, bufB = (ar[:, 2560 + 640 * i:3200 + 640 * i] for i in range(3))
        gsb = [ar[:, 2560 + 512 * i:3072 + 512 * i] for i in range(2)]
        tmp5 = ar[:, 3584:4224]
        ktok = [ar[:, 4480 + 640 * i:5120 + 640 * i] for i in range(2)]
        kvt = ar[:, 5760:7040].rearrange("p (t c) -> p t c", t=T)
        kT = ar[:, 7040:8320].rearrange("p (g t) -> p g t", g=KV_HEADS)
        kcT = ar[:, 8320:8832].rearrange("p (g t) -> p g t", g=KV_HEADS)
        ckn = ar[:, 8832:9088].rearrange("p (a c) -> p a c", a=2)
        cvn = ar[:, 9088:9344].rearrange("p (a c) -> p a c", a=2)
        lr = ar[:, 9344:9984]
        sq = [ar[:, 9984 + 640 * i:10624 + 640 * i] for i in range(2)]
        wsn = ar[:, 9984:10496].rearrange("p (g s) -> p g s", g=4)
        spare = ar[:, 11264:11392]
        s0 = ar[:, 11392:11904].rearrange("p (c v) -> p c v", c=4)
        sig = sq
        gtmp = lr
        bcA = ar[:, 0:4096].rearrange("p (v d) -> p v d", v=4)
        bcB = ar[:, 4096:8192].rearrange("p (v d) -> p v d", v=4)
        ytmp = ar[:, 8192:8448]
        R = {}
        at = 8448
        for name, width in (("lg", T * LOGITS), ("ge", 20), ("G", 20), ("gx", 20), ("gm", 5), ("gs", 5), ("gp", 5),
                            ("es", 20), ("e2", 20), ("E1", 20), ("E2", 20), ("m1", 5), ("m2", 5), ("dq", 5),
                            ("w1", 5), ("w2", 5), ("big", 80), ("M1", 80), ("M2", 80), ("M", 80), ("rk", 96),
                            ("cmp", 80), ("nt", 16), ("end", 16), ("base", 16), ("pos", 10), ("ex", TILES),
                            ("exc", TILES * NE)):
            R[name] = ar[:, at:at + width]
            at += width
        posi = ctx.enter_context(nc.sbuf_tensor("posi", [P, 10], I32))
        exi = ctx.enter_context(nc.sbuf_tensor("exi", [P, TILES], I32))
        assert at <= 11904, at
        h2 = br[:, 0:T * D].rearrange("p (t d) -> p t d", t=T)
        yg = [br[:, D * i:D * (i + 1)] for i in range(2)]
        ys = [br[:, 5120 + D * i:5120 + D * (i + 1)] for i in range(2)]
        xgT = [mg[:, D * i:D * (i + 1)].rearrange("p (k s) -> p k s", k=KD) for i in range(2)]
        xg = [mg[:, 2048 + D * i:2048 + D * (i + 1)] for i in range(2)]
        silu, hid = mg[:, 4096:4352], mg[:, 4352:4608]
        hidT = [mg[:, 4608 + 256 * i:4864 + 256 * i].rearrange("p (f s) -> p f s", f=2) for i in range(2)]

        PS = ctx.enter_context(nc.psum_tensor("PS", [P, 4, 1024], F32))

        x_in = A["x"]
        y_out = A["y"]
        rows_in = A["rows_in"]
        rows_out = A["rows_out"]

        filled, act_moved, dve_moved = sem("filled"), sem("act_moved"), sem("dve_moved")
        landed = [sem(f"landed{i}") for i in range(RING)]
        const_in, x_first, zero_set, w2_zero, zeroed = (sem(n) for n in ("const_in", "x_first", "zero_set", "w2_zero", "zeroed"))
        params, x_landed, layer_done = sem("params"), sem("x_landed"), sem("layer_done")
        act_step, dve_step = sem("act_step"), sem("dve_step")
        cond_ready, mod_ready = sem("cond_ready"), sem("mod_ready")
        abs_done, softplus, decay_ready, exp_ready, qk_ready = (
            sem(n) for n in ("abs_done", "softplus", "decay_ready", "exp_ready", "qk_ready"))
        var_ready, std_ready, vn_ready = sem("var_ready"), sem("std_ready"), sem("vn_ready")
        rope_ready, states_in, square_ready, bra_ready = (
            sem(n) for n in ("rope_ready", "states_in", "square_ready", "bra_ready"))
        negmax, esink, p_ready = sem("negmax"), sem("esink"), sem("p_ready")
        merged, brb_ready, lng_in, x_back, ln_rows = sem("merged"), sem("brb_ready"), sem("lng_in"), sem("x_back"), sem("ln_rows")
        x1_done, h2_ready, masks_ready, route_ready, scattered = (
            sem(n) for n in ("x1_done", "h2_ready", "masks_ready", "route_ready", "scattered"))
        gexp_in, gexp = sem("gexp_in"), sem("gexp")
        silu_ready = sem("silu_ready")
        xg_in = [sem(f"xg_in{i}") for i in range(2)]
        y_stored = [sem(f"y_stored{i}") for i in range(2)]
        yg_in = [sem(f"yg_in{i}") for i in range(2)]
        yg_used, x2_done, out_stored, kv_out = sem("yg_used"), sem("x2_done"), sem("out_stored"), sem("kv_out")

        MOVED_SEM = {"A": act_moved, "D": dve_moved}

        def slot(key):
            return PS[:, NUMBER[key] % 4, :]

        def wait_filled(eng, key, more=0):
            eng.wait_ge(filled, NUMBER[key] + 1 + more)
            return slot(key)

        def wait_moved(eng, key, more=0):
            who, n = MOVED[key]
            eng.wait_ge(MOVED_SEM[who], n + more)

        def wait_slot(pe, key):
            n = NUMBER[key]
            if n >= 4:
                wait_moved(pe, JOBS[n - 4][0])
            return slot(key)

        def ring_slot(name):
            s = BLOCK_NO[name] % RING
            return ring[:, s * BLK:(s + 1) * BLK]

        def wait_block(pe, name, more=0):
            n = BLOCK_NO[name]
            pe.wait_ge(landed[n % RING], 16 * (n // RING + 1) + more)
            return ring_slot(name)

        def tok2(ap):
            return ap.rearrange("p (h t) -> p h t", h=2)

        def ps2(ps):
            return ps.rearrange("p (h t) -> p h t", h=2)[:, :, 0:HALF]

        class Steps:

            def __init__(self, eng, semaphore):
                self.eng, self.semaphore, self.n = eng, semaphore, 0

            def __call__(self, instruction):
                self.n += 1
                instruction.then_inc(self.semaphore, 1)
                self.eng.wait_ge(self.semaphore, self.n)

        with nc.Block() as block:
            @block.gpsimd
            def _(pool):
                pool.dma_start(const[:, :], A["const"]).then_inc(const_in, 16)
                pool.dma_start(y_out, x_in).then_inc(x_first, 16)
                pool.memset(w2[:, :], 0.0).then_inc(w2_zero, 1)
                pool.memset(zero, 0.0).then_inc(zero_set, 1)
                pool.wait_ge(zero_set, 1)
                pool.wait_ge(w2_zero, 1)
                pool.dma_start(rows_in.rearrange("(n p) d -> p n d", p=P), zero.unsqueeze(1).to_broadcast([P, TILES + 1, D]))\
                    .then_inc(zeroed, 16)
                pool.wait_ge(x_first, 16)
                pool.wait_ge(const_in, 16)
                pool.wait_ge(zeroed, 16)

        with nc.Fori(0, DEPTH) as l:
            with nc.Block() as block:

                def block_source(l, name):
                    kind = name[0]
                    if kind == "ada":
                        return A["ada_w"][l, :, 256 * name[1]:256 * (name[1] + 1)].rearrange("(k p) c -> p k c", p=P)
                    if kind == "win":
                        return A["w_in"][l, :, name[1]:name[1] + name[2]].rearrange("(k p) c -> p k c", p=P)
                    if kind == "wb":
                        return A["w_branch"][l, name[2], :, 512 * name[1]:512 * (name[1] + 1)].rearrange("(k p) c -> p k c", p=P)
                    if kind == "mg":
                        col = C_MG + name[2] * D + 512 * name[1] + 256 * name[3]
                        return A["w_in"][l, :, col:col + 256].rearrange("(k p) c -> p k c", p=P)
                    return A["w_out"][l, :, 256 * name[1]:256 * (name[1] + 1)].rearrange("(k p) c -> p k c", p=P)

                @block.sync
                def _(sp):
                    for n, (name, _) in enumerate(BLOCKS[:MOE_BLOCK]):
                        if n >= RING:
                            wait_filled(sp, BLOCKS[n - RING][1])
                        src = block_source(l, name)
                        k, c = src.shape[1], src.shape[2]
                        sp.dma_start(ring_slot(name)[:, 0:k * c].rearrange("p (k c) -> p k c", k=k), src)\
                            .then_inc(landed[n % RING], 16)
                    sp.wait_ge(route_ready, 1)
                    sp.wait_ge(scattered, 16 * 2 * T)
                    sp.dma_start(xg[0], rows_in[0:P, :]).then_inc(xg_in[0], 16)
                    with sp.Fori(0, TILES // 2) as i:
                        for s in range(2):
                            e = sp.value_load(exi[0:1, bass.ds(2 * i + s, 1)], min_val=0, max_val=NE - 1)
                            n = MOE_BLOCK + 3 * s
                            strip = ring[:, 3 * s * BLK:(3 * s + 2) * BLK].rearrange("p (k c) -> p k c", k=KD)
                            if s == 0:
                                sp.wait_ge(filled, MOE_JOB + 2 * PER_TILE * i - 2 * PER_TILE + 1)
                            else:
                                sp.wait_ge(filled, MOE_JOB + 2 * PER_TILE * i - PER_TILE + 1)
                            sp.dma_start(strip[:, :, 0:FF], A["expert_w_gate"][l, e, :, :].rearrange("(k p) f -> p k f", p=P))\
                                .then_inc(landed[3 * s], 16)
                            sp.dma_start(strip[:, :, FF:2 * FF], A["expert_w_up"][l, e, :, :].rearrange("(k p) f -> p k f", p=P))\
                                .then_inc(landed[3 * s + 1], 16)
                            sp.wait_ge(filled, MOE_JOB + 2 * PER_TILE * i + PER_TILE * (s - 1))
                            sp.dma_start(xg[(s + 1) % 2], rows_in[bass.ds(P * (2 * i + s + 1), P), :])\
                                .then_inc(xg_in[(s + 1) % 2], 16)
                            sp.dma_start(ring[:, (3 * s + 2) * BLK:(3 * s + 3) * BLK].rearrange("p (k c) -> p k c", k=2),
                                         A["expert_w_down"][l, e, :, :].rearrange("(k p) d -> p k d", p=P))\
                                .then_inc(landed[3 * s + 2], 16)

                def small_loads(l):
                    yield vst[V_ADA:48, :], A["ada_b"][l, :].rearrange("(r c) -> r c", c=P)
                    yield vst[V_NORM:52, :], A["gla_norm_g"][l, :].rearrange("(r c) -> r c", c=P)
                    yield vst[V_GB:56, :], A["gla_gate_b"][l, :, :].rearrange("d (r c) -> (d r) c", c=P)
                    yield vst[56:64, :], A["c"][0, :].rearrange("(r c) -> r c", c=P)
                    yield vst[64:72, :], A["c_ctx"][:].rearrange("(r c) -> r c", c=P)
                    for d in range(2):
                        yield w2[RANK * d:RANK * (d + 1), 256 * d:256 * (d + 1)], A["gla_gate_w"][l, d, :, :]
                    yield wsn, A["gmlp_ws"][l, :, :, :].rearrange("g t s -> t g s")
                    yield lng, A["gmlp_ln_g"][l, :].partition_broadcast(P)
                    yield lnb, A["gmlp_ln_b"][l, :].partition_broadcast(P)
                    yield bsb[:, :].rearrange("p (g t) -> p g t", g=4), A["gmlp_bs"][l, :, :].partition_broadcast(P)
                    yield ckn, A["cache_k"][0, l, :, :, :].rearrange("(a p) g d -> p a (g d)", p=P)
                    yield cvn, A["cache_v"][0, l, :, :, :].rearrange("(a p) g d -> p a (g d)", p=P)
                    for d in range(2):
                        yield s0[:, 2 * d:2 * d + 2, :], A["state_gla"][0, l, d, :, :, :].rearrange("(q h) k v -> (h k) q v", h=2)
                    yield sink[:, 0:HEADS], A["attn_sink"][l, :].partition_broadcast(P)
                    rw3 = rw[:, :].rearrange("p (k c) -> p k c", k=KD)
                    yield rw3[:, :, 0:NG], A["router_group_w"][l, :, :].rearrange("(k p) c -> p k c", p=P)
                    yield rw3[:, :, NG:LOGITS], A["router_expert_w"][l, :, :].rearrange("(k p) c -> p k c", p=P)
                    yield rb[:, 0:NG], A["router_group_b"][l, :].partition_broadcast(P)
                    yield rb[:, NG:LOGITS], A["router_expert_b"][l, :].partition_broadcast(P)

                N_PARAMS = 20

                @block.gpsimd
                def _(pool):
                    pool.dma_start(x3, y_out.rearrange("(t p) d -> p t d", p=P)).then_inc(x_landed, 16)
                    loads = list(small_loads(l))
                    assert len(loads) == N_PARAMS
                    for dst, src in loads:
                        pool.dma_start(dst, src).then_inc(params, 16)
                    wait_moved(pool, ("ckv", 0))
                    pool.dma_start(A["new_k"][l, :, :], kvt[:, 0, 0:P]).then_inc(kv_out, 16)
                    pool.dma_start(A["new_v"][l, :, :], kvt[:, 0, P:2 * P]).then_inc(kv_out, 16)
                    for c in range(4):
                        wait_moved(pool, ("kv", c))
                        pool.dma_start(A["new_state"][l, c // 2, 2 * (c % 2):2 * (c % 2) + 2, :, :].rearrange("h k v -> (h k) v"),
                                       t1[:, c, 0, :]).then_inc(kv_out, 16)
                    pool.wait_ge(kv_out, 16 * 6)
                    pool.wait_ge(merged, KD)
                    pool.dma_start(x3, y_out.rearrange("(t p) d -> p t d", p=P)).then_inc(x_back, 16)
                    pool.dma_start(bcA[:, 2, :], A["ln1_g"][l, :].partition_broadcast(P)).then_inc(ln_rows, 16)
                    pool.dma_start(bcA[:, 3, :], A["ln1_b"][l, :].partition_broadcast(P)).then_inc(ln_rows, 16)
                    pool.wait_ge(x1_done, T)
                    pool.wait_ge(ln_rows, 16 * (2))
                    pool.dma_start(bcA[:, 2, :], A["ln2_g"][l, :].partition_broadcast(P)).then_inc(ln_rows, 16)
                    pool.dma_start(bcA[:, 3, :], A["ln2_b"][l, :].partition_broadcast(P)).then_inc(ln_rows, 16)
                    pool.wait_ge(route_ready, 1)
                    for t in range(T):
                        for w in range(2):
                            pool.indirect_dma_start(rows_in, bass.IndirectOffsetOnAxis(ap=posi[:, 2 * t + w:2 * t + w + 1], axis=0),
                                                    h2[:, t, :], None).then_inc(scattered, 16)
                    pool.wait_ge(scattered, 16 * 2 * T)
                    wait_moved(pool, ("dn", TILES - 1))
                    for s in range(2):
                        pool.wait_ge(y_stored[s], 16 * (TILES // 2 + 1))
                    for t in range(T):
                        for w in range(2):
                            if t:
                                pool.wait_ge(yg_used, 2 * t + w - 1)
                            pool.indirect_dma_start(yg[w], None, rows_out,
                                                    bass.IndirectOffsetOnAxis(ap=posi[:, 2 * t + w:2 * t + w + 1], axis=0))\
                                .then_inc(yg_in[w], 16)
                    for t in range(T):
                        pool.wait_ge(x2_done, t + 1)
                        pool.dma_start(y_out[P * t:P * (t + 1), :], x3[:, t, :]).then_inc(out_stored, 16)
                    pool.wait_ge(out_stored, 16 * T)
                    pool.wait_ge(x_landed, 16)
                    pool.wait_ge(params, 16 * N_PARAMS)
                    pool.wait_ge(x_back, 16)
                    pool.wait_ge(ln_rows, 16 * 4)
                    for w in range(2):
                        pool.wait_ge(yg_in[w], 16 * T)

                @block.tensor
                def _(pe):
                    def mm(out, lhsT, rhs, start, stop):
                        return nc.tensor.matmul(out, lhsT, rhs, start=start, stop=stop, skip_group_check=True)

                    def turn(out, in_):
                        n = in_.shape[0]
                        return nc.tensor.transpose(out, in_, ident[0:n, 0:n])

                    def feature_major(key, w, rhs3, cols, k0=0):
                        ps = wait_slot(pe, key)
                        k_n = w.shape[1]
                        m = cols.stop - cols.start
                        for h in range(2):
                            for k in range(k_n):
                                last = mm(ps[0:m, 512 * h:512 * h + HALF], w[:, k, cols], rhs3[:, k0 + k, HALF * h:HALF * (h + 1)],
                                          k == 0, k == k_n - 1)
                        last.then_inc(filled, 1)

                    def token_major(key, w, lhs3, t):
                        ps = wait_slot(pe, key)
                        n = w.shape[2]
                        for k in range(KD):
                            last = mm(ps[:, 0:n], lhs3[:, k, P * t:P * (t + 1)], w[:, k, :], k == 0, k == KD - 1)
                        last.then_inc(filled, 1)

                    def view(ap, k):
                        return ap.rearrange("p (k c) -> p k c", k=k)

                    pe.wait_ge(params, 16 * N_PARAMS)
                    ps = wait_slot(pe, ("vec",))
                    turn(ps[:, 0:72], vst[0:72, :]).then_inc(filled, 1)
                    pe.wait_ge(cond_ready, 1)
                    cs3 = cs[:, :].rearrange("p (c k) -> p k c", c=2)
                    for b in range(24):
                        ps = wait_slot(pe, ("mod", b))
                        w = view(wait_block(pe, ("ada", b)), KD)
                        for ct in range(2):
                            for k in range(KD):
                                last = mm(ps[:, 2 * ct:2 * ct + 2], w[:, k, P * ct:P * (ct + 1)], cs3[:, k, :], k == 0, k == KD - 1)
                        last.then_inc(filled, 1)
                    pe.wait_ge(x_landed, 16)
                    for k in range(KD):
                        ps = wait_slot(pe, ("hT", k))
                        for t in range(T):
                            last = turn(ps[:, P * t:P * (t + 1)], x3[:, t, P * k:P * (k + 1)])
                        last.then_inc(filled, 1)
                    for k in range(KD):
                        wait_moved(pe, ("hT", k))
                    w = view(wait_block(pe, ("win", C_LR, 32))[:, 0:32 * KD], KD)
                    feature_major(("lr",), w, h3, slice(0, 32))
                    for name, col in (("aq", C_AQ), ("ak", C_AK)):
                        w = view(wait_block(pe, ("win", col, 256)), KD)
                        for c in range(2):
                            feature_major((name, c), w, h3, slice(P * c, P * (c + 1)))
                    wait_moved(pe, ("lr",))
                    for c in range(4):
                        ps = wait_slot(pe, ("z", c))
                        for h in range(2):
                            last = mm(ps[:, 512 * h:512 * h + HALF], w2[0:32, P * c:P * (c + 1)], lr[0:32, HALF * h:HALF * (h + 1)],
                                      True, True)
                        last.then_inc(filled, 1)
                        name, col = ("vtok", C_V) if c < 2 else ("av", C_AV)
                        w = view(wait_block(pe, ("win", col + 256 * (c % 2), 256)), KD)
                        for t in range(T):
                            token_major((name, c % 2, t), w, h3, t)
                    for name, col in (("ag", C_AG), ("u", C_U), ("cq", C_CQ)):
                        for c in range(4):
                            if c % 2 == 0:
                                w = view(wait_block(pe, ("win", col + P * c, 256)), KD)
                            feature_major((name, c), w, h3, slice(P * (c % 2), P * (c % 2) + P))
                    w = view(wait_block(pe, ("win", C_CK, 256)), KD)
                    for t in range(T):
                        token_major(("ckv", t), w, h3, t)
                    ps = wait_slot(pe, ("wsT",))
                    for g in range(4):
                        last = turn(ps[:, P * g:P * (g + 1)], wsn[:, g, :])
                    last.then_inc(filled, 1)
                    ps = wait_slot(pe, ("kcT",))
                    for g in range(KV_HEADS):
                        for a in range(2):
                            for half in range(2):
                                last = mm(ps[64 * half:64 * half + 64, 256 * g + P * a:256 * g + P * (a + 1)],
                                          ckn[:, a, HD * g:HD * (g + 1)], ident, True, True)
                    last.then_inc(filled, 1)
                    for g in range(KV_HEADS):
                        wait_moved(pe, ("ckv", T - 1))
                        ps = wait_slot(pe, ("kT", g))
                        for t in range(T):
                            for half in range(2):
                                last = mm(ps[64 * half:64 * half + 64, P * t:P * (t + 1)], kvt[:, t, HD * g:HD * (g + 1)],
                                          ident, True, True)
                        last.then_inc(filled, 1)
                    for c in range(4 + KV_HEADS):
                        wait_moved(pe, ("cq", c) if c < 4 else ("kT", c - 4))
                        ps = wait_slot(pe, ("rot", c))
                        src = br3[:, 8 + c, P:TOK] if c < 4 else kT[:, c - 4, P:TOK]
                        mm(ps[:, 0:4 * P], cst("swap"), src, True, True).then_inc(filled, 1)
                    pe.wait_ge(vn_ready, 1)
                    wait_moved(pe, ("wsT",))
                    for g in range(4):
                        ps = wait_slot(pe, ("mix", g))
                        for t in range(T):
                            last = mm(ps[:, P * t:P * (t + 1)], vtok[:, t, P * g:P * (g + 1)], wsT[:, P * g:P * (g + 1)], True, True)
                        last.then_inc(filled, 1)
                    pe.wait_ge(qk_ready, 4)
                    for c in range(5):
                        if c < 4:
                            ps = wait_slot(pe, ("ktok", c))
                            for t in range(T):
                                last = turn(ps[:, P * t:P * (t + 1)], mg3[:, 4 + c, P * t:P * (t + 1)])
                            last.then_inc(filled, 1)
                        if c:
                            wait_moved(pe, ("ktok", c - 1))
                            ps = wait_slot(pe, ("kv", c - 1))
                            for t in range(T):
                                for j in range(2):
                                    head = 2 * ((c - 1) % 2) + j
                                    last = mm(ps[64 * j:64 * j + 64, P * t:P * (t + 1)],
                                              ktok[(c - 1) % 2][:, P * t + 64 * j:P * t + 64 * j + 64],
                                              av[:, t, DV * head:DV * (head + 1)], True, True)
                            last.then_inc(filled, 1)
                    for p in range(PAIRS):
                        for t in range(T + 1):
                            if t < T:
                                ps = wait_slot(pe, ("gs", p, t))
                                for j in range(2):
                                    for d in range(2):
                                        rows = slice(64 * j, 64 * j + 64)
                                        last = mm(ps[:, 512 * j + P * d:512 * j + P * (d + 1)],
                                                  mg3[rows, 4 + 2 * d + p, P * t:P * (t + 1)],
                                                  mg3[rows, 2 * d + p, P * t:P * (t + 1)], True, True)
                                last.then_inc(filled, 1)
                            if t == 0 and p == 0:
                                pe.wait_ge(states_in, 4)
                            if t:
                                u = t - 1
                                wait_moved(pe, ("gs", p, u))
                                ps = wait_slot(pe, ("o", p, u))
                                for j in range(2):
                                    head = 2 * p + j
                                    out = ps[:, 512 * j:512 * j + P]
                                    for d in range(2):
                                        last = mm(out, av[:, u, DV * head:DV * (head + 1)],
                                                  gsb[u % 2][:, P * (2 * j + d):P * (2 * j + d + 1)], d == 0, d == 1 and u == 0)
                                    for d in range(2 if u else 0):
                                        rows = slice(64 * j, 64 * j + 64)
                                        last = mm(out, t1[rows, 2 * d + p, u, :], mg3[rows, 2 * d + p, P * u:P * (u + 1)],
                                                  False, d == 1)
                                last.then_inc(filled, 1)
                    for h in range(GLA_H):
                        pe.wait_ge(square_ready, h + 1)
                        ps = wait_slot(pe, ("ms", h))
                        for half in range(2):
                            last = mm(ps[:, 512 * half:512 * half + HALF], cst("ones"), sq[h % 2][:, HALF * half:HALF * (half + 1)],
                                      True, True)
                        last.then_inc(filled, 1)
                    pe.wait_ge(rope_ready, 6)
                    wait_moved(pe, ("kcT",))

                    def local_tiles(n):
                        return [0] if n == 0 else list(range(max(1, n - 1), min(4, n + 1) + 1))

                    for i in range(UNITS + 3):
                        if i < UNITS:
                            n, h = divmod(i, HEADS)
                            g, rows = h // 4, slice(64 * (h % 2), 64 * (h % 2) + 64)
                            ps = wait_slot(pe, ("s", i))
                            q = br3[rows, 8 + h // 2, P * n:P * (n + 1)]
                            if n == 0:
                                last = mm(ps[:, 0:P], q, kT[rows, g, 0:P], True, True)
                            else:
                                mm(ps[:, 0:CTX], q, kcT[rows, g, :], True, True)
                                col = CTX
                                for m in local_tiles(n):
                                    last = mm(ps[:, col:col + P], q, kT[rows, g, P * m:P * (m + 1)], True, m == n)
                                    if m != n:
                                        which = 0 if m < n else 1
                                        last = mm(ps[:, col:col + P], ident, cst("att_mask")[:, P * which:P * (which + 1)], False, True)
                                    col += P
                            last.then_inc(filled, 1)
                        if 1 <= i <= UNITS:
                            n = (i - 1) // HEADS
                            tiles = (0 if n == 0 else 2) + len(local_tiles(n))
                            pe.wait_ge(p_ready, i)
                            ps = wait_slot(pe, ("pT", i - 1))
                            for m in range(tiles):
                                last = turn(ps[:, P * m:P * (m + 1)], pbuf[(i - 1) % 2][:, P * m:P * (m + 1)])
                            last.then_inc(filled, 1)
                        if i >= 3 and i % 2:
                            m = (i - 3) // 2
                            n, pair = divmod(m, HEADS // 2)
                            ps = wait_slot(pe, ("pv", m))
                            wait_moved(pe, ("pT", 2 * m + 1))
                            for j in range(2):
                                g = (2 * pair + j) // 4
                                values = [] if n == 0 else [cvn[:, a, HD * g:HD * (g + 1)] for a in range(2)]
                                values += [kvt[:, a, P + HD * g:P + HD * (g + 1)] for a in local_tiles(n)]
                                for a, v in enumerate(values):
                                    last = mm(ps[64 * j:64 * j + 64, 0:P], v, pTbuf[(2 * m + j) % 3][:, P * a:P * (a + 1)],
                                              a == 0, a == len(values) - 1)
                            last.then_inc(filled, 1)
                    pe.wait_ge(bra_ready, GLA_H)
                    pe.wait_ge(brb_ready, 4)
                    wait_moved(pe, ("pv", UNITS // 2 - 1))
                    for half in range(2):
                        for n in range(3):
                            wb = view(wait_block(pe, ("wb", half, n)), 4)
                            for q in range(4):
                                if q % 2 == 0:
                                    w = view(wait_block(pe, ("mg", half, n, q // 2)), KD)
                                feature_major(("gate", half, n, q), w, h3, slice(P * (q % 2), P * (q % 2) + P))
                                feature_major(("proj", half, n, q), wb, br3, slice(P * q, P * (q + 1)), 4 * n)

                    def row(v):
                        base, cond = ((16, 1), (16, 0), (32, 1), (32, 0), (24, 1), (24, 0), (40, 1), (40, 0))[v]
                        ps = wait_slot(pe, ("row", v))
                        for k in range(KD):
                            last = mm(ps[:, P * k:P * (k + 1)], mod3[:, base + k, cond:cond + 1].to_broadcast([P, P]), ident, True, True)
                        last.then_inc(filled, 1)

                    for v in range(6):
                        row(v)
                    pe.wait_ge(merged, KD)
                    for cb in range(4):
                        w = view(wait_block(pe, ("wout", cb)), KD)
                        for t in range(T):
                            token_major(("y", cb, t), w, mg3, t)
                    pe.wait_ge(h2_ready, T)
                    for k in range(KD):
                        ps = wait_slot(pe, ("h2T", k))
                        for t in range(T):
                            last = turn(ps[:, P * t:P * (t + 1)], h2[:, t, P * k:P * (k + 1)])
                        last.then_inc(filled, 1)
                    for k in range(KD):
                        wait_moved(pe, ("h2T", k))
                    ps = wait_slot(pe, ("logit",))
                    for t in range(T):
                        for k in range(KD):
                            last = mm(ps[:, 32 * t:32 * t + LOGITS], h3[:, k, P * t:P * (t + 1)], rw[:, LOGITS * k:LOGITS * (k + 1)],
                                      k == 0, k == KD - 1)
                    last.then_inc(filled, 1)
                    pe.wait_ge(masks_ready, 1)
                    ps = wait_slot(pe, ("rank",))
                    for t in range(T + 1):
                        for u in range(min(t + 1, T)):
                            last = mm(ps[:, NE * t:NE * (t + 1)], cst("before") if u == t else cst("ones"),
                                      R["M"][:, NE * u:NE * (u + 1)], u == 0, u == min(t, T - 1))
                    last.then_inc(filled, 1)
                    for v in range(6, 8):
                        row(v)

                    def expert_rows(s, more):
                        ps = slot(("xg", s))
                        for k in range(KD):
                            last = turn(ps[:, P * k:P * (k + 1)], xg[s % 2][:, P * k:P * (k + 1)])
                        last.then_inc(filled, 1)

                    wait_slot(pe, ("xg", 0))
                    pe.wait_ge(xg_in[0], 16)
                    expert_rows(0, 0)
                    wait_moved(pe, ("row", 7))
                    with pe.Fori(0, TILES // 2) as i:
                        more = 4 * i
                        for s in range(2):
                            strip = ring[:, 3 * s * BLK:(3 * s + 2) * BLK].rearrange("p (k c) -> p k c", k=KD)
                            down = ring[:, (3 * s + 2) * BLK:(3 * s + 3) * BLK].rearrange("p (k c) -> p k c", k=2)
                            wait_moved(pe, ("xg", s), more)
                            wait_block(pe, ("gate", s), 16 * i)
                            wait_block(pe, ("up", s), 16 * i)
                            ps = slot(("gu", s))
                            for k in range(KD):
                                last = mm(ps[:, 0:2 * FF], xgT[s][:, k, :], strip[:, k, :], k == 0, k == KD - 1)
                            last.then_inc(filled, 1)
                            pe.wait_ge(xg_in[(s + 1) % 2], 16 * (i + 1 + s))
                            expert_rows(s + 1, 0)
                            wait_moved(pe, ("gu", s), more)
                            pe.wait_ge(act_moved, MOVED[("ht", s)][1] - 1 + more)
                            ps = slot(("ht", s))
                            for f in range(2):
                                last = turn(ps[:, P * f:P * (f + 1)], hid[:, P * f:P * (f + 1)])
                            last.then_inc(filled, 1)
                            wait_moved(pe, ("ht", s), more)
                            wait_block(pe, ("down", s), 16 * i)
                            ps = slot(("dn", s))
                            for half in range(2):
                                for f in range(2):
                                    last = mm(ps[:, 512 * half:512 * (half + 1)], hidT[s][:, f, :], down[:, f, 512 * half:512 * (half + 1)],
                                              f == 0, f == 1)
                            last.then_inc(filled, 1)

                @block.scalar
                def _(act):
                    step = Steps(act, act_step)

                    def f(out, in_, func, **kw):
                        return nc.scalar.activation(out, in_, func, **kw)

                    def moved(instruction):
                        instruction.then_inc(act_moved, 1)

                    wait_moved(act, ("vec",))
                    f(cs[:, :], vec[:, 56:72], ACT.Silu).then_inc(cond_ready, 1)
                    act.wait_ge(mod_ready, 1)
                    for k in range(1, KD, 2):
                        ps = wait_filled(act, ("hT", k))
                        f(h3[:, k, 0:P], ps[:, 0:P], ACT.Identity, scale=mod3[:, 8 + k, 1:2], bias=mod3[:, k, 1:2])
                        moved(f(h3[:, k, P:TOK], ps[:, P:TOK], ACT.Identity, scale=mod3[:, 8 + k, 0:1], bias=mod3[:, k, 0:1]))
                    ps = wait_filled(act, ("lr",))
                    moved(f(tok2(lr[0:32, :]), ps2(ps)[0:32], ACT.Copy))
                    for c in range(2):
                        ps = wait_filled(act, ("aq", c))
                        moved(f(tok2(aqk[:, c, :]), ps2(ps), ACT.Copy, scale=DK ** -0.5))
                    for c in range(4):
                        ps = wait_filled(act, ("z", c))
                        if c:
                            act.wait_ge(qk_ready, c)
                        f(tok2(bufA), ps2(ps), ACT.Abs, bias=vec[:, V_GB + c:V_GB + c + 1]).then_inc(abs_done, 1)
                        act.wait_ge(abs_done, c + 1)
                        step(f(bufA, bufA, ACT.Exp, scale=-1.0))
                        f(bufA, bufA, ACT.Ln, bias=1.0).then_inc(softplus, 1)
                        name, dst = ("vtok", vtok) if c < 2 else ("av", av)
                        for t in range(T):
                            ps = wait_filled(act, (name, c % 2, t))
                            moved(f(dst[:, t, 256 * (c % 2):256 * (c % 2 + 1)], ps[:, 0:256], ACT.Gelu_apprx_tanh if c < 2 else ACT.Copy))
                        act.wait_ge(decay_ready, c + 1)
                        f(bufA, bufB, ACT.Exp, scale=1.0 / GLA_TAU)
                        f(bufM, bufB, ACT.Exp, scale=-1.0 / GLA_TAU)
                        f(er[:, 15 * c:15 * c + 15], er[:, 15 * c:15 * c + 15], ACT.Exp, scale=1.0 / GLA_TAU).then_inc(exp_ready, 1)
                    for c in range(4):
                        ps = wait_filled(act, ("ag", c))
                        moved(f(tok2(br3[:, c, :]), ps2(ps), ACT.Silu))
                    act.wait_ge(var_ready, 1)
                    f(st[:, 40:45], st[:, 40:45], ACT.Sqrt, bias=eps).then_inc(std_ready, 1)
                    for c in range(4):
                        ps = wait_filled(act, ("u", c))
                        moved(f(tok2(br3[:, 4 + c, :]), ps2(ps), ACT.Gelu_apprx_tanh))
                    ps = wait_filled(act, ("wsT",))
                    moved(f(wsT[:, :], ps[:, 0:512], ACT.Copy))
                    ps = wait_filled(act, ("kcT",))
                    moved(f(kcT.rearrange("p g t -> p (g t)"), ps[:, 0:512], ACT.Copy))
                    for c in range(4):
                        ps = wait_filled(act, ("ktok", c))
                        if c >= 2:
                            wait_filled(act, ("kv", c - 2))
                        moved(f(ktok[c % 2], ps[:, 0:TOK], ACT.Copy))
                    for p in range(PAIRS):
                        for t in range(T):
                            ps = wait_filled(act, ("o", p, t))
                            moved(f(oT[:, 2 * p:2 * p + 2, P * t:P * (t + 1)], ps.rearrange("p (j t) -> p j t", j=2)[:, :, 0:P], ACT.Copy))
                    for h in range(GLA_H + 1):
                        if h < GLA_H:
                            wait_moved(act, ("o", PAIRS - 1, T - 1))
                            if h >= 2:
                                act.wait_ge(bra_ready, h - 1)
                            f(sq[h % 2], oT[:, h, :], ACT.Square).then_inc(square_ready, 1)
                        if h:
                            ps = wait_filled(act, ("ms", h - 1))
                            moved(f(tok2(sq[(h - 1) % 2]), ps2(ps), ACT.Sqrt, scale=1.0 / DV, bias=eps))
                    act.wait_ge(kv_out, 16 * 6)
                    for i in range(UNITS + 1):
                        if i < UNITS:
                            h, n = i % HEADS, i // HEADS
                            keys = P if n == 0 else (CTX + (2 if n in (1, 4) else 3) * P)
                            ps = wait_filled(act, ("s", i))
                            act.wait_ge(negmax, i + 1)
                            if i >= 2:
                                wait_filled(act, ("pT", i - 2))
                            nm, rsum = sm[:, i % 2:i % 2 + 1], sm[:, 2 + i % 2:3 + i % 2]
                            moved(f(pbuf[i % 2][:, 0:keys], ps[:, 0:keys], ACT.Exp, scale=HD ** -0.5, bias=nm, accum_out=rsum))
                            f(sm[:, 4 + i % 2:5 + i % 2], sink[:, h:h + 1], ACT.Exp, bias=nm).then_inc(esink, 1)
                        if i:
                            n = (i - 1) // HEADS
                            keys = P if n == 0 else (CTX + (2 if n in (1, 4) else 3) * P)
                            ps = wait_filled(act, ("pT", i - 1))
                            if i - 1 >= 3:
                                wait_filled(act, ("pv", (i - 4) // 2))
                            moved(f(pTbuf[(i - 1) % 3][:, 0:keys], ps[:, 0:keys], ACT.Copy))
                    m = 0
                    for half in range(2):
                        for n in range(3):
                            for q in range(4):
                                ps = wait_filled(act, ("gate", half, n, q))
                                if m >= 2:
                                    before = divmod(m - 2, 12)
                                    wait_moved(act, ("proj", before[0], before[1] // 4, before[1] % 4))
                                moved(f(tok2(sig[m % 2]), ps2(ps), ACT.Sigmoid))
                                m += 1
                    for v in range(6):
                        ps = wait_filled(act, ("row", v))
                        dst = bcA[:, v, :] if v < 2 else bcB[:, v - 2, :]
                        moved(f(dst, ps, ACT.Copy))
                    act.wait_ge(var_ready, 2)
                    f(st[:, 40:45], st[:, 40:45], ACT.Sqrt, bias=eps).then_inc(std_ready, 1)
                    for k in range(KD):
                        ps = wait_filled(act, ("h2T", k))
                        moved(f(h3[:, k, :], ps[:, 0:TOK], ACT.Copy))
                    act.wait_ge(gexp_in, 1)
                    f(R["ge"], R["ge"], ACT.Exp).then_inc(gexp, 1)
                    act.wait_ge(gexp_in, 2)
                    f(R["dq"], R["dq"], ACT.Exp).then_inc(gexp, 1)
                    for v in range(6, 8):
                        ps = wait_filled(act, ("row", v))
                        act.wait_ge(x1_done, T)
                        moved(f(bcA[:, v - 6, :], ps, ACT.Copy))
                    for s in range(2):
                        act.sem_inc(y_stored[s], 16)
                    with act.Fori(0, TILES // 2) as i:
                        for s in range(2):
                            jobs_on, tiles_on = 2 * PER_TILE * i, 2 * i + s
                            ps = wait_filled(act, ("gu", s), jobs_on)
                            act.wait_ge(dve_moved, MOVED[("gu", s)][1] - 2 + 4 * i)
                            f(silu, ps[:, 0:FF], ACT.Silu).then_inc(silu_ready, 1)
                            ps = wait_filled(act, ("ht", s), jobs_on)
                            moved(f(hidT[s], ps[:, 0:2 * P].rearrange("p (f s) -> p f s", f=2), ACT.Copy))
                            ps = wait_filled(act, ("dn", s), jobs_on)
                            act.wait_ge(y_stored[s], 16 * (i + 1))
                            moved(f(ys[s], ps, ACT.Copy))
                            wait_moved(act, ("dn", s), 4 * i)
                            act.dma_start(rows_out[bass.ds(P * tiles_on, P), :], ys[s]).then_inc(y_stored[s], 16)
                    act.wait_ge(var_ready, 3)
                    f(st[:, 40:45], st[:, 40:45], ACT.Sqrt, bias=eps).then_inc(std_ready, 1)

                @block.vector
                def _(dve):
                    step = Steps(dve, dve_step)
                    V = nc.vector

                    def moved(instruction):
                        instruction.then_inc(dve_moved, 1)

                    def bc(ap, shape):
                        return ap.to_broadcast(shape)

                    def tt(out, a, b, op):
                        return V.tensor_tensor(out, a, b, op)

                    def norm_stats(x_of, width):
                        for t in range(T):
                            parts = width // 512
                            for i in range(parts):
                                step(V.bn_stats(st[:, 6 * i:6 * i + 6], x_of(t)[:, 512 * i:512 * (i + 1)]))
                            step(V.bn_aggr(st[:, 12:14], st[:, 0:6 * parts]))
                            step(V.tensor_copy(st[:, 30 + t:31 + t], st[:, 12:13]))
                            last = V.tensor_copy(st[:, 40 + t:41 + t], st[:, 13:14])
                            if t == T - 1:
                                last.then_inc(var_ready, 1)
                            else:
                                step(last)

                    def normalise(n, x_of):
                        dve.wait_ge(std_ready, n)
                        step(V.reciprocal(st[:, 50:55], st[:, 40:45]))
                        for t in range(T):
                            step(V.tensor_scalar(x_of(t), x_of(t), st[:, 30 + t:31 + t], st[:, 50 + t:51 + t], ALU.subtract, ALU.mult))

                    def one_hot(out, x, top, size):
                        x3_, o3 = (a.rearrange("p (t g) -> p t g", t=T) for a in (x, out))
                        g3 = R["gx"].rearrange("p (t g) -> p t g", t=T)
                        step(tt(g3, x3_, bc(top.unsqueeze(2), [P, T, size]), ALU.is_equal))
                        step(tt(g3, g3, bc(cst("first").unsqueeze(1), [P, T, size]), ALU.mult))
                        step(V.tensor_reduce(R["gs"], g3, AXL.X, ALU.max))
                        step(tt(o3, g3, bc(R["gs"].unsqueeze(2), [P, T, size]), ALU.is_equal))

                    ps = wait_filled(dve, ("vec",))
                    moved(V.tensor_copy(vec[:, :], ps[:, 0:72]))
                    wait_moved(dve, ("vec",))
                    for b in range(24):
                        ps = wait_filled(dve, ("mod", b))
                        moved(tt(mod3[:, 2 * b:2 * b + 2, :], ps[:, 0:4].rearrange("p (f c) -> p f c", c=2),
                                 bc(vec[:, 2 * b:2 * b + 2].unsqueeze(2), [P, 2, 2]), ALU.add))
                    wait_moved(dve, ("mod", 23))
                    V.tensor_scalar(mod[:, 16:32], mod[:, 16:32], 1.0, None, ALU.add)
                    V.tensor_scalar(mod[:, 64:80], mod[:, 64:80], 1.0, None, ALU.add).then_inc(mod_ready, 1)
                    dve.wait_ge(mod_ready, 1)
                    V.tensor_scalar(sink[:, HEADS:2 * HEADS], sink[:, 0:HEADS], -1.0, None, ALU.mult)
                    for k in range(0, KD, 2):
                        ps = wait_filled(dve, ("hT", k))
                        V.tensor_scalar(h3[:, k, 0:P], ps[:, 0:P], mod3[:, 8 + k, 1:2], mod3[:, k, 1:2], ALU.mult, ALU.add)
                        moved(V.tensor_scalar(h3[:, k, P:TOK], ps[:, P:TOK], mod3[:, 8 + k, 0:1], mod3[:, k, 0:1], ALU.mult, ALU.add))
                    for c in range(2):
                        ps = wait_filled(dve, ("ak", c))
                        moved(V.tensor_copy(tok2(aqk[:, 2 + c, :]), ps2(ps)))
                    for c in range(4):
                        d = c // 2
                        ps = wait_filled(dve, ("z", c))
                        dve.wait_ge(abs_done, c + 1)
                        moved(V.tensor_scalar(tok2(bufM), ps2(ps), vec[:, V_GB + c:V_GB + c + 1], 0.0, ALU.add, ALU.min))
                        wait_moved(dve, ("z", c))
                        dve.wait_ge(softplus, c + 1)
                        step(tt(bufM, bufM, bufA, ALU.subtract))
                        if d == 0:
                            step(V.tensor_tensor_scan(bufB, cst("run"), bufM, 0.0, ALU.mult, ALU.add))
                        else:
                            step(V.tensor_tensor_scan(bufB[:, ::-1], cst("run"), bufM[:, ::-1], 0.0, ALU.mult, ALU.add))
                        B3 = bufB.rearrange("p (t s) -> p t s", t=T)
                        e3 = er[:, 15 * c:15 * c + 15].rearrange("p (a t) -> p a t", a=3)
                        end = P - 1 if d == 0 else 0
                        step(V.tensor_copy(e3[:, 0, :], B3[:, :, P // 2]))
                        step(V.tensor_copy(e3[:, 2, :], B3[:, :, end]))
                        step(tt(e3[:, 1, :], e3[:, 2, :], e3[:, 0, :], ALU.subtract))
                        tt(B3, B3, bc(e3[:, 0, :].unsqueeze(2), [P, T, P]), ALU.subtract).then_inc(decay_ready, 1)
                        dve.wait_ge(exp_ready, c + 1)
                        tt(mg3[:, c, :], aqk[:, c % 2, :], bufA, ALU.mult)
                        tt(mg3[:, 4 + c, :], aqk[:, 2 + c % 2, :], bufM, ALU.mult).then_inc(qk_ready, 1)
                    wait_moved(dve, ("vtok", 1, T - 1))
                    norm_stats(lambda t: vtok[:, t, :], 512)
                    normalise(1, lambda t: vtok[:, t, :])
                    dve.wait_ge(params, 16 * N_PARAMS)
                    step(tt(vtok, vtok, bc(lng.unsqueeze(1), [P, T, 512]), ALU.mult))
                    tt(vtok, vtok, bc(lnb.unsqueeze(1), [P, T, 512]), ALU.add).then_inc(vn_ready, 1)
                    dve.wait_ge(vn_ready, 1)
                    for c in range(4):
                        ps = wait_filled(dve, ("cq", c))
                        moved(V.tensor_copy(tok2(br3[:, 8 + c, :]), ps2(ps)))
                    for t in range(T):
                        ps = wait_filled(dve, ("ckv", t))
                        moved(V.tensor_copy(kvt[:, t, :], ps[:, 0:256]))
                    for g in range(KV_HEADS):
                        ps = wait_filled(dve, ("kT", g))
                        moved(V.tensor_copy(kT[:, g, :], ps[:, 0:TOK]))
                    for c in range(4 + KV_HEADS):
                        x = br3[:, 8 + c, P:TOK] if c < 4 else kT[:, c - 4, P:TOK]
                        ps = wait_filled(dve, ("rot", c))
                        moved(tt(tmp5[:, 0:4 * P], ps[:, 0:4 * P], cst("sin"), ALU.mult))
                        step(tt(x, x, cst("cos"), ALU.mult))
                        wait_moved(dve, ("rot", c))
                        tt(x, x, tmp5[:, 0:4 * P], ALU.add).then_inc(rope_ready, 1)
                        dve.wait_ge(rope_ready, c + 1)
                    for g in range(4):
                        ps = wait_filled(dve, ("mix", g))
                        bias = bc(bsb[:, P * g:P * (g + 1)].unsqueeze(1), [P, T, P])
                        moved(tt(tmp5.rearrange("p (t s) -> p t s", t=T), ps[:, 0:TOK].rearrange("p (t s) -> p t s", t=T), bias, ALU.add))
                        wait_moved(dve, ("mix", g))
                        wait_moved(dve, ("u", g))
                        tt(br3[:, 4 + g, :], br3[:, 4 + g, :], tmp5, ALU.mult).then_inc(brb_ready, 1)
                        dve.wait_ge(brb_ready, g + 1)
                    for c in range(4):
                        d = c // 2
                        e3 = er[:, 15 * c:15 * c + 15].rearrange("p (a t) -> p a t", a=3)
                        ps = wait_filled(dve, ("kv", c))
                        moved(tt(t1[:, c, :, :], ps[:, 0:TOK].rearrange("p (t v) -> p t v", t=T), bc(e3[:, 1, :].unsqueeze(2), [P, T, P]), ALU.mult))
                        wait_moved(dve, ("kv", c))
                        now, nxt = s0[:, c, :], spare
                        order = [1, 2, 3, 4] if d == 0 else [4, 3, 2, 1]
                        for n, t in enumerate(order):
                            if n < 3:
                                step(V.scalar_tensor_tensor(out=nxt, in0=now, scalar=e3[:, 2, t:t + 1], in1=t1[:, c, t, :],
                                                               op0=ALU.mult, op1=ALU.add))
                            last = V.tensor_scalar(t1[:, c, t, :], now, e3[:, 0, t:t + 1], None, ALU.mult)
                            if n < 3:
                                step(last)
                            now, nxt = nxt, now
                        last.then_inc(states_in, 1)
                        dve.wait_ge(states_in, c + 1)
                    mask = bc(cst("gla_mask").unsqueeze(1), [P, 2, 2 * P])
                    for p in range(PAIRS):
                        for t in range(T):
                            ps = wait_filled(dve, ("gs", p, t))
                            if t >= 2:
                                wait_filled(dve, ("o", p, t - 2))
                            elif p:
                                wait_filled(dve, ("o", p - 1, T - 1))
                            moved(tt(gsb[t % 2].rearrange("p (j c) -> p j c", j=2), ps.rearrange("p (j c) -> p j c", j=2)[:, :, 0:2 * P], mask, ALU.mult))
                    for h in range(GLA_H):
                        wait_moved(dve, ("ms", h))
                        wait_moved(dve, ("ag", h))
                        step(V.reciprocal(sq[h % 2], sq[h % 2]))
                        step(V.scalar_tensor_tensor(out=oT[:, h, :], in0=oT[:, h, :], scalar=vec[:, V_NORM + h:V_NORM + h + 1],
                                                       in1=sq[h % 2], op0=ALU.mult, op1=ALU.mult))
                        tt(br3[:, h, :], br3[:, h, :], oT[:, h, :], ALU.mult).then_inc(bra_ready, 1)
                    for i in range(UNITS + 3):
                        if i < UNITS:
                            n, h = divmod(i, HEADS)
                            keys = P if n == 0 else (CTX + (2 if n in (1, 4) else 3) * P)
                            ps = wait_filled(dve, ("s", i))
                            nm, rsum, es = (sm[:, 2 * a + i % 2:2 * a + i % 2 + 1] for a in range(3))
                            step(V.tensor_reduce(sm[:, 6:7], ps[:, 0:keys], AXL.X, ALU.max))
                            V.tensor_scalar(nm, sm[:, 6:7], -(HD ** -0.5), sink[:, HEADS + h:HEADS + h + 1], ALU.mult, ALU.min)\
                                .then_inc(negmax, 1)
                            dve.wait_ge(esink, i + 1)
                            step(tt(sm[:, 8:9], rsum, es, ALU.add))
                            step(V.reciprocal(sm[:, 9:10], sm[:, 8:9]))
                            V.tensor_scalar(pbuf[i % 2][:, 0:keys], pbuf[i % 2][:, 0:keys], sm[:, 9:10], None, ALU.mult).then_inc(p_ready, 1)
                        if i >= 3 and i % 2:
                            m = (i - 3) // 2
                            n, pair = divmod(m, HEADS // 2)
                            ps = wait_filled(dve, ("pv", m))
                            moved(V.tensor_copy(br3[:, 8 + pair, P * n:P * (n + 1)], ps[:, 0:P]))
                    m = 0
                    for half in range(2):
                        for n in range(3):
                            for q in range(4):
                                out = tok2(mg3[:, 4 * half + q, :])
                                ps = wait_filled(dve, ("proj", half, n, q))
                                wait_moved(dve, ("gate", half, n, q))
                                if n == 0:
                                    moved(tt(out, ps2(ps), tok2(sig[m % 2]), ALU.mult))
                                else:
                                    moved(tt(tok2(gtmp), ps2(ps), tok2(sig[m % 2]), ALU.mult))
                                    wait_moved(dve, ("proj", half, n, q))
                                    last = tt(out, out, tok2(gtmp), ALU.add)
                                    if n == 2:
                                        last.then_inc(merged, 1)
                                        dve.wait_ge(merged, 4 * half + q + 1)
                                    else:
                                        step(last)
                                m += 1
                    dve.wait_ge(merged, KD)
                    dve.wait_ge(x_back, 16)
                    wait_moved(dve, ("row", 5))
                    for cb in range(4):
                        cols = slice(256 * cb, 256 * (cb + 1))
                        for t in range(T):
                            ps = wait_filled(dve, ("y", cb, t))
                            moved(tt(ytmp, ps[:, 0:256], bcA[:, 0 if t == 0 else 1, cols], ALU.mult))
                            wait_moved(dve, ("y", cb, t))
                            step(V.scalar_tensor_tensor(out=x3[:, t, cols], in0=x3[:, t, cols], scalar=ALPHA, in1=ytmp,
                                                           op0=ALU.mult, op1=ALU.add))

                    def finish_norm(n, done):
                        norm_stats(lambda t: x3[:, t, :], D)
                        normalise(n, lambda t: x3[:, t, :])
                        dve.wait_ge(ln_rows, 16 * (2 * (n - 1)))
                        for t in range(T):
                            step(tt(x3[:, t, :], x3[:, t, :], bcA[:, 2, :], ALU.mult))
                            tt(x3[:, t, :], x3[:, t, :], bcA[:, 3, :], ALU.add).then_inc(done, 1)

                    finish_norm(2, x1_done)
                    for t in range(T):
                        c = 0 if t == 0 else 1
                        dve.wait_ge(x1_done, t + 1)
                        step(tt(h2[:, t, :], x3[:, t, :], bcB[:, c, :], ALU.mult))
                        tt(h2[:, t, :], h2[:, t, :], bcB[:, 2 + c, :], ALU.add).then_inc(h2_ready, 1)
                    ps = wait_filled(dve, ("logit",))
                    lg = R["lg"].rearrange("p (t c) -> p t c", t=T)
                    moved(tt(lg, ps[:, 0:32 * T].rearrange("p (t c) -> p t c", c=32)[:, :, 0:LOGITS],
                             bc(rb[:, :].unsqueeze(1), [P, T, LOGITS]), ALU.add))
                    wait_moved(dve, ("logit",))
                    ge = R["ge"].rearrange("p (t g) -> p t g", t=T)
                    step(V.tensor_reduce(R["gm"], lg[:, :, 0:NG], AXL.X, ALU.max))
                    step(tt(ge, lg[:, :, 0:NG], bc(R["gm"].unsqueeze(2), [P, T, NG]), ALU.subtract))
                    step(V.memset(R["m1"], 0.0))
                    one_hot(R["G"], R["ge"], R["m1"], NG)
                    V.tensor_copy(R["es"], R["G"]).then_inc(gexp_in, 1)
                    dve.wait_ge(gexp, 1)
                    step(V.tensor_reduce(R["gs"], ge, AXL.X, ALU.add))
                    step(V.reciprocal(R["gp"], R["gs"]))
                    G3 = R["G"].rearrange("p (t g) -> p t g", t=T)
                    big = R["big"].rearrange("p (t g e) -> p t g e", t=T, g=NG)
                    el = lg[:, :, NG:LOGITS].rearrange("p t (g e) -> p t g e", g=NG)
                    step(tt(big, el, bc(G3.unsqueeze(3), [P, T, NG, EG]), ALU.mult))
                    es3 = R["es"].rearrange("p (t e) -> p t e", t=T)
                    step(V.tensor_reduce(es3, big.rearrange("p t g e -> p t e g"), AXL.X, ALU.add))
                    step(V.tensor_reduce(R["m1"], es3, AXL.X, ALU.max))
                    one_hot(R["E1"], R["es"], R["m1"], EG)
                    step(V.scalar_tensor_tensor(out=R["e2"], in0=R["E1"], scalar=-BIG, in1=R["es"], op0=ALU.mult, op1=ALU.add))
                    step(V.tensor_reduce(R["m2"], R["e2"].rearrange("p (t e) -> p t e", t=T), AXL.X, ALU.max))
                    one_hot(R["E2"], R["e2"], R["m2"], EG)
                    tt(R["dq"], R["m2"], R["m1"], ALU.subtract).then_inc(gexp_in, 1)
                    dve.wait_ge(gexp, 2)
                    step(V.tensor_scalar(R["gs"], R["dq"], 1.0, None, ALU.add))
                    step(V.reciprocal(R["gs"], R["gs"]))
                    step(tt(R["w1"], R["gp"], R["gs"], ALU.mult))
                    step(tt(R["w2"], R["w1"], R["dq"], ALU.mult))
                    for name, one in (("M1", "E1"), ("M2", "E2")):
                        m4 = R[name].rearrange("p (t g e) -> p t g e", t=T, g=NG)
                        e4 = R[one].rearrange("p (t e) -> p t e", t=T).unsqueeze(2)
                        step(V.tensor_copy(m4, bc(G3.unsqueeze(3), [P, T, NG, EG])))
                        step(tt(m4, m4, bc(e4, [P, T, NG, EG]), ALU.mult))
                    tt(R["M"], R["M1"], R["M2"], ALU.add).then_inc(masks_ready, 1)
                    ps = wait_filled(dve, ("rank",))
                    moved(V.tensor_copy(R["rk"], ps[:, 0:NE * (T + 1)]))
                    wait_moved(dve, ("rank",))
                    cmp3 = R["cmp"].rearrange("p (e j) -> p e j", e=NE)
                    step(tt(cmp3, bc(R["rk"][:, NE * T:NE * (T + 1)].unsqueeze(2), [P, NE, 5]), bc(cst("over").unsqueeze(1), [P, NE, 5]), ALU.is_gt))
                    step(V.tensor_reduce(R["nt"], cmp3, AXL.X, ALU.add))
                    step(V.tensor_tensor_scan(R["end"], cst("ones")[:, 0:NE], R["nt"], 0.0, ALU.mult, ALU.add))
                    step(tt(R["base"], R["end"], R["nt"], ALU.subtract))
                    step(V.tensor_scalar(R["base"], R["base"], float(P), None, ALU.mult))
                    rk3 = R["rk"][:, 0:NE * T].rearrange("p (t e) -> p t e", t=T)
                    step(tt(rk3, rk3, bc(R["base"].unsqueeze(1), [P, T, NE]), ALU.add))
                    pos3 = R["pos"].rearrange("p (t w) -> p t w", w=2)
                    for w, name in enumerate(("M1", "M2")):
                        m3 = R[name].rearrange("p (t e) -> p t e", t=T)
                        step(tt(m3, m3, rk3, ALU.mult))
                        step(V.tensor_reduce(pos3[:, :, w], m3, AXL.X, ALU.add))
                    step(V.tensor_copy(posi[:, :], R["pos"]))
                    exc = R["exc"].rearrange("p (j e) -> p j e", j=TILES)
                    step(tt(exc, bc(cst("tile").unsqueeze(2), [P, TILES, NE]), bc(R["end"].unsqueeze(1), [P, TILES, NE]), ALU.is_ge))
                    step(V.tensor_reduce(R["ex"], exc, AXL.X, ALU.add))
                    V.tensor_scalar(exi[:, :], R["ex"], float(NE - 1), None, ALU.min).then_inc(route_ready, 1)
                    ps = wait_filled(dve, ("xg", 0))
                    moved(V.tensor_copy(xgT[0], ps.rearrange("p (k s) -> p k s", k=KD)))
                    with dve.Fori(0, TILES // 2) as i:
                        for s in range(2):
                            ps = wait_filled(dve, ("gu", s), 2 * PER_TILE * i)
                            dve.wait_ge(silu_ready, 2 * i + s + 1)
                            moved(tt(hid, ps[:, FF:2 * FF], silu, ALU.mult))
                            ps = wait_filled(dve, ("xg", s + 1), 2 * PER_TILE * i)
                            moved(V.tensor_copy(xgT[(s + 1) % 2], ps.rearrange("p (k s) -> p k s", k=KD)))
                    wait_moved(dve, ("row", 7))
                    for t in range(T):
                        x, rows = x3[:, t, :], 16 * (t + 1)
                        gate = bcA[:, 0 if t == 0 else 1, :]
                        dve.wait_ge(yg_in[0], rows)
                        step(V.tensor_scalar(bcB[:, 0, :], yg[0], R["w1"][:, t:t + 1], None, ALU.mult))
                        V.tensor_copy(st[:, 60:61], st[:, 13:14]).then_inc(yg_used, 1)
                        dve.wait_ge(yg_in[1], rows)
                        V.scalar_tensor_tensor(out=bcB[:, 1, :], in0=yg[1], scalar=R["w2"][:, t:t + 1], in1=bcB[:, 0, :],
                                               op0=ALU.mult, op1=ALU.add).then_inc(yg_used, 1)
                        dve.wait_ge(yg_used, 2 * t + 2)
                        step(tt(bcB[:, 1, :], bcB[:, 1, :], gate, ALU.mult))
                        step(V.scalar_tensor_tensor(out=x, in0=x, scalar=ALPHA, in1=bcB[:, 1, :], op0=ALU.mult, op1=ALU.add))
                    finish_norm(3, x2_done)
                    dve.wait_ge(x2_done, T)
                    V.tensor_copy(st[:, 61:62], st[:, 13:14]).then_inc(layer_done, 1)

            nc.gpsimd.dma_reset()
            for semaphore in per_layer:
                nc.gpsimd.sem_clear(semaphore)
            nc.all_engine_barrier()


def launch_arrays(nc, arrays):
    A = {}
    for name, a in arrays.items():
        A[name] = nc.dram_tensor(f"in_{name}_dram", a.shape, mybir.dt.from_np(a.dtype), kind="ExternalInput").ap()
    for name, shape in _OUTS:
        A[name] = nc.dram_tensor(f"out_{name}_dram", shape, F32, kind="ExternalOutput").ap()
    for name, tiles in (("rows_in", TILES + 1), ("rows_out", TILES)):
        A[name] = nc.dram_tensor(name, (tiles * P, D), F32, kind="Internal").ap()
    return A





def kernel(**inputs):
    import concourse.bacc as _bacc
    from concourse.bass_utils import run_bass_kernel_spmd as _run

    arrays = {n: np.ascontiguousarray(inputs[n]) for n in _INS[2:]}
    arrays["x"] = np.concatenate([np.asarray(inputs["x_prompt"])[0], np.asarray(inputs["x_sample"])[0]], 0)
    arrays["const"] = const_tile()
    nc = _bacc.Bacc("TRN2", target_bir_lowering=False, num_devices=1)
    build_program(nc, launch_arrays(nc, arrays))
    r = _run(nc, [{f"in_{n}_dram": a for n, a in arrays.items()}], core_ids=[0]).results[0]
    y, state, k, v = (r[f"out_{n}_dram"] for n, _ in _OUTS)
    return (y[None, 0:P], y[None, P:TOK], state[None], k.reshape(1, DEPTH, P, KV_HEADS, HD), v.reshape(1, DEPTH, P, KV_HEADS, HD))
```

```python
from contextlib import ExitStack

import numpy as np
import concourse.bass as bass
from concourse import mybir

F32, I32 = mybir.dt.float32, mybir.dt.int32
ALU, ACT, AXL = mybir.AluOpType, mybir.ActivationFunctionType, mybir.AxisListType

P = 128
D = 1024
KD = D // P
DEPTH = 2
T = 5
TOK = T * P
HALF = TOK // 2
CTX = 256
GRID_W = 64
GLA_H, DK, DV, RANK = 4, 64, 128, 16
PAIRS = GLA_H // 2
GLA_TAU = 16.0
HEADS, KV_HEADS, HD = 8, 2, 64
EPS = 1e-5
ALPHA = (2.0 * DEPTH) ** 0.25
NG, EG = 4, 4
NE = NG * EG
FF = D // 4
LOGITS = NG + NE
N_MIXER = 9
TILES = 26
BIG = 1e30

C_AQ, C_AK, C_AV, C_AG, C_LR, C_U, C_V, C_CQ, C_CK, C_MG = 0, 256, 512, 1024, 1536, 1568, 2080, 2592, 3104, 3360
V_ADA, V_NORM, V_GB, V_ROWS = 0, 48, 52, 56

UNITS = T * HEADS
MOD_FIRST, MOD_ALL = 8, 24
RING = 6
BLK = 2048


def mod_beside(i):
    b = MOD_FIRST + (i - 5) // 2
    return b if i >= 5 and i % 2 and b < MOD_ALL else 0


def build_tables():
    jobs, blocks = [], []

    def job(eng, *key):
        jobs.append((key, eng))

    def block(name, last):
        blocks.append((name, last))

    job("D", "vec")
    for b in range(MOD_FIRST):
        job("D", "mod", b)
        block(("ada", b), ("mod", b))
    for k in range(KD):
        job("A" if k % 2 else "D", "hT", k)
    job("A", "lr")
    block(("win", C_LR, 32), ("lr",))
    for c in range(2):
        job("A", "aq", c)
    block(("win", C_AQ, 256), ("aq", 1))
    for c in range(2):
        job("D", "ak", c)
    block(("win", C_AK, 256), ("ak", 1))
    for c in range(4):
        job("D", "z", c)
        name, col = ("vtok", C_V) if c < 2 else ("av", C_AV)
        for t in range(T):
            job("A", name, c % 2, t)
        block(("win", col + 256 * (c % 2), 256), (name, c % 2, T - 1))
    for c in range(4):
        job("A", "ag", c)
        if c % 2:
            block(("win", C_AG + 128 * (c - 1), 256), ("ag", c))
    for c in range(4):
        job("A", "u", c)
        if c % 2:
            block(("win", C_U + 128 * (c - 1), 256), ("u", c))
    for c in range(4):
        job("D", "cq", c)
        if c % 2:
            block(("win", C_CQ + 128 * (c - 1), 256), ("cq", c))
    for t in range(T):
        job("D", "ckv", t)
    block(("win", C_CK, 256), ("ckv", T - 1))
    job("A", "wsT")
    job("A", "kcT")
    for g in range(KV_HEADS):
        job("D", "kT", g)
    for c in range(4 + KV_HEADS):
        job("D", "rot", c)
    for g in range(4):
        job("D", "mix", g)
    for c in range(5):
        if c < 4:
            job("A", "ktok", c)
        if c:
            job("D", "kv", c - 1)
    for p in range(PAIRS):
        for t in range(T + 1):
            if t < T:
                job("D", "gs", p, t)
            if t:
                job("A", "o", p, t - 1)
    for h in range(GLA_H):
        job("A", "ms", h)
    for i in range(UNITS + 3):
        if i < UNITS:
            job("A", "s", i)
        if 2 <= i < UNITS + 2:
            job("A", "pT", i - 2)
        if i >= 4 and i % 2 == 0:
            job("D", "pv", (i - 4) // 2)
        b = mod_beside(i)
        if b:
            job("D", "mod", b)
            block(("ada", b), ("mod", b))
    for half in range(2):
        for n in range(3):
            for q in range(4):
                job("A", "gate", half, n, q)
                job("D", "proj", half, n, q)
            block(("wb", half, n), ("proj", half, n, 3))
            block(("mg", half, n, 0), ("gate", half, n, 1))
            block(("mg", half, n, 1), ("gate", half, n, 3))
    for v in range(6):
        job("A", "row", v)
    for t in range(T + 2):
        for cb in range(4 if t < T else 0):
            job("D", "y", t, cb)
        if t >= 2:
            job("A", "h2T", t - 2)
    for cb in range(4):
        block(("wout", cb), ("y", T - 1, cb))
    job("D", "logit")
    job("D", "rank")
    for v in range(6, 8):
        job("A", "row", v)
    job("D", "xg", 0)
    assert len(blocks) % RING == 0
    moe_block = len(blocks)
    for j in range(TILES + 1):
        if j < TILES:
            job("D", "gu", j)
        if j:
            job("A", "dn", j - 1)
        if j < TILES:
            job("D", "xg", j + 1)
            job("A", "ht", j)
            block(("gate", j), ("gu", j))
            block(("up", j), ("gu", j))
            block(("down", j), ("dn", j))
    number = {}
    moved = {}
    count = {"A": 0, "D": 0}
    for n, (key, eng) in enumerate(jobs):
        count[eng] += 1
        number[key] = n
        moved[key] = (eng, count[eng])
    assert len(blocks) % RING == 0
    return jobs, number, moved, blocks, moe_block


JOBS, NUMBER, MOVED, BLOCKS, MOE_BLOCK = build_tables()
BLOCK_NO = {name: n for n, (name, _) in enumerate(BLOCKS)}
PER_TILE = 4

CONST, _at = {}, 0
for _name, _width in (("ident", P), ("ones", P), ("before", P), ("gla_mask", 2 * P), ("att_mask", 2 * P), ("swap", P),
                      ("cos", 4 * P), ("sin", 4 * P), ("run", TOK), ("eps", 1), ("over", 5), ("first", 4),
                      ("tile", TILES)):
    CONST[_name] = (_at, _width)
    _at += _width
CONST_W = _at


def const_tile():
    c = np.zeros((P, CONST_W), np.float32)
    r, q = np.arange(P)[:, None], np.arange(P)[None, :]

    def put(name, values):
        at, width = CONST[name]
        c[:, at:at + width] = values

    put("ident", r == q)
    put("ones", 1.0)
    put("before", r < q)
    put("gla_mask", np.concatenate([r <= q, r >= q], 1))
    put("att_mask", np.where(np.concatenate([q >= r, q <= r], 1), 0.0, -BIG))
    quarter = HD // 4
    swap = np.zeros((P, P), np.float32)
    for base in range(0, P, 2 * quarter):
        for i in range(quarter):
            swap[base + quarter + i, base + i] = -1.0
            swap[base + i, base + quarter + i] = 1.0
    put("swap", swap)
    freq = np.power(np.float32(10000.0), -np.arange(quarter, dtype=np.float32) / np.float32(quarter)).astype(np.float32)
    tok = np.arange(4 * P)
    row, col = (tok // GRID_W).astype(np.float32), (tok % GRID_W).astype(np.float32)
    ang = np.stack([(row if d % HD < HD // 2 else col) * freq[d % quarter] for d in range(P)]).astype(np.float32)
    put("cos", np.cos(ang))
    put("sin", np.sin(ang))
    put("run", np.broadcast_to((np.arange(TOK) % P != 0), (P, TOK)))
    put("eps", EPS)
    put("over", P * np.arange(5.0)[None, :])
    put("first", np.arange(4.0, 0.0, -1.0)[None, :])
    put("tile", np.arange(float(TILES))[None, :])
    return c


_INS = ["x_prompt", "x_sample", "state_gla", "cache_k", "cache_v", "c", "c_ctx", "ada_w", "ada_b", "w_in",
        "gla_gate_w", "gla_gate_b", "gla_norm_g", "gmlp_ln_g", "gmlp_ln_b", "gmlp_ws", "gmlp_bs", "attn_sink",
        "w_branch", "w_out", "ln1_g", "ln1_b", "ln2_g", "ln2_b", "router_group_w", "router_group_b",
        "router_expert_w", "router_expert_b", "expert_w_gate", "expert_w_up", "expert_w_down"]
_OUTS = [("y", (TOK, D)), ("new_state", (DEPTH, 2, GLA_H, DK, DV)), ("new_k", (DEPTH, P, P)), ("new_v", (DEPTH, P, P))]



def build_program(nc, A):
    with ExitStack() as ctx:
        def sb(name, width, dt=F32, parts=P):
            return ctx.enter_context(nc.sbuf_tensor(name, [parts, width], dt))

        per_layer = []

        def sem(name):
            per_layer.append(ctx.enter_context(nc.semaphore(name)))
            return per_layer[-1]

        const = sb("const", CONST_W)
        hT = sb("hT", KD * TOK)
        ring = sb("ring", RING * BLK)
        br = sb("br", 12 * TOK)
        mg = sb("mg", KD * TOK)
        xr = sb("xr", T * D)
        ar = sb("ar", 11904)
        vst = sb("vst", P)
        vec = sb("vec", 72)
        mod = sb("mod", 96)
        cs = sb("cs", 16)
        w2 = sb("w2", 512, parts=32)
        wsT = sb("wsT", 4 * P)
        bsb = sb("bsb", 4 * P)
        sink = sb("sink", 2 * HEADS)
        rw = sb("rw", KD * LOGITS)
        rb = sb("rb", LOGITS)
        st = sb("st", 64)
        er = sb("er", 4 * 15)
        sm = sb("sm", 16)
        zero = sb("zero", D // 2)

        def cst(name, parts=P):
            at, width = CONST[name]
            return const[0:parts, at:at + width]

        ident = cst("ident")
        eps = cst("eps")
        h3 = hT[:, :].rearrange("p (k t) -> p k t", k=KD)
        br3 = br[:, :].rearrange("p (k t) -> p k t", k=12)
        mg3 = mg[:, :].rearrange("p (k t) -> p k t", k=KD)
        x3 = xr[:, :].rearrange("p (t d) -> p t d", t=T)
        av = xr[:, 0:2560].rearrange("p (t c) -> p t c", t=T)
        vtok = xr[:, 2560:5120].rearrange("p (t c) -> p t c", t=T)
        oT = xr[:, 2560:5120].rearrange("p (h t) -> p h t", h=GLA_H)
        mod3 = mod[:, :].rearrange("p (f c) -> p f c", c=2)
        lng = br[:, 5120:5632]
        lnb = br[:, 5632:6144]
        aqk = ar[:, 0:2560].rearrange("p (c t) -> p c t", c=4)
        t1 = ar[:, 0:2560].rearrange("p (c t v) -> p c t v", c=4, t=T)
        pbuf = [ar[:, 640 * i:640 * (i + 1)] for i in range(3)]
        pTbuf = [ar[:, 1920 + 640 * i:2560 + 640 * i] for i in range(4)]
        diag = [ar[:, 4480 + P * i:4480 + P * (i + 1)] for i in range(3)]
        bufA, bufM, bufB = (ar[:, 2560 + 640 * i:3200 + 640 * i] for i in range(3))
        gsb = [ar[:, 2560 + 512 * i:3072 + 512 * i] for i in range(2)]
        tmp5 = ar[:, 3584:4224]
        ktok = [ar[:, 4480 + 640 * i:5120 + 640 * i] for i in range(2)]
        kvt = ar[:, 5760:7040].rearrange("p (t c) -> p t c", t=T)
        kT = ar[:, 7040:8320].rearrange("p (g t) -> p g t", g=KV_HEADS)
        kcT = ar[:, 8320:8832].rearrange("p (g t) -> p g t", g=KV_HEADS)
        ckn = ar[:, 8832:9088].rearrange("p (a c) -> p a c", a=2)
        cvn = ar[:, 9088:9344].rearrange("p (a c) -> p a c", a=2)
        lr = ar[:, 9344:9984]
        sq = [ar[:, 9984 + 640 * i:10624 + 640 * i] for i in range(2)]
        wsn = ar[:, 9984:10496].rearrange("p (g s) -> p g s", g=4)
        spare = ar[:, 11264:11392]
        s0 = ar[:, 11392:11904].rearrange("p (c v) -> p c v", c=4)
        sig = sq
        gtmp = lr
        bcA = ar[:, 0:4096].rearrange("p (v d) -> p v d", v=4)
        bcB = ar[:, 4096:8192].rearrange("p (v d) -> p v d", v=4)
        ytmp = ar[:, 8192:8448]
        R = {}
        at = 8448
        for name, width in (("lg", T * LOGITS), ("ge", 20), ("G", 20), ("gx", 20), ("gm", 5), ("gs", 5), ("gp", 5),
                            ("es", 20), ("e2", 20), ("E1", 20), ("E2", 20), ("m1", 5), ("m2", 5), ("dq", 5),
                            ("w1", 5), ("w2", 5), ("big", 80), ("M1", 80), ("M2", 80), ("M", 80), ("rk", 96),
                            ("cmp", 80), ("nt", 16), ("end", 16), ("base", 16), ("pos", 10), ("ex", TILES + 1),
                            ("exc", TILES * NE), ("pairs", TILES // 2)):
            R[name] = ar[:, at:at + width]
            at += width
        posi = ctx.enter_context(nc.sbuf_tensor("posi", [P, 10], I32))
        exi = ctx.enter_context(nc.sbuf_tensor("exi", [P, TILES + 1], I32))
        assert at <= 11904, at
        h2 = br[:, 0:T * D].rearrange("p (t d) -> p t d", t=T)
        yg = [[br[:, D * (2 * a + w):D * (2 * a + w + 1)] for w in range(2)] for a in range(2)]
        ysum = [mg[:, D * (2 + i):D * (3 + i)] for i in range(2)]
        ys = [br[:, 5120 + D * i:5120 + D * (i + 1)] for i in range(2)]
        xgT = [mg[:, D * i:D * (i + 1)].rearrange("p (k s) -> p k s", k=KD) for i in range(2)]
        xg = [mg[:, 2048 + D * i:2048 + D * (i + 1)] for i in range(2)]
        silu, hid = mg[:, 4096:4352], mg[:, 4352:4608]
        hidT = [mg[:, 4608 + 256 * i:4864 + 256 * i].rearrange("p (f s) -> p f s", f=2) for i in range(2)]

        PS = ctx.enter_context(nc.psum_tensor("PS", [P, 4, 1024], F32))

        x_in = A["x"]
        y_out = A["y"]
        rows = A["rows"]

        const_in, x_in_sem, x_copied, w2_zero, zeroed, zero_set = (
            ctx.enter_context(nc.semaphore(n)) for n in ("const_in", "x_first", "x_copied", "w2_zero", "zeroed", "zero_set"))
        filled, act_moved, dve_moved = sem("filled"), sem("act_moved"), sem("dve_moved")
        landed = [sem(f"landed{i}") for i in range(RING)]
        vectors_in, gates_in, mixer_in, router_in = (sem(n) for n in ("vectors_in", "gates_in", "mixer_in", "router_in"))
        act_step, dve_step = sem("act_step"), sem("dve_step")
        cond_ready, mod_ready = sem("cond_ready"), sem("mod_ready")
        abs_done, softplus, decay_ready, exp_ready, qk_ready = (
            sem(n) for n in ("abs_done", "softplus", "decay_ready", "exp_ready", "qk_ready"))
        var_ready, std_ready, vn_ready = sem("var_ready"), sem("std_ready"), sem("vn_ready")
        rope_ready, states_in, square_ready, bra_ready = (
            sem(n) for n in ("rope_ready", "states_in", "square_ready", "bra_ready"))
        negmax, esink, p_ready = sem("negmax"), sem("esink"), sem("p_ready")
        merged, brb_ready, x_back, ln_rows = sem("merged"), sem("brb_ready"), sem("x_back"), sem("ln_rows")
        x1_done, h2_ready, masks_ready, route_ready, scattered = (
            sem(n) for n in ("x1_done", "h2_ready", "masks_ready", "route_ready", "scattered"))
        gexp_in, gexp = sem("gexp_in"), sem("gexp")
        silu_ready = sem("silu_ready")
        xg_in = [sem(f"xg_in{i}") for i in range(2)]
        y_stored = [sem(f"y_stored{i}") for i in range(2)]
        yg_in = [[sem(f"yg_in{a}{w}") for w in range(2)] for a in range(2)]
        experts_done = sem("experts_done")
        first_scaled, rs_ready, x_norm = sem("first_scaled"), sem("rs_ready"), sem("x_norm")
        yg_used, x2_done, out_stored, kv_out = sem("yg_used"), sem("x2_done"), sem("out_stored"), sem("kv_out")

        MOVED_SEM = {"A": act_moved, "D": dve_moved}

        def slot(key):
            return PS[:, NUMBER[key] % 4, :]

        def wait_filled(eng, key, more=0):
            eng.wait_ge(filled, NUMBER[key] + 1 + more)
            return slot(key)

        def wait_moved(eng, key, more=0):
            who, n = MOVED[key]
            eng.wait_ge(MOVED_SEM[who], n + more)

        def wait_slot(pe, key):
            n = NUMBER[key]
            if n >= 4:
                wait_moved(pe, JOBS[n - 4][0])
            return slot(key)

        def ring_slot(name):
            s = BLOCK_NO[name] % RING
            return ring[:, s * BLK:(s + 1) * BLK]

        def wait_block(pe, name, more=0):
            n = BLOCK_NO[name]
            pe.wait_ge(landed[n % RING], 16 * (n // RING + 1) + more)
            return ring_slot(name)

        def tok2(ap):
            return ap.rearrange("p (h t) -> p h t", h=2)

        def ps2(ps):
            return ps.rearrange("p (h t) -> p h t", h=2)[:, :, 0:HALF]

        def keys_of(n):
            return P if n == 0 else CTX + (2 if n in (1, 4) else 3) * P

        class Steps:

            def __init__(self, eng, semaphore):
                self.eng, self.semaphore, self.n = eng, semaphore, 0

            def __call__(self, instruction):
                self.n += 1
                instruction.then_inc(self.semaphore, 1)
                self.eng.wait_ge(self.semaphore, self.n)

        with nc.Block() as block:
            @block.sync
            def _(sp):
                sp.dma_start(x3, x_in.rearrange("(t p) d -> p t d", p=P)).then_inc(x_in_sem, 16)

            @block.scalar
            def _(act):
                act.dma_start(const[:, :], A["const"]).then_inc(const_in, 16)

            @block.gpsimd
            def _(pool):
                pool.memset(w2[:, :], 0.0).then_inc(w2_zero, 1)
                pool.memset(zero[:, :], 0.0).then_inc(zero_set, 1)

        with nc.Fori(0, DEPTH) as l:
            with nc.Block() as block:

                def block_source(l, name):
                    kind = name[0]
                    if kind == "ada":
                        return A["ada_w"][l, :, 256 * name[1]:256 * (name[1] + 1)].rearrange("(k p) c -> p k c", p=P)
                    if kind == "win":
                        return A["w_in"][l, :, name[1]:name[1] + name[2]].rearrange("(k p) c -> p k c", p=P)
                    if kind == "wb":
                        return A["w_branch"][l, name[2], :, 512 * name[1]:512 * (name[1] + 1)].rearrange("(k p) c -> p k c", p=P)
                    if kind == "mg":
                        col = C_MG + name[2] * D + 512 * name[1] + 256 * name[3]
                        return A["w_in"][l, :, col:col + 256].rearrange("(k p) c -> p k c", p=P)
                    return A["w_out"][l, :, 256 * name[1]:256 * (name[1] + 1)].rearrange("(k p) c -> p k c", p=P)

                @block.sync
                def _(sp):
                    for n, (name, _) in enumerate(BLOCKS[:MOE_BLOCK]):
                        if n >= RING:
                            wait_filled(sp, BLOCKS[n - RING][1])
                        src = block_source(l, name)
                        k, c = src.shape[1], src.shape[2]
                        sp.dma_start(ring_slot(name)[:, 0:k * c].rearrange("p (k c) -> p k c", k=k), src)\
                            .then_inc(landed[n % RING], 16)
                    sp.wait_ge(route_ready, 1)

                    def strip_load(e, s):
                        strip = ring[:, 3 * s * BLK:(3 * s + 2) * BLK].rearrange("p (k c) -> p k c", k=KD)
                        sp.dma_start(strip[:, :, 0:FF], A["expert_w_gate"][l, e, :, :].rearrange("(k p) f -> p k f", p=P))\
                            .then_inc(landed[3 * s], 16)
                        sp.dma_start(strip[:, :, FF:2 * FF], A["expert_w_up"][l, e, :, :].rearrange("(k p) f -> p k f", p=P))\
                            .then_inc(landed[3 * s + 1], 16)

                    def down_load(e, s):
                        sp.dma_start(ring[:, (3 * s + 2) * BLK:(3 * s + 3) * BLK].rearrange("p (k c) -> p k c", k=2),
                                     A["expert_w_down"][l, e, :, :].rearrange("(k p) d -> p k d", p=P))\
                            .then_inc(landed[3 * s + 2], 16)

                    def rows_load(tile, s):
                        sp.dma_start(xg[s], rows[bass.ds(P * tile, P), :]).then_inc(xg_in[s], 16)

                    for s in range(2):
                        e = sp.value_load(exi[0:1, s:s + 1], min_val=0, max_val=NE - 1)
                        strip_load(e, s)
                        down_load(e, s)
                        if s == 0:
                            sp.wait_ge(scattered, 16 * 2 * T)
                            rows_load(0, 0)
                            rows_load(1, 1)
                    wait_filled(sp, ("xg", 0))
                    rows_load(2, 0)
                    pairs = sp.value_load(exi[0:1, TILES:TILES + 1], min_val=1, max_val=TILES // 2)
                    with sp.Fori(1, TILES // 2) as i:
                        with sp.If(i < pairs):
                            more = 2 * PER_TILE * (i - 1)
                            for s in range(2):
                                e = sp.value_load(exi[0:1, bass.ds(2 * i + s, 1)], min_val=0, max_val=NE - 1)
                                wait_filled(sp, ("gu", s), more)
                                strip_load(e, s)
                                wait_filled(sp, ("xg", s + 1), more)
                                rows_load(2 * i + s + 1, (s + 1) % 2)
                                wait_filled(sp, ("dn", s), more)
                                down_load(e, s)

                def vector_loads(l):
                    yield vst[V_ADA:48, :], A["ada_b"][l, :].rearrange("(r c) -> r c", c=P)
                    yield vst[V_NORM:52, :], A["gla_norm_g"][l, :].rearrange("(r c) -> r c", c=P)
                    yield vst[V_GB:56, :], A["gla_gate_b"][l, :, :].rearrange("d (r c) -> (d r) c", c=P)
                    yield vst[56:64, :], A["c"][0, :].rearrange("(r c) -> r c", c=P)
                    yield vst[64:72, :], A["c_ctx"][:].rearrange("(r c) -> r c", c=P)

                def mixer_loads(l):
                    yield wsn, A["gmlp_ws"][l, :, :, :].rearrange("g t s -> t g s")
                    yield lng, A["gmlp_ln_g"][l, :].partition_broadcast(P)
                    yield lnb, A["gmlp_ln_b"][l, :].partition_broadcast(P)
                    yield bsb[:, :].rearrange("p (g t) -> p g t", g=4), A["gmlp_bs"][l, :, :].partition_broadcast(P)
                    yield ckn, A["cache_k"][0, l, :, :, :].rearrange("(a p) g d -> p a (g d)", p=P)
                    yield cvn, A["cache_v"][0, l, :, :, :].rearrange("(a p) g d -> p a (g d)", p=P)
                    for d in range(2):
                        yield s0[:, 2 * d:2 * d + 2, :], A["state_gla"][0, l, d, :, :, :].rearrange("(q h) k v -> (h k) q v", h=2)
                    yield sink[:, 0:HEADS], A["attn_sink"][l, :].partition_broadcast(P)

                def router_loads(l):
                    rw3 = rw[:, :].rearrange("p (k c) -> p k c", k=KD)
                    yield rw3[:, :, 0:NG], A["router_group_w"][l, :, :].rearrange("(k p) c -> p k c", p=P)
                    yield rw3[:, :, NG:LOGITS], A["router_expert_w"][l, :, :].rearrange("(k p) c -> p k c", p=P)
                    yield rb[:, 0:NG], A["router_group_b"][l, :].partition_broadcast(P)
                    yield rb[:, NG:LOGITS], A["router_expert_b"][l, :].partition_broadcast(P)

                @block.gpsimd
                def _(pool):
                    pool.wait_ge(w2_zero, 1)
                    for d in range(2):
                        pool.dma_start(w2[RANK * d:RANK * (d + 1), 256 * d:256 * (d + 1)], A["gla_gate_w"][l, d, :, :])\
                            .then_inc(gates_in, 16)
                    for dst, src in mixer_loads(l):
                        pool.dma_start(dst, src).then_inc(mixer_in, 16)
                    for dst, src in router_loads(l):
                        pool.dma_start(dst, src).then_inc(router_in, 16)
                    with pool.If(l < 1):
                        pool.dma_start(y_out, x_in).then_inc(x_copied, 16)
                        wait_filled(pool, ("kT", 0))
                        pool.wait_ge(zero_set, 1)
                        pool.dma_start(rows.rearrange("(p n) (k c) -> p (n k) c", p=P, k=2),
                                       zero[:, :].unsqueeze(1).to_broadcast([P, (TILES + 1) * 2, D // 2])).then_inc(zeroed, 16)
                    wait_moved(pool, ("ckv", 0))
                    pool.dma_start(A["new_k"][l, :, :], kvt[:, 0, 0:P]).then_inc(kv_out, 16)
                    pool.dma_start(A["new_v"][l, :, :], kvt[:, 0, P:2 * P]).then_inc(kv_out, 16)
                    for c in range(4):
                        wait_moved(pool, ("kv", c))
                        pool.dma_start(A["new_state"][l, c // 2, 2 * (c % 2):2 * (c % 2) + 2, :, :].rearrange("h k v -> (h k) v"),
                                       t1[:, c, 0, :]).then_inc(kv_out, 16)
                    pool.wait_ge(kv_out, 16 * 6)
                    pool.wait_ge(x_copied, 16)
                    pool.wait_ge(merged, KD)
                    pool.dma_start(x3, y_out.rearrange("(t p) d -> p t d", p=P)).then_inc(x_back, 16)
                    pool.dma_start(bcA[:, 2, :], A["ln1_g"][l, :].partition_broadcast(P)).then_inc(ln_rows, 16)
                    pool.dma_start(bcA[:, 3, :], A["ln1_b"][l, :].partition_broadcast(P)).then_inc(ln_rows, 16)
                    pool.wait_ge(x1_done, T)
                    pool.wait_ge(ln_rows, 16 * (2))
                    pool.dma_start(bcA[:, 2, :], A["ln2_g"][l, :].partition_broadcast(P)).then_inc(ln_rows, 16)
                    pool.dma_start(bcA[:, 3, :], A["ln2_b"][l, :].partition_broadcast(P)).then_inc(ln_rows, 16)
                    pool.wait_ge(zeroed, 16)
                    pool.wait_ge(route_ready, 1)
                    for t in range(T):
                        for w in range(2):
                            pool.indirect_dma_start(rows, bass.IndirectOffsetOnAxis(ap=posi[:, 2 * t + w:2 * t + w + 1], axis=0),
                                                    h2[:, t, :], None).then_inc(scattered, 16)
                    pool.wait_ge(scattered, 16 * 2 * T)
                    pool.wait_ge(experts_done, 1)
                    pool.wait_ge(ln_rows, 16 * 4)
                    for t in range(T):
                        for w in range(2):
                            if t >= 2:
                                pool.wait_ge(first_scaled if w == 0 else yg_used, t - 1)
                            pool.indirect_dma_start(yg[t % 2][w], None, rows,
                                                    bass.IndirectOffsetOnAxis(ap=posi[:, 2 * t + w:2 * t + w + 1], axis=0))\
                                .then_inc(yg_in[t % 2][w], 16)
                    for t in range(T):
                        pool.wait_ge(x2_done, t + 1)
                        pool.dma_start(y_out[P * t:P * (t + 1), :], x3[:, t, :]).then_inc(out_stored, 16)
                    pool.wait_ge(out_stored, 16 * T)
                    for a in range(2):
                        for w in range(2):
                            pool.wait_ge(yg_in[a][w], 16 * (3 - a))

                @block.tensor
                def _(pe):
                    def mm(out, lhsT, rhs, start, stop):
                        return nc.tensor.matmul(out, lhsT, rhs, start=start, stop=stop, skip_group_check=True)

                    def turn(out, in_):
                        n = in_.shape[0]
                        return nc.tensor.transpose(out, in_, ident[0:n, 0:n])

                    def feature_major(key, w, rhs3, cols, k0=0):
                        ps = wait_slot(pe, key)
                        k_n = w.shape[1]
                        m = cols.stop - cols.start
                        for h in range(2):
                            for k in range(k_n):
                                last = mm(ps[0:m, 512 * h:512 * h + HALF], w[:, k, cols], rhs3[:, k0 + k, HALF * h:HALF * (h + 1)],
                                          k == 0, k == k_n - 1)
                        last.then_inc(filled, 1)

                    def token_major(key, w, lhs3, t):
                        ps = wait_slot(pe, key)
                        n = w.shape[2]
                        for k in range(KD):
                            last = mm(ps[:, 0:n], lhs3[:, k, P * t:P * (t + 1)], w[:, k, :], k == 0, k == KD - 1)
                        last.then_inc(filled, 1)

                    def view(ap, k):
                        return ap.rearrange("p (k c) -> p k c", k=k)

                    pe.wait_ge(const_in, 16)
                    pe.wait_ge(vectors_in, 16 * 5)
                    ps = wait_slot(pe, ("vec",))
                    turn(ps[:, 0:72], vst[0:72, :]).then_inc(filled, 1)
                    pe.wait_ge(cond_ready, 1)
                    cs3 = cs[:, :].rearrange("p (c k) -> p k c", c=2)

                    def modulation(b):
                        ps = wait_slot(pe, ("mod", b))
                        w = view(wait_block(pe, ("ada", b)), KD)
                        for ct in range(2):
                            for k in range(KD):
                                last = mm(ps[:, 2 * ct:2 * ct + 2], w[:, k, P * ct:P * (ct + 1)], cs3[:, k, :], k == 0, k == KD - 1)
                        last.then_inc(filled, 1)

                    for b in range(MOD_FIRST):
                        modulation(b)
                    pe.wait_ge(x_in_sem, 16)
                    for k in range(KD):
                        ps = wait_slot(pe, ("hT", k))
                        for t in range(T):
                            last = turn(ps[:, P * t:P * (t + 1)], x3[:, t, P * k:P * (k + 1)])
                        last.then_inc(filled, 1)
                    for k in range(KD):
                        wait_moved(pe, ("hT", k))
                    w = view(wait_block(pe, ("win", C_LR, 32))[:, 0:32 * KD], KD)
                    feature_major(("lr",), w, h3, slice(0, 32))
                    for name, col in (("aq", C_AQ), ("ak", C_AK)):
                        w = view(wait_block(pe, ("win", col, 256)), KD)
                        for c in range(2):
                            feature_major((name, c), w, h3, slice(P * c, P * (c + 1)))
                    wait_moved(pe, ("lr",))
                    pe.wait_ge(gates_in, 16 * 2)
                    for c in range(4):
                        ps = wait_slot(pe, ("z", c))
                        for h in range(2):
                            last = mm(ps[:, 512 * h:512 * h + HALF], w2[0:32, P * c:P * (c + 1)], lr[0:32, HALF * h:HALF * (h + 1)],
                                      True, True)
                        last.then_inc(filled, 1)
                        name, col = ("vtok", C_V) if c < 2 else ("av", C_AV)
                        w = view(wait_block(pe, ("win", col + 256 * (c % 2), 256)), KD)
                        for t in range(T):
                            token_major((name, c % 2, t), w, h3, t)
                    for name, col in (("ag", C_AG), ("u", C_U), ("cq", C_CQ)):
                        for c in range(4):
                            if c % 2 == 0:
                                w = view(wait_block(pe, ("win", col + P * c, 256)), KD)
                            feature_major((name, c), w, h3, slice(P * (c % 2), P * (c % 2) + P))
                    w = view(wait_block(pe, ("win", C_CK, 256)), KD)
                    for t in range(T):
                        token_major(("ckv", t), w, h3, t)
                    pe.wait_ge(mixer_in, 16 * N_MIXER)
                    ps = wait_slot(pe, ("wsT",))
                    for g in range(4):
                        last = turn(ps[:, P * g:P * (g + 1)], wsn[:, g, :])
                    last.then_inc(filled, 1)
                    ps = wait_slot(pe, ("kcT",))
                    for g in range(KV_HEADS):
                        for a in range(2):
                            for half in range(2):
                                last = mm(ps[64 * half:64 * half + 64, 256 * g + P * a:256 * g + P * (a + 1)],
                                          ckn[:, a, HD * g:HD * (g + 1)], ident, True, True)
                    last.then_inc(filled, 1)
                    for g in range(KV_HEADS):
                        wait_moved(pe, ("ckv", T - 1))
                        ps = wait_slot(pe, ("kT", g))
                        for t in range(T):
                            for half in range(2):
                                last = mm(ps[64 * half:64 * half + 64, P * t:P * (t + 1)], kvt[:, t, HD * g:HD * (g + 1)],
                                          ident, True, True)
                        last.then_inc(filled, 1)
                    for c in range(4 + KV_HEADS):
                        wait_moved(pe, ("cq", c) if c < 4 else ("kT", c - 4))
                        ps = wait_slot(pe, ("rot", c))
                        src = br3[:, 8 + c, P:TOK] if c < 4 else kT[:, c - 4, P:TOK]
                        mm(ps[:, 0:4 * P], cst("swap"), src, True, True).then_inc(filled, 1)
                    pe.wait_ge(vn_ready, 1)
                    wait_moved(pe, ("wsT",))
                    for g in range(4):
                        ps = wait_slot(pe, ("mix", g))
                        for t in range(T):
                            last = mm(ps[:, P * t:P * (t + 1)], vtok[:, t, P * g:P * (g + 1)], wsT[:, P * g:P * (g + 1)], True, True)
                        last.then_inc(filled, 1)
                    pe.wait_ge(qk_ready, 4)
                    for c in range(5):
                        if c < 4:
                            ps = wait_slot(pe, ("ktok", c))
                            for t in range(T):
                                last = turn(ps[:, P * t:P * (t + 1)], mg3[:, 4 + c, P * t:P * (t + 1)])
                            last.then_inc(filled, 1)
                        if c:
                            wait_moved(pe, ("ktok", c - 1))
                            ps = wait_slot(pe, ("kv", c - 1))
                            for t in range(T):
                                for j in range(2):
                                    head = 2 * ((c - 1) % 2) + j
                                    last = mm(ps[64 * j:64 * j + 64, P * t:P * (t + 1)],
                                              ktok[(c - 1) % 2][:, P * t + 64 * j:P * t + 64 * j + 64],
                                              av[:, t, DV * head:DV * (head + 1)], True, True)
                            last.then_inc(filled, 1)
                    for p in range(PAIRS):
                        for t in range(T + 1):
                            if t < T:
                                ps = wait_slot(pe, ("gs", p, t))
                                for j in range(2):
                                    for d in range(2):
                                        rows = slice(64 * j, 64 * j + 64)
                                        last = mm(ps[:, 512 * j + P * d:512 * j + P * (d + 1)],
                                                  mg3[rows, 4 + 2 * d + p, P * t:P * (t + 1)],
                                                  mg3[rows, 2 * d + p, P * t:P * (t + 1)], True, True)
                                last.then_inc(filled, 1)
                            if t == 0 and p == 0:
                                pe.wait_ge(states_in, 4)
                            if t:
                                u = t - 1
                                wait_moved(pe, ("gs", p, u))
                                ps = wait_slot(pe, ("o", p, u))
                                for j in range(2):
                                    head = 2 * p + j
                                    out = ps[:, 512 * j:512 * j + P]
                                    for d in range(2):
                                        last = mm(out, av[:, u, DV * head:DV * (head + 1)],
                                                  gsb[u % 2][:, P * (2 * j + d):P * (2 * j + d + 1)], d == 0, d == 1 and u == 0)
                                    for d in range(2 if u else 0):
                                        rows = slice(64 * j, 64 * j + 64)
                                        last = mm(out, t1[rows, 2 * d + p, u, :], mg3[rows, 2 * d + p, P * u:P * (u + 1)],
                                                  False, d == 1)
                                last.then_inc(filled, 1)
                    for h in range(GLA_H):
                        pe.wait_ge(square_ready, h + 1)
                        ps = wait_slot(pe, ("ms", h))
                        for half in range(2):
                            last = mm(ps[:, 512 * half:512 * half + HALF], cst("ones"), sq[h % 2][:, HALF * half:HALF * (half + 1)],
                                      True, True)
                        last.then_inc(filled, 1)
                    pe.wait_ge(rope_ready, 6)
                    wait_moved(pe, ("kcT",))

                    def local_tiles(n):
                        return [0] if n == 0 else list(range(max(1, n - 1), min(4, n + 1) + 1))

                    for i in range(UNITS + 3):
                        if i < UNITS:
                            n, h = divmod(i, HEADS)
                            g, rows = h // 4, slice(64 * (h % 2), 64 * (h % 2) + 64)
                            ps = wait_slot(pe, ("s", i))
                            q = br3[rows, 8 + h // 2, P * n:P * (n + 1)]
                            if n == 0:
                                last = mm(ps[:, 0:P], q, kT[rows, g, 0:P], True, True)
                            else:
                                mm(ps[:, 0:CTX], q, kcT[rows, g, :], True, True)
                                col = CTX
                                for m in local_tiles(n):
                                    last = mm(ps[:, col:col + P], q, kT[rows, g, P * m:P * (m + 1)], True, m == n)
                                    if m != n:
                                        which = 0 if m < n else 1
                                        last = mm(ps[:, col:col + P], ident, cst("att_mask")[:, P * which:P * (which + 1)], False, True)
                                    col += P
                            last.then_inc(filled, 1)
                        if 2 <= i < UNITS + 2:
                            u = i - 2
                            n = u // HEADS
                            tiles = (0 if n == 0 else 2) + len(local_tiles(n))
                            pe.wait_ge(p_ready, u + 1)
                            ps = wait_slot(pe, ("pT", u))
                            for m in range(tiles):
                                last = mm(ps[:, P * m:P * (m + 1)], pbuf[u % 3][:, P * m:P * (m + 1)], diag[u % 3], True, True)
                            last.then_inc(filled, 1)
                        if i >= 4 and i % 2 == 0:
                            m = (i - 4) // 2
                            n, pair = divmod(m, HEADS // 2)
                            wait_moved(pe, ("pT", 2 * m + 1))
                            ps = wait_slot(pe, ("pv", m))
                            for j in range(2):
                                g = (2 * pair + j) // 4
                                values = [] if n == 0 else [cvn[:, a, HD * g:HD * (g + 1)] for a in range(2)]
                                values += [kvt[:, a, P + HD * g:P + HD * (g + 1)] for a in local_tiles(n)]
                                for a, v in enumerate(values):
                                    last = mm(ps[64 * j:64 * j + 64, 0:P], v, pTbuf[(2 * m + j) % 4][:, P * a:P * (a + 1)],
                                              a == 0, a == len(values) - 1)
                            last.then_inc(filled, 1)
                        if mod_beside(i):
                            modulation(mod_beside(i))
                    pe.wait_ge(bra_ready, GLA_H)
                    pe.wait_ge(brb_ready, 4)
                    wait_moved(pe, ("pv", UNITS // 2 - 1))
                    for half in range(2):
                        for n in range(3):
                            wb = view(wait_block(pe, ("wb", half, n)), 4)
                            for q in range(4):
                                if q % 2 == 0:
                                    w = view(wait_block(pe, ("mg", half, n, q // 2)), KD)
                                feature_major(("gate", half, n, q), w, h3, slice(P * (q % 2), P * (q % 2) + P))
                                feature_major(("proj", half, n, q), wb, br3, slice(P * q, P * (q + 1)), 4 * n)

                    def row(v):
                        base, cond = ((16, 1), (16, 0), (32, 1), (32, 0), (24, 1), (24, 0), (40, 1), (40, 0))[v]
                        ps = wait_slot(pe, ("row", v))
                        for k in range(KD):
                            last = mm(ps[:, P * k:P * (k + 1)], mod3[:, base + k, cond:cond + 1].to_broadcast([P, P]), ident, True, True)
                        last.then_inc(filled, 1)

                    pe.wait_ge(mod_ready, 2)
                    for v in range(6):
                        row(v)
                    pe.wait_ge(merged, KD)
                    w = [view(wait_block(pe, ("wout", cb)), KD) for cb in range(4)]
                    for t in range(T + 2):
                        for cb in range(4 if t < T else 0):
                            ps = wait_slot(pe, ("y", t, cb))
                            for k in range(KD):
                                last = mm(ps[:, 0:256], mg3[:, k, P * t:P * (t + 1)], w[cb][:, k, :], k == 0, k == KD - 1)
                            last.then_inc(filled, 1)
                        if t >= 2:
                            pe.wait_ge(h2_ready, t - 1)
                            ps = wait_slot(pe, ("h2T", t - 2))
                            for k in range(KD):
                                last = turn(ps[:, P * k:P * (k + 1)], h2[:, t - 2, P * k:P * (k + 1)])
                            last.then_inc(filled, 1)
                    pe.wait_ge(router_in, 16 * 4)
                    wait_moved(pe, ("h2T", T - 1))
                    ps = wait_slot(pe, ("logit",))
                    for t in range(T):
                        for k in range(KD):
                            last = mm(ps[:, 32 * t:32 * t + LOGITS], h3[:, k, P * t:P * (t + 1)], rw[:, LOGITS * k:LOGITS * (k + 1)],
                                      k == 0, k == KD - 1)
                    last.then_inc(filled, 1)
                    pe.wait_ge(masks_ready, 1)
                    ps = wait_slot(pe, ("rank",))
                    for t in range(T + 1):
                        for u in range(min(t + 1, T)):
                            last = mm(ps[:, NE * t:NE * (t + 1)], cst("before") if u == t else cst("ones"),
                                      R["M"][:, NE * u:NE * (u + 1)], u == 0, u == min(t, T - 1))
                    last.then_inc(filled, 1)
                    for v in range(6, 8):
                        row(v)

                    def gate_up(j, n):
                        wait_moved(pe, ("xg", j), 4 * n)
                        wait_block(pe, ("gate", j), 16 * n)
                        wait_block(pe, ("up", j), 16 * n)
                        strip = view(ring[:, 3 * (j % 2) * BLK:(3 * (j % 2) + 2) * BLK], KD)
                        ps = slot(("gu", j))
                        for k in range(KD):
                            last = mm(ps[:, 0:2 * FF], xgT[j % 2][:, k, :], strip[:, k, :], k == 0, k == KD - 1)
                        last.then_inc(filled, 1)

                    def down(j, n):
                        wait_moved(pe, ("ht", j), 4 * n)
                        w = view(wait_block(pe, ("down", j), 16 * n), 2)
                        ps = slot(("dn", j))
                        for half in range(2):
                            for f in range(2):
                                last = mm(ps[:, 512 * half:512 * (half + 1)], hidT[j % 2][:, f, :], w[:, f, 512 * half:512 * (half + 1)],
                                          f == 0, f == 1)
                        last.then_inc(filled, 1)

                    def rows_turned(j, n):
                        pe.wait_ge(xg_in[j % 2], 16 * (j // 2 + 1) + 16 * n)
                        ps = slot(("xg", j))
                        for k in range(KD):
                            last = turn(ps[:, P * k:P * (k + 1)], xg[j % 2][:, P * k:P * (k + 1)])
                        last.then_inc(filled, 1)

                    def hidden_turned(j, n):
                        wait_moved(pe, ("gu", j), 4 * n)
                        ps = slot(("ht", j))
                        for f in range(2):
                            last = turn(ps[:, P * f:P * (f + 1)], hid[:, P * f:P * (f + 1)])
                        last.then_inc(filled, 1)

                    wait_slot(pe, ("xg", 0))
                    rows_turned(0, 0)
                    for j in range(2):
                        wait_slot(pe, ("gu", j))
                        gate_up(j, 0)
                        if j:
                            wait_slot(pe, ("dn", 0))
                            down(0, 0)
                        wait_slot(pe, ("xg", j + 1))
                        rows_turned(j + 1, 0)
                        wait_slot(pe, ("ht", j))
                        hidden_turned(j, 0)
                    pairs = pe.value_load(exi[0:1, TILES:TILES + 1], min_val=1, max_val=TILES // 2)
                    with pe.Fori(1, TILES // 2) as i:
                        with pe.If(i < pairs):
                            for j in range(2, 4):
                                gate_up(j, i - 1)
                                down(j - 1, i - 1)
                                rows_turned(j + 1, i - 1)
                                hidden_turned(j, i - 1)
                    down(1, pairs - 1)

                @block.scalar
                def _(act):
                    step = Steps(act, act_step)

                    def f(out, in_, func, **kw):
                        return nc.scalar.activation(out, in_, func, **kw)

                    def moved(instruction):
                        instruction.then_inc(act_moved, 1)

                    for dst, src in vector_loads(l):
                        act.dma_start(dst, src).then_inc(vectors_in, 16)
                    def root(t, before):
                        act.wait_ge(var_ready, before + t + 1)
                        f(st[:, 40 + t:41 + t], st[:, 13 + 2 * t:14 + 2 * t], ACT.Sqrt, bias=eps).then_inc(std_ready, 1)

                    wait_moved(act, ("vec",))
                    f(cs[:, :], vec[:, 56:72], ACT.Silu).then_inc(cond_ready, 1)
                    act.wait_ge(mod_ready, 1)
                    for k in range(1, KD, 2):
                        ps = wait_filled(act, ("hT", k))
                        f(h3[:, k, 0:P], ps[:, 0:P], ACT.Identity, scale=mod3[:, 8 + k, 1:2], bias=mod3[:, k, 1:2])
                        moved(f(h3[:, k, P:TOK], ps[:, P:TOK], ACT.Identity, scale=mod3[:, 8 + k, 0:1], bias=mod3[:, k, 0:1]))
                    ps = wait_filled(act, ("lr",))
                    moved(f(tok2(lr[0:32, :]), ps2(ps)[0:32], ACT.Copy))
                    for c in range(2):
                        ps = wait_filled(act, ("aq", c))
                        moved(f(tok2(aqk[:, c, :]), ps2(ps), ACT.Copy, scale=DK ** -0.5))
                    for c in range(4):
                        ps = wait_filled(act, ("z", c))
                        if c:
                            act.wait_ge(qk_ready, c)
                        f(tok2(bufA), ps2(ps), ACT.Abs, bias=vec[:, V_GB + c:V_GB + c + 1]).then_inc(abs_done, 1)
                        act.wait_ge(abs_done, c + 1)
                        step(f(bufA, bufA, ACT.Exp, scale=-1.0))
                        f(bufA, bufA, ACT.Ln, bias=1.0).then_inc(softplus, 1)
                        name, dst = ("vtok", vtok) if c < 2 else ("av", av)
                        for t in range(T):
                            ps = wait_filled(act, (name, c % 2, t))
                            moved(f(dst[:, t, 256 * (c % 2):256 * (c % 2 + 1)], ps[:, 0:256], ACT.Gelu_apprx_tanh if c < 2 else ACT.Copy))
                        act.wait_ge(decay_ready, c + 1)
                        f(bufA, bufB, ACT.Exp, scale=1.0 / GLA_TAU)
                        f(bufM, bufB, ACT.Exp, scale=-1.0 / GLA_TAU)
                        f(er[:, 15 * c:15 * c + 15], er[:, 15 * c:15 * c + 15], ACT.Exp, scale=1.0 / GLA_TAU).then_inc(exp_ready, 1)
                    for c in range(4):
                        ps = wait_filled(act, ("ag", c))
                        moved(f(tok2(br3[:, c, :]), ps2(ps), ACT.Silu))
                    act.wait_ge(var_ready, T)
                    f(st[:, 40:45], st[:, 12:22].rearrange("p (t v) -> p t v", v=2)[:, :, 1], ACT.Sqrt, bias=eps).then_inc(std_ready, 1)
                    for c in range(4):
                        ps = wait_filled(act, ("u", c))
                        moved(f(tok2(br3[:, 4 + c, :]), ps2(ps), ACT.Gelu_apprx_tanh))
                    ps = wait_filled(act, ("wsT",))
                    moved(f(wsT[:, :], ps[:, 0:512], ACT.Copy))
                    ps = wait_filled(act, ("kcT",))
                    moved(f(kcT.rearrange("p g t -> p (g t)"), ps[:, 0:512], ACT.Copy))
                    for c in range(4):
                        ps = wait_filled(act, ("ktok", c))
                        if c >= 2:
                            wait_filled(act, ("kv", c - 2))
                        moved(f(ktok[c % 2], ps[:, 0:TOK], ACT.Copy))
                    for p in range(PAIRS):
                        for t in range(T):
                            ps = wait_filled(act, ("o", p, t))
                            moved(f(oT[:, 2 * p:2 * p + 2, P * t:P * (t + 1)], ps.rearrange("p (j t) -> p j t", j=2)[:, :, 0:P], ACT.Copy))
                    for h in range(GLA_H + 1):
                        if h < GLA_H:
                            wait_moved(act, ("o", PAIRS - 1, T - 1))
                            if h >= 2:
                                act.wait_ge(bra_ready, h - 1)
                            f(sq[h % 2], oT[:, h, :], ACT.Square).then_inc(square_ready, 1)
                        if h:
                            ps = wait_filled(act, ("ms", h - 1))
                            moved(f(tok2(sq[(h - 1) % 2]), ps2(ps), ACT.Sqrt, scale=1.0 / DV, bias=eps))
                    act.wait_ge(kv_out, 16 * 6)
                    for i in range(UNITS + 2):
                        if i < UNITS:
                            n, h = divmod(i, HEADS)
                            ps = wait_filled(act, ("s", i))
                            act.wait_ge(negmax, i + 1)
                            if i >= 3:
                                wait_filled(act, ("pT", i - 3))
                            nm, rsum, es = (sm[:, 3 * a + i % 3:3 * a + i % 3 + 1] for a in range(3))
                            moved(f(pbuf[i % 3][:, 0:keys_of(n)], ps[:, 0:keys_of(n)], ACT.Exp, scale=HD ** -0.5, bias=nm, accum_out=rsum))
                            f(es, sink[:, h:h + 1], ACT.Exp, bias=nm).then_inc(esink, 1)
                        if i >= 2:
                            u = i - 2
                            n = u // HEADS
                            ps = wait_filled(act, ("pT", u))
                            if u >= 4:
                                wait_filled(act, ("pv", (u - 4) // 2))
                            moved(f(pTbuf[u % 4][:, 0:keys_of(n)], ps[:, 0:keys_of(n)], ACT.Copy))
                    m = 0
                    for half in range(2):
                        for n in range(3):
                            for q in range(4):
                                ps = wait_filled(act, ("gate", half, n, q))
                                if m >= 2:
                                    before = divmod(m - 2, 12)
                                    wait_moved(act, ("proj", before[0], before[1] // 4, before[1] % 4))
                                moved(f(tok2(sig[m % 2]), ps2(ps), ACT.Sigmoid))
                                m += 1
                    for v in range(6):
                        ps = wait_filled(act, ("row", v))
                        dst = bcA[:, v, :] if v < 2 else bcB[:, v - 2, :]
                        moved(f(dst, ps, ACT.Copy))
                    for t in range(T + 2):
                        if t < T:
                            root(t, T)
                        if t >= 2:
                            u = t - 2
                            ps = wait_filled(act, ("h2T", u))
                            moved(f(h3[:, :, P * u:P * (u + 1)], ps.rearrange("p (k t) -> p k t", k=KD), ACT.Copy))
                    act.wait_ge(gexp_in, 1)
                    f(R["ge"], R["ge"], ACT.Exp).then_inc(gexp, 1)
                    act.wait_ge(gexp_in, 2)
                    f(R["dq"], R["dq"], ACT.Exp).then_inc(gexp, 1)
                    for v in range(6, 8):
                        ps = wait_filled(act, ("row", v))
                        act.wait_ge(x1_done, T)
                        moved(f(bcA[:, v - 6, :], ps, ACT.Copy))
                    def silu_of(s, more):
                        ps = wait_filled(act, ("gu", s), more)
                        f(silu, ps[:, 0:FF], ACT.Silu).then_inc(silu_ready, 1)

                    def hidden_moved(s, more):
                        ps = wait_filled(act, ("ht", s), more)
                        moved(f(hidT[s % 2], ps[:, 0:2 * P].rearrange("p (f s) -> p f s", f=2), ACT.Copy))

                    def rows_stored(s, more, stores, tile):
                        ps = wait_filled(act, ("dn", s), more)
                        act.wait_ge(y_stored[s % 2], 16 * stores + 16)
                        moved(f(ys[s % 2], ps, ACT.Copy))
                        wait_moved(act, ("dn", s), moved_more)
                        act.dma_start(rows[bass.ds(P * tile, P), :], ys[s % 2]).then_inc(y_stored[s % 2], 16)

                    for s in range(2):
                        act.sem_inc(y_stored[s], 16)
                    moved_more = 0
                    silu_of(0, 0)
                    hidden_moved(0, 0)
                    silu_of(1, 0)
                    rows_stored(0, 0, 0, 0)
                    hidden_moved(1, 0)
                    pairs = act.value_load(exi[0:1, TILES:TILES + 1], min_val=1, max_val=TILES // 2)
                    with act.Fori(1, TILES // 2) as i:
                        with act.If(i < pairs):
                            more = 2 * PER_TILE * (i - 1)
                            moved_more = 4 * (i - 1)
                            for s in range(2):
                                silu_of(2 + s, more)
                                rows_stored(1 + s, more, i - 1 + s, 2 * i - 1 + s)
                                hidden_moved(2 + s, more)
                    moved_more = 4 * (pairs - 1)
                    rows_stored(1, 2 * PER_TILE * (pairs - 1) - 1, pairs - 1, 2 * pairs - 1)
                    for s in range(2):
                        act.wait_ge(y_stored[s], 16 * pairs + 16)
                    act.sem_inc(experts_done, 1)
                    for t in range(T + 1):
                        if t < T:
                            act.wait_ge(yg_in[t % 2][0], 16 * (t // 2 + 1))
                            if t >= 2:
                                act.wait_ge(yg_used, t - 1)
                            f(ysum[t % 2], yg[t % 2][0], ACT.Copy, scale=R["w1"][:, t:t + 1]).then_inc(first_scaled, 1)
                        if t:
                            u = t - 1
                            root(u, 2 * T)
                            act.wait_ge(rs_ready, u + 1)
                            f(x3[:, u, :], x3[:, u, :], ACT.Identity, scale=st[:, 50 + u:51 + u], bias=st[:, 56 + u:57 + u])\
                                .then_inc(x_norm, 1)

                @block.vector
                def _(dve):
                    step = Steps(dve, dve_step)
                    V = nc.vector

                    def moved(instruction):
                        instruction.then_inc(dve_moved, 1)

                    def bc(ap, shape):
                        return ap.to_broadcast(shape)

                    def tt(out, a, b, op):
                        return V.tensor_tensor(out, a, b, op)

                    def stats(x, t, width):
                        parts = width // 512
                        for i in range(parts):
                            last = V.bn_stats(st[:, 6 * i:6 * i + 6], x[:, 512 * i:512 * (i + 1)])
                        step(last)
                        V.bn_aggr(st[:, 12 + 2 * t:14 + 2 * t], st[:, 0:6 * parts]).then_inc(var_ready, 1)
                        dve.wait_ge(var_ready, var_before + t + 1)

                    def normalise(x, t):
                        step(V.tensor_scalar(x, x, st[:, 12 + 2 * t:13 + 2 * t], st[:, 50 + t:51 + t], ALU.subtract, ALU.mult))

                    def one_hot(out, x, top, size):
                        x3_, o3 = (a.rearrange("p (t g) -> p t g", t=T) for a in (x, out))
                        g3 = R["gx"].rearrange("p (t g) -> p t g", t=T)
                        step(tt(g3, x3_, bc(top.unsqueeze(2), [P, T, size]), ALU.is_equal))
                        step(tt(g3, g3, bc(cst("first").unsqueeze(1), [P, T, size]), ALU.mult))
                        step(V.tensor_reduce(R["gs"], g3, AXL.X, ALU.max))
                        step(tt(o3, g3, bc(R["gs"].unsqueeze(2), [P, T, size]), ALU.is_equal))

                    ps = wait_filled(dve, ("vec",))
                    moved(V.tensor_copy(vec[:, :], ps[:, 0:72]))
                    wait_moved(dve, ("vec",))

                    def modulation(b):
                        ps = wait_filled(dve, ("mod", b))
                        moved(tt(mod3[:, 2 * b:2 * b + 2, :], ps[:, 0:4].rearrange("p (f c) -> p f c", c=2),
                                 bc(vec[:, 2 * b:2 * b + 2].unsqueeze(2), [P, 2, 2]), ALU.add))

                    for b in range(MOD_FIRST):
                        modulation(b)
                    wait_moved(dve, ("mod", MOD_FIRST - 1))
                    V.tensor_scalar(mod[:, 16:32], mod[:, 16:32], 1.0, None, ALU.add).then_inc(mod_ready, 1)
                    dve.wait_ge(mod_ready, 1)
                    for k in range(0, KD, 2):
                        ps = wait_filled(dve, ("hT", k))
                        V.tensor_scalar(h3[:, k, 0:P], ps[:, 0:P], mod3[:, 8 + k, 1:2], mod3[:, k, 1:2], ALU.mult, ALU.add)
                        moved(V.tensor_scalar(h3[:, k, P:TOK], ps[:, P:TOK], mod3[:, 8 + k, 0:1], mod3[:, k, 0:1], ALU.mult, ALU.add))
                    for c in range(2):
                        ps = wait_filled(dve, ("ak", c))
                        moved(V.tensor_copy(tok2(aqk[:, 2 + c, :]), ps2(ps)))
                    for c in range(4):
                        d = c // 2
                        ps = wait_filled(dve, ("z", c))
                        dve.wait_ge(abs_done, c + 1)
                        moved(V.tensor_scalar(tok2(bufM), ps2(ps), vec[:, V_GB + c:V_GB + c + 1], 0.0, ALU.add, ALU.min))
                        wait_moved(dve, ("z", c))
                        dve.wait_ge(softplus, c + 1)
                        step(tt(bufM, bufM, bufA, ALU.subtract))
                        if d == 0:
                            step(V.tensor_tensor_scan(bufB, cst("run"), bufM, 0.0, ALU.mult, ALU.add))
                        else:
                            step(V.tensor_tensor_scan(bufB[:, ::-1], cst("run"), bufM[:, ::-1], 0.0, ALU.mult, ALU.add))
                        B3 = bufB.rearrange("p (t s) -> p t s", t=T)
                        e3 = er[:, 15 * c:15 * c + 15].rearrange("p (a t) -> p a t", a=3)
                        end = P - 1 if d == 0 else 0
                        step(V.tensor_copy(e3[:, 0, :], B3[:, :, P // 2]))
                        step(V.tensor_copy(e3[:, 2, :], B3[:, :, end]))
                        step(tt(e3[:, 1, :], e3[:, 2, :], e3[:, 0, :], ALU.subtract))
                        tt(B3, B3, bc(e3[:, 0, :].unsqueeze(2), [P, T, P]), ALU.subtract).then_inc(decay_ready, 1)
                        dve.wait_ge(exp_ready, c + 1)
                        tt(mg3[:, c, :], aqk[:, c % 2, :], bufA, ALU.mult)
                        tt(mg3[:, 4 + c, :], aqk[:, 2 + c % 2, :], bufM, ALU.mult).then_inc(qk_ready, 1)
                    wait_moved(dve, ("vtok", 1, T - 1))
                    var_before = 0
                    for t in range(T):
                        stats(vtok[:, t, :], t, 512)
                    dve.wait_ge(std_ready, 1)
                    step(V.reciprocal(st[:, 50:55], st[:, 40:45]))
                    for t in range(T):
                        normalise(vtok[:, t, :], t)
                    dve.wait_ge(mixer_in, 16 * N_MIXER)
                    V.tensor_scalar(sink[:, HEADS:2 * HEADS], sink[:, 0:HEADS], -1.0, None, ALU.mult)
                    step(tt(vtok, vtok, bc(lng.unsqueeze(1), [P, T, 512]), ALU.mult))
                    tt(vtok, vtok, bc(lnb.unsqueeze(1), [P, T, 512]), ALU.add).then_inc(vn_ready, 1)
                    dve.wait_ge(vn_ready, 1)
                    for c in range(4):
                        ps = wait_filled(dve, ("cq", c))
                        moved(V.tensor_copy(tok2(br3[:, 8 + c, :]), ps2(ps)))
                    for t in range(T):
                        ps = wait_filled(dve, ("ckv", t))
                        moved(V.tensor_copy(kvt[:, t, :], ps[:, 0:256]))
                    for g in range(KV_HEADS):
                        ps = wait_filled(dve, ("kT", g))
                        moved(V.tensor_copy(kT[:, g, :], ps[:, 0:TOK]))
                    for c in range(4 + KV_HEADS):
                        x = br3[:, 8 + c, P:TOK] if c < 4 else kT[:, c - 4, P:TOK]
                        ps = wait_filled(dve, ("rot", c))
                        moved(tt(tmp5[:, 0:4 * P], ps[:, 0:4 * P], cst("sin"), ALU.mult))
                        step(tt(x, x, cst("cos"), ALU.mult))
                        wait_moved(dve, ("rot", c))
                        tt(x, x, tmp5[:, 0:4 * P], ALU.add).then_inc(rope_ready, 1)
                        dve.wait_ge(rope_ready, c + 1)
                    for g in range(4):
                        ps = wait_filled(dve, ("mix", g))
                        bias = bc(bsb[:, P * g:P * (g + 1)].unsqueeze(1), [P, T, P])
                        moved(tt(tmp5.rearrange("p (t s) -> p t s", t=T), ps[:, 0:TOK].rearrange("p (t s) -> p t s", t=T), bias, ALU.add))
                        wait_moved(dve, ("mix", g))
                        wait_moved(dve, ("u", g))
                        tt(br3[:, 4 + g, :], br3[:, 4 + g, :], tmp5, ALU.mult).then_inc(brb_ready, 1)
                        dve.wait_ge(brb_ready, g + 1)
                    for c in range(4):
                        d = c // 2
                        e3 = er[:, 15 * c:15 * c + 15].rearrange("p (a t) -> p a t", a=3)
                        ps = wait_filled(dve, ("kv", c))
                        moved(tt(t1[:, c, :, :], ps[:, 0:TOK].rearrange("p (t v) -> p t v", t=T), bc(e3[:, 1, :].unsqueeze(2), [P, T, P]), ALU.mult))
                        wait_moved(dve, ("kv", c))
                        now, nxt = s0[:, c, :], spare
                        order = [1, 2, 3, 4] if d == 0 else [4, 3, 2, 1]
                        for n, t in enumerate(order):
                            if n < 3:
                                step(V.scalar_tensor_tensor(out=nxt, in0=now, scalar=e3[:, 2, t:t + 1], in1=t1[:, c, t, :],
                                                               op0=ALU.mult, op1=ALU.add))
                            last = V.tensor_scalar(t1[:, c, t, :], now, e3[:, 0, t:t + 1], None, ALU.mult)
                            if n < 3:
                                step(last)
                            now, nxt = nxt, now
                        last.then_inc(states_in, 1)
                        dve.wait_ge(states_in, c + 1)
                    mask = bc(cst("gla_mask").unsqueeze(1), [P, 2, 2 * P])
                    for p in range(PAIRS):
                        for t in range(T):
                            ps = wait_filled(dve, ("gs", p, t))
                            if t >= 2:
                                wait_filled(dve, ("o", p, t - 2))
                            elif p:
                                wait_filled(dve, ("o", p - 1, T - 1))
                            moved(tt(gsb[t % 2].rearrange("p (j c) -> p j c", j=2), ps.rearrange("p (j c) -> p j c", j=2)[:, :, 0:2 * P], mask, ALU.mult))
                    for h in range(GLA_H):
                        wait_moved(dve, ("ms", h))
                        wait_moved(dve, ("ag", h))
                        step(V.reciprocal(sq[h % 2], sq[h % 2]))
                        step(V.scalar_tensor_tensor(out=oT[:, h, :], in0=oT[:, h, :], scalar=vec[:, V_NORM + h:V_NORM + h + 1],
                                                       in1=sq[h % 2], op0=ALU.mult, op1=ALU.mult))
                        tt(br3[:, h, :], br3[:, h, :], oT[:, h, :], ALU.mult).then_inc(bra_ready, 1)
                    for i in range(UNITS + 3):
                        if i < UNITS:
                            n, h = divmod(i, HEADS)
                            ps = wait_filled(dve, ("s", i))
                            if i >= 3:
                                dve.wait_ge(esink, i - 2)
                            step(V.tensor_reduce(sm[:, 9 + i % 2:10 + i % 2], ps[:, 0:keys_of(n)], AXL.X, ALU.max))
                            V.tensor_scalar(sm[:, i % 3:i % 3 + 1], sm[:, 9 + i % 2:10 + i % 2], -(HD ** -0.5), sink[:, HEADS + h:HEADS + h + 1],
                                            ALU.mult, ALU.min).then_inc(negmax, 1)
                        if 1 <= i <= UNITS:
                            u = i - 1
                            dve.wait_ge(esink, u + 1)
                            step(tt(sm[:, 11:12], sm[:, 3 + u % 3:4 + u % 3], sm[:, 6 + u % 3:7 + u % 3], ALU.add))
                            step(V.reciprocal(sm[:, 12:13], sm[:, 11:12]))
                            if u >= 3:
                                wait_filled(dve, ("pT", u - 3))
                            V.tensor_scalar(diag[u % 3], ident, sm[:, 12:13], None, ALU.mult).then_inc(p_ready, 1)
                        if i >= 4 and i % 2 == 0:
                            m = (i - 4) // 2
                            n, pair = divmod(m, HEADS // 2)
                            ps = wait_filled(dve, ("pv", m))
                            moved(V.tensor_copy(br3[:, 8 + pair, P * n:P * (n + 1)], ps[:, 0:P]))
                        if mod_beside(i):
                            modulation(mod_beside(i))
                    wait_moved(dve, ("mod", MOD_ALL - 1))
                    V.tensor_scalar(mod[:, 64:80], mod[:, 64:80], 1.0, None, ALU.add).then_inc(mod_ready, 1)
                    m = 0
                    for half in range(2):
                        for n in range(3):
                            for q in range(4):
                                out = tok2(mg3[:, 4 * half + q, :])
                                ps = wait_filled(dve, ("proj", half, n, q))
                                wait_moved(dve, ("gate", half, n, q))
                                if n == 0:
                                    moved(tt(out, ps2(ps), tok2(sig[m % 2]), ALU.mult))
                                else:
                                    moved(tt(tok2(gtmp), ps2(ps), tok2(sig[m % 2]), ALU.mult))
                                    wait_moved(dve, ("proj", half, n, q))
                                    last = tt(out, out, tok2(gtmp), ALU.add)
                                    if n == 2:
                                        last.then_inc(merged, 1)
                                        dve.wait_ge(merged, 4 * half + q + 1)
                                    else:
                                        step(last)
                                m += 1
                    dve.wait_ge(merged, KD)
                    dve.wait_ge(x_back, 16)
                    wait_moved(dve, ("row", 5))
                    dve.wait_ge(ln_rows, 16 * 2)
                    var_before = T
                    for t in range(T + 1):
                        if t < T:
                            for cb in range(4):
                                cols = slice(256 * cb, 256 * (cb + 1))
                                ps = wait_filled(dve, ("y", t, cb))
                                moved(tt(ytmp, ps[:, 0:256], bcA[:, 0 if t == 0 else 1, cols], ALU.mult))
                                wait_moved(dve, ("y", t, cb))
                                step(V.scalar_tensor_tensor(out=x3[:, t, cols], in0=x3[:, t, cols], scalar=ALPHA, in1=ytmp,
                                                               op0=ALU.mult, op1=ALU.add))
                            stats(x3[:, t, :], t, D)
                        if t:
                            u = t - 1
                            dve.wait_ge(std_ready, 1 + u + 1)
                            step(V.reciprocal(st[:, 50 + u:51 + u], st[:, 40 + u:41 + u]))
                            normalise(x3[:, u, :], u)
                            step(tt(x3[:, u, :], x3[:, u, :], bcA[:, 2, :], ALU.mult))
                            tt(x3[:, u, :], x3[:, u, :], bcA[:, 3, :], ALU.add).then_inc(x1_done, 1)
                            c = 0 if u == 0 else 1
                            dve.wait_ge(x1_done, u + 1)
                            step(tt(h2[:, u, :], x3[:, u, :], bcB[:, c, :], ALU.mult))
                            tt(h2[:, u, :], h2[:, u, :], bcB[:, 2 + c, :], ALU.add).then_inc(h2_ready, 1)
                    ps = wait_filled(dve, ("logit",))
                    lg = R["lg"].rearrange("p (t c) -> p t c", t=T)
                    moved(tt(lg, ps[:, 0:32 * T].rearrange("p (t c) -> p t c", c=32)[:, :, 0:LOGITS],
                             bc(rb[:, :].unsqueeze(1), [P, T, LOGITS]), ALU.add))
                    wait_moved(dve, ("logit",))
                    ge = R["ge"].rearrange("p (t g) -> p t g", t=T)
                    step(V.tensor_reduce(R["gm"], lg[:, :, 0:NG], AXL.X, ALU.max))
                    step(tt(ge, lg[:, :, 0:NG], bc(R["gm"].unsqueeze(2), [P, T, NG]), ALU.subtract))
                    step(V.memset(R["m1"], 0.0))
                    one_hot(R["G"], R["ge"], R["m1"], NG)
                    V.tensor_copy(R["es"], R["G"]).then_inc(gexp_in, 1)
                    dve.wait_ge(gexp, 1)
                    step(V.tensor_reduce(R["gs"], ge, AXL.X, ALU.add))
                    step(V.reciprocal(R["gp"], R["gs"]))
                    G3 = R["G"].rearrange("p (t g) -> p t g", t=T)
                    big = R["big"].rearrange("p (t g e) -> p t g e", t=T, g=NG)
                    el = lg[:, :, NG:LOGITS].rearrange("p t (g e) -> p t g e", g=NG)
                    step(tt(big, el, bc(G3.unsqueeze(3), [P, T, NG, EG]), ALU.mult))
                    es3 = R["es"].rearrange("p (t e) -> p t e", t=T)
                    step(V.tensor_reduce(es3, big.rearrange("p t g e -> p t e g"), AXL.X, ALU.add))
                    step(V.tensor_reduce(R["m1"], es3, AXL.X, ALU.max))
                    one_hot(R["E1"], R["es"], R["m1"], EG)
                    step(V.scalar_tensor_tensor(out=R["e2"], in0=R["E1"], scalar=-BIG, in1=R["es"], op0=ALU.mult, op1=ALU.add))
                    step(V.tensor_reduce(R["m2"], R["e2"].rearrange("p (t e) -> p t e", t=T), AXL.X, ALU.max))
                    one_hot(R["E2"], R["e2"], R["m2"], EG)
                    tt(R["dq"], R["m2"], R["m1"], ALU.subtract).then_inc(gexp_in, 1)
                    dve.wait_ge(gexp, 2)
                    step(V.tensor_scalar(R["gs"], R["dq"], 1.0, None, ALU.add))
                    step(V.reciprocal(R["gs"], R["gs"]))
                    step(tt(R["w1"], R["gp"], R["gs"], ALU.mult))
                    step(tt(R["w2"], R["w1"], R["dq"], ALU.mult))
                    for name, one in (("M1", "E1"), ("M2", "E2")):
                        m4 = R[name].rearrange("p (t g e) -> p t g e", t=T, g=NG)
                        e4 = R[one].rearrange("p (t e) -> p t e", t=T).unsqueeze(2)
                        step(V.tensor_copy(m4, bc(G3.unsqueeze(3), [P, T, NG, EG])))
                        step(tt(m4, m4, bc(e4, [P, T, NG, EG]), ALU.mult))
                    tt(R["M"], R["M1"], R["M2"], ALU.add).then_inc(masks_ready, 1)
                    ps = wait_filled(dve, ("rank",))
                    moved(V.tensor_copy(R["rk"], ps[:, 0:NE * (T + 1)]))
                    wait_moved(dve, ("rank",))
                    cmp3 = R["cmp"].rearrange("p (e j) -> p e j", e=NE)
                    step(tt(cmp3, bc(R["rk"][:, NE * T:NE * (T + 1)].unsqueeze(2), [P, NE, 5]), bc(cst("over").unsqueeze(1), [P, NE, 5]), ALU.is_gt))
                    step(V.tensor_reduce(R["nt"], cmp3, AXL.X, ALU.add))
                    step(V.tensor_tensor_scan(R["end"], cst("ones")[:, 0:NE], R["nt"], 0.0, ALU.mult, ALU.add))
                    step(tt(R["base"], R["end"], R["nt"], ALU.subtract))
                    step(V.tensor_scalar(R["base"], R["base"], float(P), None, ALU.mult))
                    rk3 = R["rk"][:, 0:NE * T].rearrange("p (t e) -> p t e", t=T)
                    step(tt(rk3, rk3, bc(R["base"].unsqueeze(1), [P, T, NE]), ALU.add))
                    pos3 = R["pos"].rearrange("p (t w) -> p t w", w=2)
                    for w, name in enumerate(("M1", "M2")):
                        m3 = R[name].rearrange("p (t e) -> p t e", t=T)
                        step(tt(m3, m3, rk3, ALU.mult))
                        step(V.tensor_reduce(pos3[:, :, w], m3, AXL.X, ALU.add))
                    step(V.tensor_copy(posi[:, :], R["pos"]))
                    exc = R["exc"].rearrange("p (j e) -> p j e", j=TILES)
                    step(tt(exc, bc(cst("tile").unsqueeze(2), [P, TILES, NE]), bc(R["end"].unsqueeze(1), [P, TILES, NE]), ALU.is_ge))
                    step(V.tensor_reduce(R["ex"][:, 0:TILES], exc, AXL.X, ALU.add))
                    step(V.tensor_scalar(R["pairs"], cst("tile")[:, 0:TILES // 2], 2.0, R["end"][:, NE - 1:NE], ALU.mult, ALU.is_lt))
                    step(V.tensor_reduce(R["ex"][:, TILES:TILES + 1], R["pairs"], AXL.X, ALU.add))
                    V.tensor_scalar(exi[:, :], R["ex"], float(NE - 1), None, ALU.min).then_inc(route_ready, 1)
                    def rows_moved(s, more):
                        ps = wait_filled(dve, ("xg", s), more)
                        moved(V.tensor_copy(xgT[s % 2], ps.rearrange("p (k s) -> p k s", k=KD)))

                    def hidden(s, more, tile):
                        ps = wait_filled(dve, ("gu", s), more)
                        dve.wait_ge(silu_ready, tile + 1)
                        moved(tt(hid, ps[:, FF:2 * FF], silu, ALU.mult))

                    rows_moved(0, 0)
                    for s in range(2):
                        hidden(s, 0, s)
                        rows_moved(s + 1, 0)
                    pairs = dve.value_load(exi[0:1, TILES:TILES + 1], min_val=1, max_val=TILES // 2)
                    with dve.Fori(1, TILES // 2) as i:
                        with dve.If(i < pairs):
                            more = 2 * PER_TILE * (i - 1)
                            for s in range(2):
                                hidden(2 + s, more, 2 * i + s)
                                rows_moved(3 + s, more)
                    var_before = 2 * T
                    wait_moved(dve, ("row", 7))
                    dve.wait_ge(ln_rows, 16 * 4)
                    for t in range(T + 1):
                        if t < T:
                            x, out = x3[:, t, :], ysum[t % 2]
                            dve.wait_ge(first_scaled, t + 1)
                            dve.wait_ge(yg_in[t % 2][1], 16 * (t // 2 + 1))
                            step(V.scalar_tensor_tensor(out=out, in0=yg[t % 2][1], scalar=R["w2"][:, t:t + 1], in1=out,
                                                        op0=ALU.mult, op1=ALU.add))
                            step(tt(out, out, bcA[:, 0 if t == 0 else 1, :], ALU.mult))
                            V.scalar_tensor_tensor(out=x, in0=x, scalar=ALPHA, in1=out, op0=ALU.mult, op1=ALU.add).then_inc(yg_used, 1)
                            dve.wait_ge(yg_used, t + 1)
                            stats(x, t, D)
                            dve.wait_ge(std_ready, 1 + T + t + 1)
                            step(V.reciprocal(st[:, 50 + t:51 + t], st[:, 40 + t:41 + t]))
                            V.scalar_tensor_tensor(out=st[:, 56 + t:57 + t], in0=st[:, 12 + 2 * t:13 + 2 * t], scalar=-1.0,
                                                   in1=st[:, 50 + t:51 + t], op0=ALU.mult, op1=ALU.mult).then_inc(rs_ready, 1)
                        if t:
                            u = t - 1
                            dve.wait_ge(x_norm, u + 1)
                            step(tt(x3[:, u, :], x3[:, u, :], bcA[:, 2, :], ALU.mult))
                            tt(x3[:, u, :], x3[:, u, :], bcA[:, 3, :], ALU.add).then_inc(x2_done, 1)

            nc.gpsimd.dma_reset()
            for semaphore in per_layer:
                nc.gpsimd.sem_clear(semaphore)
            nc.all_engine_barrier()


def launch_arrays(nc, arrays):
    A = {}
    for name, a in arrays.items():
        A[name] = nc.dram_tensor(f"in_{name}_dram", a.shape, mybir.dt.from_np(a.dtype), kind="ExternalInput").ap()
    for name, shape in _OUTS:
        A[name] = nc.dram_tensor(f"out_{name}_dram", shape, F32, kind="ExternalOutput").ap()
    A["rows"] = nc.dram_tensor("rows", ((TILES + 1) * P, D), F32, kind="Internal").ap()
    return A





def kernel(**inputs):
    import concourse.bacc as _bacc
    from concourse.bass_utils import run_bass_kernel_spmd as _run

    arrays = {n: np.ascontiguousarray(inputs[n]) for n in _INS[2:]}
    arrays["x"] = np.concatenate([np.asarray(inputs["x_prompt"])[0], np.asarray(inputs["x_sample"])[0]], 0)
    arrays["const"] = const_tile()
    nc = _bacc.Bacc("TRN2", target_bir_lowering=False, num_devices=1)
    build_program(nc, launch_arrays(nc, arrays))
    r = _run(nc, [{f"in_{n}_dram": a for n, a in arrays.items()}], core_ids=[0]).results[0]
    y, state, k, v = (r[f"out_{n}_dram"] for n, _ in _OUTS)
    return (y[None, 0:P], y[None, P:TOK], state[None], k.reshape(1, DEPTH, P, KV_HEADS, HD), v.reshape(1, DEPTH, P, KV_HEADS, HD))
```

```python
from contextlib import ExitStack

import numpy as np
import concourse.bass as bass
from concourse import mybir

F32, I32, BF16 = mybir.dt.float32, mybir.dt.int32, mybir.dt.bfloat16
ALU, ACT, AXL = mybir.AluOpType, mybir.ActivationFunctionType, mybir.AxisListType

P = 128
D = 1024
KD = D // P
DEPTH = 2
T = 5
TOK = T * P
HALF = TOK // 2
CTX = 256
GRID_W = 64
GLA_H, DK, DV, RANK = 4, 64, 128, 16
PAIRS = GLA_H // 2
GLA_TAU = 16.0
HEADS, KV_HEADS, HD = 8, 2, 64
EPS = 1e-5
ALPHA = (2.0 * DEPTH) ** 0.25
NG, EG = 4, 4
NE = NG * EG
FF = D // 4
LOGITS = NG + NE
N_MIXER = 9
TILES = 26
BIG = 1e30

C_AQ, C_AK, C_AV, C_AG, C_LR, C_U, C_V, C_CQ, C_CK, C_MG = 0, 256, 512, 1024, 1536, 1568, 2080, 2592, 3104, 3360
V_COND, V_NEXT, V_ADA, V_NORM, V_GB, V_ROWS = 0, 16, 32, 80, 84, 88

UNITS = T * HEADS
MOD_FIRST, MOD_ALL = 8, 24
RING = 6
BLK = 2048


def rot_beside(p, t):
    c = 3 * p + t - 1
    return c if 1 <= t <= 3 else None


def heads_beside(i):
    return {3: (0, 1), 9: (2, 3)}.get(i, ())


def mod_beside(m):
    return (MOD_FIRST + m) % MOD_ALL


def build_tables():
    jobs, blocks = [], []

    def job(eng, *key):
        jobs.append((key, eng))

    def block(name, last):
        blocks.append((name, last))

    for k in range(KD):
        job("A" if k % 2 else "D", "hT", k)
    job("D", "vec")
    job("A", "lr")
    block(("win", C_LR, 32), ("lr",))
    for c in range(2):
        job("A", "aq", c)
    block(("win", C_AQ, 256), ("aq", 1))
    for c in range(2):
        job("D", "ak", c)
    block(("win", C_AK, 256), ("ak", 1))
    for c in range(4):
        job("D", "z", c)
        name, col = ("vtok", C_V) if c < 2 else ("av", C_AV)
        for t in range(T):
            job("A", name, c % 2, t)
        block(("win", col + 256 * (c % 2), 256), (name, c % 2, T - 1))
    for c in range(4):
        job("A", "ag", c)
        if c % 2:
            block(("win", C_AG + 128 * (c - 1), 256), ("ag", c))
    for c in range(4):
        job("A", "u", c)
        if c % 2:
            block(("win", C_U + 128 * (c - 1), 256), ("u", c))
    for c in range(4):
        job("D", "cq", c)
        if c % 2:
            block(("win", C_CQ + 128 * (c - 1), 256), ("cq", c))
    for t in range(T):
        job("D", "ckv", t)
    block(("win", C_CK, 256), ("ckv", T - 1))
    job("A", "wsT")
    job("A", "kcT")
    for g in range(KV_HEADS):
        job("D", "kT", g)
    for g in range(4):
        job("D", "mix", g)
    for c in range(5):
        if c < 4:
            job("A", "ktok", c)
        if c:
            job("D", "kv", c - 1)
    for p in range(PAIRS):
        for t in range(T + 1):
            if t < T:
                job("D", "gs", p, t)
                if rot_beside(p, t) is not None:
                    job("D", "rot", rot_beside(p, t))
            if t:
                job("A", "o", p, t - 1)
    for i in range(UNITS + 3):
        for h in heads_beside(i):
            job("A", "ms", h)
        if i < UNITS:
            job("A", "s", i)
        if 2 <= i < UNITS + 2:
            job("A", "pT", i - 2)
        if i >= 4 and i % 2 == 0:
            job("D", "pv", (i - 4) // 2)
    for half in range(2):
        for n in range(3):
            for q in range(4):
                if q % 2 == 0:
                    block(("mg", half, n, q // 2), ("gate", half, n, q + 1))
                    block(("wb", half, n, q // 2), ("proj", half, n, q + 1))
                job("A", "gate", half, n, q)
                job("D", "proj", half, n, q)
                b = mod_beside(12 * half + 4 * n + q)
                job("D", "mod", b)
                block(("ada", b), ("mod", b))
    for t in range(T + 2):
        for cb in range(4 if t < T else 0):
            job("D", "y", t, cb)
        if t >= 2:
            job("A", "h2T", t - 2)
        if t >= 3:
            job("A", "lgT", t - 3)
    for cb in range(4):
        block(("wout", cb), ("y", T - 1, cb))
    job("A", "lgT", T - 1)
    job("D", "logit")
    job("D", "rank")
    job("D", "xg", 0)
    assert len(blocks) % RING == 0
    moe_block = len(blocks)
    for j in range(TILES + 1):
        if j < TILES:
            job("D", "gu", j)
            job("D", "xg", j + 1)
        if j:
            job("A", "dn", j - 1)
        if j < TILES:
            job("A", "ht", j)
            block(("gate", j), ("gu", j))
            block(("up", j), ("gu", j))
            block(("down", j), ("dn", j))
    number = {}
    moved = {}
    count = {"A": 0, "D": 0}
    for n, (key, eng) in enumerate(jobs):
        count[eng] += 1
        number[key] = n
        moved[key] = (eng, count[eng])
    assert len(blocks) % RING == 0
    return jobs, number, moved, blocks, moe_block


JOBS, NUMBER, MOVED, BLOCKS, MOE_BLOCK = build_tables()
BLOCK_NO = {name: n for n, (name, _) in enumerate(BLOCKS)}
PER_TILE = 4

CONST, _at = {}, 0
for _name, _width in (("ident", P), ("pick", 3), ("ones", P), ("before", P), ("gla_mask", 2 * P), ("att_mask", 2 * P), ("swap", P),
                      ("cos", 4 * P), ("sin", 4 * P), ("run", TOK), ("eps", 1), ("over", 5), ("first", 4),
                      ("tile", TILES)):
    CONST[_name] = (_at, _width)
    _at += _width
CONST_W = _at


def const_tile():
    c = np.zeros((P, CONST_W), np.float32)
    r, q = np.arange(P)[:, None], np.arange(P)[None, :]

    def put(name, values):
        at, width = CONST[name]
        c[:, at:at + width] = values

    put("ident", r == q)
    put("ones", 1.0)
    put("before", r < q)
    put("gla_mask", np.concatenate([r <= q, r >= q], 1))
    put("att_mask", np.where(np.concatenate([q >= r, q <= r], 1), 0.0, -BIG))
    quarter = HD // 4
    swap = np.zeros((P, P), np.float32)
    for base in range(0, P, 2 * quarter):
        for i in range(quarter):
            swap[base + quarter + i, base + i] = -1.0
            swap[base + i, base + quarter + i] = 1.0
    put("swap", swap)
    freq = np.power(np.float32(10000.0), -np.arange(quarter, dtype=np.float32) / np.float32(quarter)).astype(np.float32)
    tok = np.arange(4 * P)
    row, col = (tok // GRID_W).astype(np.float32), (tok % GRID_W).astype(np.float32)
    ang = np.stack([(row if d % HD < HD // 2 else col) * freq[d % quarter] for d in range(P)]).astype(np.float32)
    put("cos", np.cos(ang))
    put("sin", np.sin(ang))
    put("run", np.broadcast_to((np.arange(TOK) % P != 0), (P, TOK)))
    put("eps", EPS)
    put("pick", np.array([[1.0, 0.0, 1.0]]))
    put("over", P * np.arange(5.0)[None, :])
    put("first", np.arange(4.0, 0.0, -1.0)[None, :])
    put("tile", np.arange(float(TILES))[None, :])
    return c


_INS = ["x_prompt", "x_sample", "state_gla", "cache_k", "cache_v", "c", "c_ctx", "ada_w", "ada_b", "w_in",
        "gla_gate_w", "gla_gate_b", "gla_norm_g", "gmlp_ln_g", "gmlp_ln_b", "gmlp_ws", "gmlp_bs", "attn_sink",
        "w_branch", "w_out", "ln1_g", "ln1_b", "ln2_g", "ln2_b", "router_group_w", "router_group_b",
        "router_expert_w", "router_expert_b", "expert_w_gate", "expert_w_up", "expert_w_down"]
_OUTS = [("y", (TOK, D)), ("new_state", (DEPTH, 2, GLA_H, DK, DV)), ("new_k", (DEPTH, P, P)), ("new_v", (DEPTH, P, P))]


def build_program(nc, A):
    with ExitStack() as ctx:
        def sb(name, width, dt=F32, parts=P):
            return ctx.enter_context(nc.sbuf_tensor(name, [parts, width], dt))

        per_layer = []

        def sem(name):
            per_layer.append(ctx.enter_context(nc.semaphore(name)))
            return per_layer[-1]

        const = sb("const", CONST_W)
        hT = sb("hT", KD * TOK)
        ring = sb("ring", RING * BLK)
        br = sb("br", 12 * TOK)
        mg = sb("mg", KD * TOK)
        xr = sb("xr", T * D)
        ar = sb("ar", 11904)
        vst = sb("vst", P)
        vec = sb("vec", V_ROWS)
        mod = sb("mod", 32)
        cs = sb("cs", 16)
        w2 = sb("w2", 512, parts=32)
        small = sb("small", 8 * P)
        wsT = small[:, 0:4 * P]
        bsb = small[:, 4 * P:8 * P]
        sink = sb("sink", 2 * HEADS)
        rw = sb("rw", KD * LOGITS)
        rb = sb("rb", LOGITS)
        st = sb("st", 64)
        er = sb("er", 4 * 15)
        sm = sb("sm", 16)
        zero = sb("zero", D // 2)

        def cst(name, parts=P):
            at, width = CONST[name]
            return const[0:parts, at:at + width]

        ident = cst("ident")
        eps = cst("eps")
        h3 = hT[:, :].rearrange("p (k t) -> p k t", k=KD)
        br3 = br[:, :].rearrange("p (k t) -> p k t", k=12)
        mg3 = mg[:, :].rearrange("p (k t) -> p k t", k=KD)
        x3 = xr[:, :].rearrange("p (t d) -> p t d", t=T)
        av = xr[:, 0:2560].rearrange("p (t c) -> p t c", t=T)
        vtok = xr[:, 2560:5120].rearrange("p (t c) -> p t c", t=T)
        oT = xr[:, 2560:5120].rearrange("p (h t) -> p h t", h=GLA_H)
        mod3 = mod[:, :].rearrange("p (f c) -> p f c", c=2)
        late_rows = [xr[0:2, D * i:D * (i + 1)] for i in range(3)] + [small[0:2, :]]
        lng = br[:, 5120:5632]
        lnb = br[:, 5632:6144]
        aqk = ar[:, 0:2560].rearrange("p (c t) -> p c t", c=4)
        t1 = ar[:, 0:2560].rearrange("p (c t v) -> p c t v", c=4, t=T)
        pbuf = [ar[:, 640 * i:640 * (i + 1)] for i in range(3)]
        pTbuf = [ar[:, 1920 + 640 * i:2560 + 640 * i] for i in range(4)]
        diag = [ar[:, 4480 + P * i:4480 + P * (i + 1)] for i in range(3)]
        bufA, bufM, bufB = (ar[:, 2560 + 640 * i:3200 + 640 * i] for i in range(3))
        gsb = [ar[:, 2560 + 512 * i:3072 + 512 * i] for i in range(2)]
        tmp5 = ar[:, 3584:4224]
        ktok = [ar[:, 4480 + 640 * i:5120 + 640 * i] for i in range(2)]
        kvt = ar[:, 5760:7040].rearrange("p (t c) -> p t c", t=T)
        kT = ar[:, 7040:8320].rearrange("p (g t) -> p g t", g=KV_HEADS)
        kcT = ar[:, 8320:8832].rearrange("p (g t) -> p g t", g=KV_HEADS)
        ckn = ar[:, 8832:9088].rearrange("p (a c) -> p a c", a=2)
        cvn = ar[:, 9088:9344].rearrange("p (a c) -> p a c", a=2)
        lr = ar[:, 9344:9984]
        sq = [ar[:, 9984 + 640 * i:10624 + 640 * i] for i in range(2)]
        wsn = ar[:, 9984:10496].rearrange("p (g s) -> p g s", g=4)
        spare = ar[:, 11264:11392]
        s0 = ar[:, 11392:11904].rearrange("p (c v) -> p c v", c=4)
        sig = sq
        gtmp = lr
        bcA = ar[:, 0:4096].rearrange("p (v d) -> p v d", v=4)
        acc = [ar[:, 8192 + 512 * i:8704 + 512 * i] for i in range(2)]
        bcB = ar[:, 4096:8192].rearrange("p (v d) -> p v d", v=4)
        ytmp = ar[:, 8192:8448]
        R = {}
        at = 8448
        for name, width in (("lg", T * LOGITS), ("ge", 20), ("G", 20), ("gx", 20), ("gm", 5), ("gs", 5), ("gp", 5),
                            ("es", 20), ("e2", 20), ("E1", 20), ("E2", 20), ("m1", 5), ("m2", 5), ("dq", 5),
                            ("w1", 5), ("w2", 5), ("big", 80), ("M1", 80), ("M2", 80), ("M", 80), ("rk", 96),
                            ("cmp", 80), ("nt", 16), ("end", 16), ("base", 16), ("pos", 10), ("ex", TILES + 1),
                            ("exc", TILES * NE), ("pairs", TILES // 2)):
            R[name] = ar[:, at:at + width]
            at += width
        counting = sb("counting", 2 * P, BF16)
        chosen = sb("chosen", T * NE, BF16)
        lgT = lr[0:LOGITS, :]
        posi = ctx.enter_context(nc.sbuf_tensor("posi", [P, 10], I32))
        exi = ctx.enter_context(nc.sbuf_tensor("exi", [P, TILES + 1], I32))
        assert at <= 11904, at
        h2 = br[:, 0:T * D].rearrange("p (t d) -> p t d", t=T)
        yg = [[(hT, br)[w][:, D * t:D * (t + 1)] for w in range(2)] for t in range(T)]
        ysum = [mg[:, D * (2 + i):D * (3 + i)] for i in range(2)]
        ys = [br[:, 5120 + D * i:5120 + D * (i + 1)] for i in range(2)]
        xgT = [mg[:, D * i:D * (i + 1)].rearrange("p (k s) -> p k s", k=KD) for i in range(2)]
        xg = [mg[:, 2048 + D * i:2048 + D * (i + 1)] for i in range(2)]
        silu, hid = mg[:, 4096:4352], mg[:, 4352:4608]
        hidT = [mg[:, 4608 + 256 * i:4864 + 256 * i].rearrange("p (f s) -> p f s", f=2) for i in range(2)]

        PS = ctx.enter_context(nc.psum_tensor("PS", [P, 4, 1024], F32))

        x_in = A["x"]
        y_out = A["y"]
        mod_rows = A["mod_rows"]
        rows = A["rows"]

        start_in, const_in, x_in_sem, x_copied, w2_zero, zeroed, zero_set = (
            ctx.enter_context(nc.semaphore(n)) for n in ("start_in", "const_in", "x_in", "x_copied", "w2_zero", "zeroed", "zero_set"))
        filled, act_moved, dve_moved = sem("filled"), sem("act_moved"), sem("dve_moved")
        landed = [sem(f"landed{i}") for i in range(RING)]
        vectors_in, gates_in, mixer_in, router_in = (sem(n) for n in ("vectors_in", "gates_in", "mixer_in", "router_in"))
        act_step, dve_step = sem("act_step"), sem("dve_step")
        acc_ready = sem("acc_ready")
        abs_done, softplus, decay_ready, exp_ready, qk_ready = (
            sem(n) for n in ("abs_done", "softplus", "decay_ready", "exp_ready", "qk_ready"))
        var_ready, std_ready, vn_ready = sem("var_ready"), sem("std_ready"), sem("vn_ready")
        rope_ready, states_in, square_ready, bra_ready = (
            sem(n) for n in ("rope_ready", "states_in", "square_ready", "bra_ready"))
        negmax, esink, p_ready = sem("negmax"), sem("esink"), sem("p_ready")
        merged, brb_ready, x_back, ln_rows = sem("merged"), sem("brb_ready"), sem("x_back"), sem("ln_rows")
        x1_done, h2_ready, masks_ready, route_ready, scattered = (
            sem(n) for n in ("x1_done", "h2_ready", "masks_ready", "route_ready", "scattered"))
        gexp_in, gexp = sem("gexp_in"), sem("gexp")
        silu_ready = sem("silu_ready")
        xg_in = [sem(f"xg_in{i}") for i in range(2)]
        y_stored = [sem(f"y_stored{i}") for i in range(2)]
        yg_in = [[sem(f"yg_in{t}{w}") for w in range(2)] for t in range(T)]
        experts_done = sem("experts_done")
        x2_last = sem("x2_last")
        x2_scaled, places_ready = sem("x2_scaled"), sem("places_ready")
        mod_stored, mod_rows_in = sem("mod_stored"), sem("mod_rows_in")
        first_scaled, rs_ready, x_norm = sem("first_scaled"), sem("rs_ready"), sem("x_norm")
        yg_used, x2_done, out_stored, kv_out = sem("yg_used"), sem("x2_done"), sem("out_stored"), sem("kv_out")

        start_moved, start_filled, start_acc, start_step, cond_ready = (
            ctx.enter_context(nc.semaphore(n)) for n in ("start_moved", "start_filled", "start_acc", "start_step", "cond_ready"))
        start_landed = [ctx.enter_context(nc.semaphore(f"start_landed{i}")) for i in range(RING)]

        MOVED_SEM = {"A": act_moved, "D": dve_moved}

        def slot(key):
            return PS[:, NUMBER[key] % 4, :]

        def wait_filled(eng, key, more=0):
            eng.wait_ge(filled, NUMBER[key] + 1 + more)
            return slot(key)

        def wait_moved(eng, key, more=0):
            who, n = MOVED[key]
            eng.wait_ge(MOVED_SEM[who], n + more)

        def wait_slot(pe, key):
            n = NUMBER[key]
            if n >= 4:
                wait_moved(pe, JOBS[n - 4][0])
            return slot(key)

        def ring_slot(name):
            s = BLOCK_NO[name] % RING
            return ring[:, s * BLK:(s + 1) * BLK]

        def wait_block(pe, name, more=0):
            n = BLOCK_NO[name]
            pe.wait_ge(landed[n % RING], 16 * (n // RING + 1) + more)
            return ring_slot(name)

        def tok2(ap):
            return ap.rearrange("p (h t) -> p h t", h=2)

        def ps2(ps):
            return ps.rearrange("p (h t) -> p h t", h=2)[:, :, 0:HALF]

        def keys_of(n):
            return P if n == 0 else CTX + (2 if n in (1, 4) else 3) * P

        class Steps:

            def __init__(self, eng, semaphore):
                self.eng, self.semaphore, self.n = eng, semaphore, 0

            def __call__(self, instruction):
                self.n += 1
                instruction.then_inc(self.semaphore, 1)
                self.eng.wait_ge(self.semaphore, self.n)

        def row_sums(step, block, sums):
            w = block.rearrange("p (k c) -> p k c", k=KD)
            for k in range(KD):
                for c in range(2):
                    out, scalar = sums[:, 256 * c:256 * (c + 1)], cs[:, KD * c + k:KD * c + k + 1]
                    if k == 0:
                        last = nc.vector.tensor_scalar(out, w[:, k, :], scalar, None, ALU.mult)
                    else:
                        last = nc.vector.scalar_tensor_tensor(out=out, in0=w[:, k, :], scalar=scalar, in1=out, op0=ALU.mult, op1=ALU.add)
                if k < KD - 1:
                    step(last)
            return last

        def column_sums(ps, sums):
            for ct in range(2):
                for c in range(2):
                    last = nc.tensor.matmul(ps[:, 2 * ct:2 * ct + 2], sums[:, 256 * c + P * ct:256 * c + P * (ct + 1)],
                                            cst("pick")[:, c:c + 2], start=c == 0, stop=c == 1, skip_group_check=True)
            return last

        def first_mod(b, ps):
            return nc.vector.tensor_tensor(mod3[:, 2 * b:2 * b + 2, :], ps[:, 0:4].rearrange("p (f c) -> p f c", c=2),
                                           vec[:, V_NEXT + 2 * b:V_NEXT + 2 * b + 2].unsqueeze(2).to_broadcast([P, 2, 2]), ALU.add)

        with nc.Block() as block:
            @block.scalar
            def _(act):
                at, width = 0, P + 3
                act.dma_start(const[:, at:width], A["const"][:, at:width]).then_inc(start_in, 16)
                act.dma_start(vst[V_COND:V_COND + KD, :], A["c"][0, :].rearrange("(r c) -> r c", c=P)).then_inc(start_in, 16)
                act.dma_start(vst[V_COND + KD:V_NEXT, :], A["c_ctx"][:].rearrange("(r c) -> r c", c=P)).then_inc(start_in, 16)
                act.dma_start(vst[V_NEXT:V_ADA, :], A["ada_b"][0, 0:2 * D].rearrange("(r c) -> r c", c=P)).then_inc(start_in, 16)
                act.wait_ge(start_moved, 1)
                nc.scalar.activation(cs[:, :], vec[:, V_COND:V_NEXT], ACT.Silu).then_inc(cond_ready, 1)

            @block.sync
            def _(sp):
                for b in range(MOD_FIRST):
                    if b >= RING:
                        sp.wait_ge(start_filled, b - RING + 2)
                    if b == 1:
                        sp.wait_ge(start_in, 16 * 4)
                    sp.dma_start(ring[:, b % RING * BLK:(b % RING + 1) * BLK].rearrange("p (k c) -> p k c", k=KD),
                                 A["ada_w"][0, :, 256 * b:256 * (b + 1)].rearrange("(k p) c -> p k c", p=P)).then_inc(start_landed[b % RING], 16)

            @block.gpsimd
            def _(pool):
                pool.memset(w2[:, :], 0.0).then_inc(w2_zero, 1)
                pool.memset(zero[:, :], 0.0).then_inc(zero_set, 1)
                pool.wait_ge(start_landed[3], 16)
                pool.dma_start(x3, x_in.rearrange("(t p) d -> p t d", p=P)).then_inc(x_in_sem, 16)
                pool.dma_start(const[:, P + 3:CONST_W], A["const"][:, P + 3:CONST_W]).then_inc(const_in, 16)

            @block.tensor
            def _(pe):
                pe.wait_ge(start_in, 16 * 4)
                nc.tensor.transpose(PS[:, 0, 0:V_ADA], vst[0:V_ADA, :], ident[0:V_ADA, 0:V_ADA])\
                    .then_inc(start_filled, 1)
                pe.wait_ge(cond_ready, 1)
                for b in range(MOD_FIRST):
                    ps = PS[:, (b + 1) % 4, :]
                    if b >= 3:
                        pe.wait_ge(start_moved, b - 2)
                    if b % 2:
                        pe.wait_ge(start_acc, b // 2 + 1)
                        column_sums(ps, acc[b // 2 % 2]).then_inc(start_filled, 1)
                    else:
                        pe.wait_ge(start_landed[b % RING], 16 * (b // RING + 1))
                        w = ring[:, b % RING * BLK:(b % RING + 1) * BLK].rearrange("p (k c) -> p k c", k=KD)
                        for ct in range(2):
                            for k in range(KD):
                                last = nc.tensor.matmul(ps[:, 2 * ct:2 * ct + 2], w[:, k, P * ct:P * (ct + 1)],
                                                        cs[:, :].rearrange("p (c k) -> p k c", c=2)[:, k, :],
                                                        start=k == 0, stop=k == KD - 1, skip_group_check=True)
                        last.then_inc(start_filled, 1)

            @block.vector
            def _(dve):
                def bias_added(b):
                    dve.wait_ge(start_filled, b + 2)
                    first_mod(b, PS[:, (b + 1) % 4, :]).then_inc(start_moved, 1)

                dve.wait_ge(start_filled, 1)
                nc.vector.tensor_copy(vec[:, 0:V_ADA], PS[:, 0, 0:V_ADA]).then_inc(start_moved, 1)
                dve.wait_ge(cond_ready, 1)
                step = Steps(dve, start_step)
                for b in range(1, MOD_FIRST, 2):
                    dve.wait_ge(start_landed[b % RING], 16 * (b // RING + 1))
                    row_sums(step, ring[:, b % RING * BLK:(b % RING + 1) * BLK], acc[b // 2 % 2]).then_inc(start_acc, 1)
                    if b > 1:
                        bias_added(b - 2)
                    bias_added(b - 1)
                bias_added(MOD_FIRST - 1)
                dve.wait_ge(start_moved, MOD_FIRST + 1)
                nc.vector.tensor_scalar(mod[:, 16:32], mod[:, 16:32], 1.0, None, ALU.add).then_inc(start_moved, 1)

        with nc.Fori(0, DEPTH) as l:
            with nc.Block() as block:

                next_layer = (l + 1) % DEPTH

                def block_source(l, name):
                    kind = name[0]
                    if kind == "ada":
                        return A["ada_w"][next_layer if name[1] < MOD_FIRST else l, :, 256 * name[1]:256 * (name[1] + 1)].rearrange("(k p) c -> p k c", p=P)
                    if kind == "win":
                        return A["w_in"][l, :, name[1]:name[1] + name[2]].rearrange("(k p) c -> p k c", p=P)
                    if kind == "wb":
                        col = 512 * name[1] + 256 * name[3]
                        return A["w_branch"][l, name[2], :, col:col + 256].rearrange("(k p) c -> p k c", p=P)
                    if kind == "mg":
                        col = C_MG + name[2] * D + 512 * name[1] + 256 * name[3]
                        return A["w_in"][l, :, col:col + 256].rearrange("(k p) c -> p k c", p=P)
                    return A["w_out"][l, :, 256 * name[1]:256 * (name[1] + 1)].rearrange("(k p) c -> p k c", p=P)

                @block.sync
                def _(sp):
                    for n, (name, _) in enumerate(BLOCKS[:MOE_BLOCK]):
                        if n >= RING:
                            wait_filled(sp, BLOCKS[n - RING][1])
                        src = block_source(l, name)
                        k, c = src.shape[1], src.shape[2]
                        sp.dma_start(ring_slot(name)[:, 0:k * c].rearrange("p (k c) -> p k c", k=k), src)\
                            .then_inc(landed[n % RING], 16)
                    sp.wait_ge(route_ready, 1)

                    def strip_load(e, s):
                        strip = ring[:, 3 * s * BLK:(3 * s + 2) * BLK].rearrange("p (k c) -> p k c", k=KD)
                        sp.dma_start(strip[:, :, 0:FF], A["expert_w_gate"][l, e, :, :].rearrange("(k p) f -> p k f", p=P))\
                            .then_inc(landed[3 * s], 16)
                        sp.dma_start(strip[:, :, FF:2 * FF], A["expert_w_up"][l, e, :, :].rearrange("(k p) f -> p k f", p=P))\
                            .then_inc(landed[3 * s + 1], 16)

                    def down_load(e, s):
                        sp.dma_start(ring[:, (3 * s + 2) * BLK:(3 * s + 3) * BLK].rearrange("p (k c) -> p k c", k=2),
                                     A["expert_w_down"][l, e, :, :].rearrange("(k p) d -> p k d", p=P))\
                            .then_inc(landed[3 * s + 2], 16)

                    def rows_load(tile, s):
                        sp.dma_start(xg[s], rows[bass.ds(P * tile, P), :]).then_inc(xg_in[s], 16)

                    for s in range(2):
                        e = sp.value_load(exi[0:1, s:s + 1], min_val=0, max_val=NE - 1)
                        strip_load(e, s)
                        if s == 0:
                            sp.wait_ge(scattered, 16 * 2 * T)
                        rows_load(s, s)
                        down_load(e, s)
                    wait_filled(sp, ("xg", 0))
                    rows_load(2, 0)
                    pairs = sp.value_load(exi[0:1, TILES:TILES + 1], min_val=1, max_val=TILES // 2)
                    with sp.Fori(1, TILES // 2) as i:
                        with sp.If(i < pairs):
                            more = 2 * PER_TILE * (i - 1)
                            for s in range(2):
                                e = sp.value_load(exi[0:1, bass.ds(2 * i + s, 1)], min_val=0, max_val=NE - 1)
                                wait_filled(sp, ("gu", s), more)
                                strip_load(e, s)
                                wait_filled(sp, ("xg", s + 1), more)
                                rows_load(2 * i + s + 1, (s + 1) % 2)
                                wait_filled(sp, ("dn", s), more)
                                down_load(e, s)
                    for t in range(T):
                        sp.wait_ge(x2_done if t < T - 1 else x2_last, t + 1 if t < T - 1 else 1)
                        sp.dma_start(y_out[P * t:P * (t + 1), :], x3[:, t, :]).then_inc(out_stored, 16)
                    sp.wait_ge(out_stored, 16 * T)

                def vector_loads(l):
                    yield vst[V_ADA:V_NORM, :], A["ada_b"][l, :].rearrange("(r c) -> r c", c=P)
                    yield vst[V_NORM:V_GB, :], A["gla_norm_g"][l, :].rearrange("(r c) -> r c", c=P)
                    yield vst[V_GB:V_ROWS, :], A["gla_gate_b"][l, :, :].rearrange("d (r c) -> (d r) c", c=P)
                    yield vst[V_NEXT:V_ADA, :], A["ada_b"][next_layer, 0:2 * D].rearrange("(r c) -> r c", c=P)

                def mixer_loads(l):
                    yield wsn, A["gmlp_ws"][l, :, :, :].rearrange("g t s -> t g s")
                    yield lng, A["gmlp_ln_g"][l, :].partition_broadcast(P)
                    yield lnb, A["gmlp_ln_b"][l, :].partition_broadcast(P)
                    yield bsb[:, :].rearrange("p (g t) -> p g t", g=4), A["gmlp_bs"][l, :, :].partition_broadcast(P)
                    yield ckn, A["cache_k"][0, l, :, :, :].rearrange("(a p) g d -> p a (g d)", p=P)
                    yield cvn, A["cache_v"][0, l, :, :, :].rearrange("(a p) g d -> p a (g d)", p=P)
                    for d in range(2):
                        yield s0[:, 2 * d:2 * d + 2, :], A["state_gla"][0, l, d, :, :, :].rearrange("(q h) k v -> (h k) q v", h=2)
                    yield sink[:, 0:HEADS], A["attn_sink"][l, :].partition_broadcast(P)

                def router_loads(l):
                    rw3 = rw[:, :].rearrange("p (k c) -> p k c", k=KD)
                    yield rw3[:, :, 0:NG], A["router_group_w"][l, :, :].rearrange("(k p) c -> p k c", p=P)
                    yield rw3[:, :, NG:LOGITS], A["router_expert_w"][l, :, :].rearrange("(k p) c -> p k c", p=P)
                    yield rb[:, 0:NG], A["router_group_b"][l, :].partition_broadcast(P)
                    yield rb[:, NG:LOGITS], A["router_expert_b"][l, :].partition_broadcast(P)

                @block.gpsimd
                def _(pool):
                    pool.wait_ge(w2_zero, 1)
                    for d in range(2):
                        pool.dma_start(w2[RANK * d:RANK * (d + 1), 256 * d:256 * (d + 1)], A["gla_gate_w"][l, d, :, :])\
                            .then_inc(gates_in, 16)
                    for dst, src in mixer_loads(l):
                        pool.dma_start(dst, src).then_inc(mixer_in, 16)
                    for dst, src in router_loads(l):
                        pool.dma_start(dst, src).then_inc(router_in, 16)
                    with pool.If(l < 1):
                        pool.dma_start(y_out, x_in).then_inc(x_copied, 16)
                        wait_filled(pool, ("kT", 0))
                        pool.wait_ge(zero_set, 1)
                        pool.dma_start(rows.rearrange("(p n) (k c) -> p (n k) c", p=P, k=2),
                                       zero[:, :].unsqueeze(1).to_broadcast([P, (TILES + 1) * 2, D // 2])).then_inc(zeroed, 16)
                    wait_moved(pool, ("ckv", 0))
                    pool.dma_start(A["new_k"][l, :, :], kvt[:, 0, 0:P]).then_inc(kv_out, 16)
                    pool.dma_start(A["new_v"][l, :, :], kvt[:, 0, P:2 * P]).then_inc(kv_out, 16)
                    for c in range(4):
                        wait_moved(pool, ("kv", c))
                        pool.dma_start(A["new_state"][l, c // 2, 2 * (c % 2):2 * (c % 2) + 2, :, :].rearrange("h k v -> (h k) v"),
                                       t1[:, c, 0, :]).then_inc(kv_out, 16)
                    pool.wait_ge(kv_out, 16 * 6)
                    wait_moved(pool, ("mod", MOD_ALL - 1))
                    for vector in range(4):
                        pool.dma_start(mod_rows[vector, :, :], late_rows[vector]).then_inc(mod_stored, 16)
                    pool.wait_ge(mod_stored, 16 * 4)
                    wait_filled(pool, ("pv", UNITS // 2 - 1))
                    for v, (vector, cond) in enumerate(((0, 1), (0, 0), (2, 1), (2, 0), (1, 1), (1, 0))):
                        pool.dma_start(bcA[:, v, :] if v < 2 else bcB[:, v - 2, :], mod_rows[vector, cond, :].partition_broadcast(P))\
                            .then_inc(mod_rows_in, 16)
                    pool.wait_ge(x_copied, 16)
                    pool.wait_ge(merged, KD)
                    pool.dma_start(x3, y_out.rearrange("(t p) d -> p t d", p=P)).then_inc(x_back, 16)
                    pool.dma_start(bcA[:, 2, :], A["ln1_g"][l, :].partition_broadcast(P)).then_inc(ln_rows, 16)
                    pool.dma_start(bcA[:, 3, :], A["ln1_b"][l, :].partition_broadcast(P)).then_inc(ln_rows, 16)
                    pool.wait_ge(x1_done, T)
                    pool.wait_ge(ln_rows, 16 * 2)
                    pool.dma_start(bcA[:, 2, :], A["ln2_g"][l, :].partition_broadcast(P)).then_inc(ln_rows, 16)
                    pool.dma_start(bcA[:, 3, :], A["ln2_b"][l, :].partition_broadcast(P)).then_inc(ln_rows, 16)
                    pool.wait_ge(zeroed, 16)
                    for cond in range(2):
                        pool.dma_start(bcA[:, 1 - cond, :], mod_rows[3, cond, :].partition_broadcast(P)).then_inc(mod_rows_in, 16)
                    pool.wait_ge(places_ready, 1)
                    for t in range(T):
                        for w in range(2):
                            pool.indirect_dma_start(rows, bass.IndirectOffsetOnAxis(ap=posi[:, 2 * t + w:2 * t + w + 1], axis=0),
                                                    h2[:, t, :], None).then_inc(scattered, 16)
                    pool.wait_ge(scattered, 16 * 2 * T)
                    pool.wait_ge(experts_done, 1)
                    pool.wait_ge(ln_rows, 16 * 4)
                    for t in range(T):
                        for w in range(2):
                            pool.indirect_dma_start(yg[t][w], None, rows,
                                                    bass.IndirectOffsetOnAxis(ap=posi[:, 2 * t + w:2 * t + w + 1], axis=0))\
                                .then_inc(yg_in[t][w], 16)
                    for t in range(T - 1):
                        x = x3[:, t, :]
                        pool.wait_ge(x_norm, t + 1)
                        nc.gpsimd.tensor_tensor(x, x, bcA[:, 2, :], ALU.mult).then_inc(x2_scaled, 1)
                        pool.wait_ge(x2_scaled, t + 1)
                        nc.gpsimd.tensor_tensor(x, x, bcA[:, 3, :], ALU.add).then_inc(x2_done, 1)
                    pool.wait_ge(mod_rows_in, 16 * 8)
                    for t in range(T):
                        for w in range(2):
                            pool.wait_ge(yg_in[t][w], 16)

                @block.tensor
                def _(pe):
                    def mm(out, lhsT, rhs, start, stop):
                        return nc.tensor.matmul(out, lhsT, rhs, start=start, stop=stop, skip_group_check=True)

                    def turn(out, in_):
                        n = in_.shape[0]
                        return nc.tensor.transpose(out, in_, ident[0:n, 0:n])

                    def feature_major(key, w, rhs3, cols, k0=0):
                        ps = wait_slot(pe, key)
                        k_n = w.shape[1]
                        m = cols.stop - cols.start
                        for h in range(2):
                            for k in range(k_n):
                                last = mm(ps[0:m, 512 * h:512 * h + HALF], w[:, k, cols], rhs3[:, k0 + k, HALF * h:HALF * (h + 1)],
                                          k == 0, k == k_n - 1)
                        last.then_inc(filled, 1)

                    def token_major(key, w, lhs3, t):
                        ps = wait_slot(pe, key)
                        n = w.shape[2]
                        for k in range(KD):
                            last = mm(ps[:, 0:n], lhs3[:, k, P * t:P * (t + 1)], w[:, k, :], k == 0, k == KD - 1)
                        last.then_inc(filled, 1)

                    def view(ap, k):
                        return ap.rearrange("p (k c) -> p k c", k=k)

                    pe.wait_ge(x_in_sem, 16)
                    pe.wait_ge(const_in, 16)
                    for k in range(KD):
                        ps = wait_slot(pe, ("hT", k))
                        for t in range(T):
                            last = turn(ps[:, P * t:P * (t + 1)], x3[:, t, P * k:P * (k + 1)])
                        last.then_inc(filled, 1)
                    pe.wait_ge(vectors_in, 16 * 4)
                    ps = wait_slot(pe, ("vec",))
                    turn(ps[:, 0:V_ROWS], vst[0:V_ROWS, :]).then_inc(filled, 1)
                    for k in range(KD):
                        wait_moved(pe, ("hT", k))
                    w = view(wait_block(pe, ("win", C_LR, 32))[:, 0:32 * KD], KD)
                    feature_major(("lr",), w, h3, slice(0, 32))
                    for name, col in (("aq", C_AQ), ("ak", C_AK)):
                        w = view(wait_block(pe, ("win", col, 256)), KD)
                        for c in range(2):
                            feature_major((name, c), w, h3, slice(P * c, P * (c + 1)))
                    wait_moved(pe, ("lr",))
                    pe.wait_ge(gates_in, 16 * 2)
                    for c in range(4):
                        ps = wait_slot(pe, ("z", c))
                        for h in range(2):
                            last = mm(ps[:, 512 * h:512 * h + HALF], w2[0:32, P * c:P * (c + 1)], lr[0:32, HALF * h:HALF * (h + 1)],
                                      True, True)
                        last.then_inc(filled, 1)
                        name, col = ("vtok", C_V) if c < 2 else ("av", C_AV)
                        w = view(wait_block(pe, ("win", col + 256 * (c % 2), 256)), KD)
                        for t in range(T):
                            token_major((name, c % 2, t), w, h3, t)
                    for name, col in (("ag", C_AG), ("u", C_U), ("cq", C_CQ)):
                        for c in range(4):
                            if c % 2 == 0:
                                w = view(wait_block(pe, ("win", col + P * c, 256)), KD)
                            feature_major((name, c), w, h3, slice(P * (c % 2), P * (c % 2) + P))
                    w = view(wait_block(pe, ("win", C_CK, 256)), KD)
                    for t in range(T):
                        token_major(("ckv", t), w, h3, t)
                    pe.wait_ge(mixer_in, 16 * N_MIXER)
                    ps = wait_slot(pe, ("wsT",))
                    for g in range(4):
                        last = turn(ps[:, P * g:P * (g + 1)], wsn[:, g, :])
                    last.then_inc(filled, 1)
                    ps = wait_slot(pe, ("kcT",))
                    for g in range(KV_HEADS):
                        for a in range(2):
                            for half in range(2):
                                last = mm(ps[64 * half:64 * half + 64, 256 * g + P * a:256 * g + P * (a + 1)],
                                          ckn[:, a, HD * g:HD * (g + 1)], ident, True, True)
                    last.then_inc(filled, 1)
                    for g in range(KV_HEADS):
                        wait_moved(pe, ("ckv", T - 1))
                        ps = wait_slot(pe, ("kT", g))
                        for t in range(T):
                            for half in range(2):
                                last = mm(ps[64 * half:64 * half + 64, P * t:P * (t + 1)], kvt[:, t, HD * g:HD * (g + 1)],
                                          ident, True, True)
                        last.then_inc(filled, 1)
                    def swapped(c):
                        wait_moved(pe, ("cq", c) if c < 4 else ("kT", c - 4))
                        ps = wait_slot(pe, ("rot", c))
                        src = br3[:, 8 + c, P:TOK] if c < 4 else kT[:, c - 4, P:TOK]
                        mm(ps[:, 0:4 * P], cst("swap"), src, True, True).then_inc(filled, 1)

                    pe.wait_ge(vn_ready, 1)
                    wait_moved(pe, ("wsT",))
                    for g in range(4):
                        ps = wait_slot(pe, ("mix", g))
                        for t in range(T):
                            last = mm(ps[:, P * t:P * (t + 1)], vtok[:, t, P * g:P * (g + 1)], wsT[:, P * g:P * (g + 1)], True, True)
                        last.then_inc(filled, 1)
                    pe.wait_ge(qk_ready, 4)
                    for c in range(5):
                        if c < 4:
                            ps = wait_slot(pe, ("ktok", c))
                            for t in range(T):
                                last = turn(ps[:, P * t:P * (t + 1)], mg3[:, 4 + c, P * t:P * (t + 1)])
                            last.then_inc(filled, 1)
                        if c:
                            wait_moved(pe, ("ktok", c - 1))
                            ps = wait_slot(pe, ("kv", c - 1))
                            for t in range(T):
                                for j in range(2):
                                    head = 2 * ((c - 1) % 2) + j
                                    last = mm(ps[64 * j:64 * j + 64, P * t:P * (t + 1)],
                                              ktok[(c - 1) % 2][:, P * t + 64 * j:P * t + 64 * j + 64],
                                              av[:, t, DV * head:DV * (head + 1)], True, True)
                            last.then_inc(filled, 1)
                    for p in range(PAIRS):
                        for t in range(T + 1):
                            if t < T:
                                ps = wait_slot(pe, ("gs", p, t))
                                for j in range(2):
                                    for d in range(2):
                                        rows = slice(64 * j, 64 * j + 64)
                                        last = mm(ps[:, 512 * j + P * d:512 * j + P * (d + 1)],
                                                  mg3[rows, 4 + 2 * d + p, P * t:P * (t + 1)],
                                                  mg3[rows, 2 * d + p, P * t:P * (t + 1)], True, True)
                                last.then_inc(filled, 1)
                                if rot_beside(p, t) is not None:
                                    swapped(rot_beside(p, t))
                            if t == 0 and p == 0:
                                pe.wait_ge(states_in, 4)
                            if t:
                                u = t - 1
                                wait_moved(pe, ("gs", p, u))
                                ps = wait_slot(pe, ("o", p, u))
                                for j in range(2):
                                    head = 2 * p + j
                                    out = ps[:, 512 * j:512 * j + P]
                                    for d in range(2):
                                        last = mm(out, av[:, u, DV * head:DV * (head + 1)],
                                                  gsb[u % 2][:, P * (2 * j + d):P * (2 * j + d + 1)], d == 0, d == 1 and u == 0)
                                    for d in range(2 if u else 0):
                                        rows = slice(64 * j, 64 * j + 64)
                                        last = mm(out, t1[rows, 2 * d + p, u, :], mg3[rows, 2 * d + p, P * u:P * (u + 1)],
                                                  False, d == 1)
                                last.then_inc(filled, 1)
                    def head_squares(h):
                        pe.wait_ge(square_ready, h + 1)
                        ps = wait_slot(pe, ("ms", h))
                        for half in range(2):
                            last = mm(ps[:, 512 * half:512 * half + HALF], cst("ones"), sq[h % 2][:, HALF * half:HALF * (half + 1)],
                                      True, True)
                        last.then_inc(filled, 1)

                    pe.wait_ge(rope_ready, 6)
                    wait_moved(pe, ("kcT",))

                    def local_tiles(n):
                        return [0] if n == 0 else list(range(max(1, n - 1), min(4, n + 1) + 1))

                    for i in range(UNITS + 3):
                        for head in heads_beside(i):
                            head_squares(head)
                        if i < UNITS:
                            n, h = divmod(i, HEADS)
                            g, rows = h // 4, slice(64 * (h % 2), 64 * (h % 2) + 64)
                            ps = wait_slot(pe, ("s", i))
                            q = br3[rows, 8 + h // 2, P * n:P * (n + 1)]
                            if n == 0:
                                last = mm(ps[:, 0:P], q, kT[rows, g, 0:P], True, True)
                            else:
                                mm(ps[:, 0:CTX], q, kcT[rows, g, :], True, True)
                                col = CTX
                                for m in local_tiles(n):
                                    last = mm(ps[:, col:col + P], q, kT[rows, g, P * m:P * (m + 1)], True, m == n)
                                    if m != n:
                                        which = 0 if m < n else 1
                                        last = mm(ps[:, col:col + P], ident, cst("att_mask")[:, P * which:P * (which + 1)], False, True)
                                    col += P
                            last.then_inc(filled, 1)
                        if 2 <= i < UNITS + 2:
                            u = i - 2
                            n = u // HEADS
                            tiles = (0 if n == 0 else 2) + len(local_tiles(n))
                            pe.wait_ge(p_ready, u + 1)
                            ps = wait_slot(pe, ("pT", u))
                            for m in range(tiles):
                                last = mm(ps[:, P * m:P * (m + 1)], pbuf[u % 3][:, P * m:P * (m + 1)], diag[u % 3], True, True)
                            last.then_inc(filled, 1)
                        if i >= 4 and i % 2 == 0:
                            m = (i - 4) // 2
                            n, pair = divmod(m, HEADS // 2)
                            wait_moved(pe, ("pT", 2 * m + 1))
                            ps = wait_slot(pe, ("pv", m))
                            for j in range(2):
                                g = (2 * pair + j) // 4
                                values = [] if n == 0 else [cvn[:, a, HD * g:HD * (g + 1)] for a in range(2)]
                                values += [kvt[:, a, P + HD * g:P + HD * (g + 1)] for a in local_tiles(n)]
                                for a, v in enumerate(values):
                                    last = mm(ps[64 * j:64 * j + 64, 0:P], v, pTbuf[(2 * m + j) % 4][:, P * a:P * (a + 1)],
                                              a == 0, a == len(values) - 1)
                            last.then_inc(filled, 1)
                    def modulation(m, b):
                        ps = wait_slot(pe, ("mod", b))
                        pe.wait_ge(acc_ready, m + 1)
                        if b < MOD_FIRST:
                            last = column_sums(ps, acc[b % 2])
                        else:
                            for c in range(2):
                                mm(ps[0:2, 0:256], cst("pick")[:, c:c + 2], acc[b % 2][:, 256 * c:256 * (c + 1)], c == 0, False)
                            for ct in range(2):
                                r = V_ADA + 2 * b + ct
                                last = mm(ps[0:2, P * ct:P * (ct + 1)], ident[0:V_NORM, r:r + 1].to_broadcast([V_NORM, 2]), vst[0:V_NORM, :], False, ct == 1)
                        last.then_inc(filled, 1)

                    pe.wait_ge(bra_ready, GLA_H)
                    pe.wait_ge(brb_ready, 4)
                    wait_moved(pe, ("pv", UNITS // 2 - 1))
                    for half in range(2):
                        for n in range(3):
                            for q in range(4):
                                if q % 2 == 0:
                                    w = view(wait_block(pe, ("mg", half, n, q // 2)), KD)
                                    wb = view(wait_block(pe, ("wb", half, n, q // 2))[:, 0:4 * 256], 4)
                                feature_major(("gate", half, n, q), w, h3, slice(P * (q % 2), P * (q % 2) + P))
                                feature_major(("proj", half, n, q), wb, br3, slice(P * (q % 2), P * (q % 2) + P), 4 * n)
                                m = 12 * half + 4 * n + q
                                modulation(m, mod_beside(m))

                    pe.wait_ge(merged, KD)
                    def router_product(t):
                        wait_moved(pe, ("h2T", t))
                        ps = wait_slot(pe, ("lgT", t))
                        for k in range(KD):
                            last = mm(ps[0:LOGITS, 0:P], rw[:, LOGITS * k:LOGITS * (k + 1)], h3[:, k, P * t:P * (t + 1)],
                                      k == 0, k == KD - 1)
                        last.then_inc(filled, 1)

                    pe.wait_ge(router_in, 16 * 4)
                    w = [view(wait_block(pe, ("wout", cb)), KD) for cb in range(4)]
                    for t in range(T + 2):
                        for cb in range(4 if t < T else 0):
                            ps = wait_slot(pe, ("y", t, cb))
                            for k in range(KD):
                                last = mm(ps[:, 0:256], mg3[:, k, P * t:P * (t + 1)], w[cb][:, k, :], k == 0, k == KD - 1)
                            last.then_inc(filled, 1)
                        if t >= 2:
                            pe.wait_ge(h2_ready, t - 1)
                            ps = wait_slot(pe, ("h2T", t - 2))
                            for k in range(KD):
                                last = turn(ps[:, P * k:P * (k + 1)], h2[:, t - 2, P * k:P * (k + 1)])
                            last.then_inc(filled, 1)
                        if t >= 3:
                            router_product(t - 3)
                    router_product(T - 1)
                    wait_moved(pe, ("lgT", T - 1))
                    ps = wait_slot(pe, ("logit",))
                    for t in range(T):
                        last = turn(ps[:, 32 * t:32 * t + LOGITS], lgT[:, P * t:P * (t + 1)])
                    last.then_inc(filled, 1)
                    pe.wait_ge(masks_ready, 1)
                    ps = wait_slot(pe, ("rank",))
                    for t in range(T + 1):
                        for u in range(min(t + 1, T)):
                            last = mm(ps[:, NE * t:NE * (t + 1)], counting[:, P:2 * P] if u == t else counting[:, 0:P],
                                      chosen[:, NE * u:NE * (u + 1)], u == 0, u == min(t, T - 1))
                    last.then_inc(filled, 1)
                    def gate_up(j, n):
                        wait_moved(pe, ("xg", j), 4 * n)
                        wait_block(pe, ("gate", j), 16 * n)
                        wait_block(pe, ("up", j), 16 * n)
                        strip = view(ring[:, 3 * (j % 2) * BLK:(3 * (j % 2) + 2) * BLK], KD)
                        ps = slot(("gu", j))
                        for k in range(KD):
                            last = mm(ps[:, 0:2 * FF], xgT[j % 2][:, k, :], strip[:, k, :], k == 0, k == KD - 1)
                        last.then_inc(filled, 1)

                    def down(j, n):
                        wait_moved(pe, ("ht", j), 4 * n)
                        w = view(wait_block(pe, ("down", j), 16 * n), 2)
                        ps = slot(("dn", j))
                        for half in range(2):
                            for f in range(2):
                                last = mm(ps[:, 512 * half:512 * (half + 1)], hidT[j % 2][:, f, :], w[:, f, 512 * half:512 * (half + 1)],
                                          f == 0, f == 1)
                        last.then_inc(filled, 1)

                    def rows_turned(j, n):
                        pe.wait_ge(xg_in[j % 2], 16 * (j // 2 + 1) + 16 * n)
                        ps = slot(("xg", j))
                        for k in range(KD):
                            last = turn(ps[:, P * k:P * (k + 1)], xg[j % 2][:, P * k:P * (k + 1)])
                        last.then_inc(filled, 1)

                    def hidden_turned(j, n):
                        wait_moved(pe, ("gu", j), 4 * n)
                        ps = slot(("ht", j))
                        for f in range(2):
                            last = turn(ps[:, P * f:P * (f + 1)], hid[:, P * f:P * (f + 1)])
                        last.then_inc(filled, 1)

                    wait_slot(pe, ("xg", 0))
                    rows_turned(0, 0)
                    for j in range(2):
                        wait_slot(pe, ("gu", j))
                        gate_up(j, 0)
                        wait_slot(pe, ("xg", j + 1))
                        rows_turned(j + 1, 0)
                        if j:
                            wait_slot(pe, ("dn", 0))
                            down(0, 0)
                        wait_slot(pe, ("ht", j))
                        hidden_turned(j, 0)
                    pairs = pe.value_load(exi[0:1, TILES:TILES + 1], min_val=1, max_val=TILES // 2)
                    with pe.Fori(1, TILES // 2) as i:
                        with pe.If(i < pairs):
                            for j in range(2, 4):
                                gate_up(j, i - 1)
                                rows_turned(j + 1, i - 1)
                                down(j - 1, i - 1)
                                hidden_turned(j, i - 1)
                    down(1, pairs - 1)

                @block.scalar
                def _(act):
                    step = Steps(act, act_step)

                    def f(out, in_, func, **kw):
                        return nc.scalar.activation(out, in_, func, **kw)

                    def moved(instruction):
                        instruction.then_inc(act_moved, 1)

                    for dst, src in vector_loads(l):
                        act.dma_start(dst, src).then_inc(vectors_in, 16)
                    def root(t, before):
                        act.wait_ge(var_ready, before + t + 1)
                        f(st[:, 40 + t:41 + t], st[:, 13 + 2 * t:14 + 2 * t], ACT.Sqrt, bias=eps).then_inc(std_ready, 1)

                    for k in range(1, KD, 2):
                        ps = wait_filled(act, ("hT", k))
                        f(h3[:, k, 0:P], ps[:, 0:P], ACT.Identity, scale=mod3[:, 8 + k, 1:2], bias=mod3[:, k, 1:2])
                        moved(f(h3[:, k, P:TOK], ps[:, P:TOK], ACT.Identity, scale=mod3[:, 8 + k, 0:1], bias=mod3[:, k, 0:1]))
                    ps = wait_filled(act, ("lr",))
                    moved(f(tok2(lr[0:32, :]), ps2(ps)[0:32], ACT.Copy))
                    for c in range(2):
                        ps = wait_filled(act, ("aq", c))
                        moved(f(tok2(aqk[:, c, :]), ps2(ps), ACT.Copy, scale=DK ** -0.5))
                    wait_moved(act, ("vec",))
                    for c in range(4):
                        ps = wait_filled(act, ("z", c))
                        if c:
                            act.wait_ge(qk_ready, c)
                        f(tok2(bufA), ps2(ps), ACT.Abs, bias=vec[:, V_GB + c:V_GB + c + 1]).then_inc(abs_done, 1)
                        act.wait_ge(abs_done, c + 1)
                        step(f(bufA, bufA, ACT.Exp, scale=-1.0))
                        f(bufA, bufA, ACT.Ln, bias=1.0).then_inc(softplus, 1)
                        name, dst = ("vtok", vtok) if c < 2 else ("av", av)
                        for t in range(T):
                            ps = wait_filled(act, (name, c % 2, t))
                            moved(f(dst[:, t, 256 * (c % 2):256 * (c % 2 + 1)], ps[:, 0:256], ACT.Gelu_apprx_tanh if c < 2 else ACT.Copy))
                        act.wait_ge(decay_ready, c + 1)
                        f(bufA, bufB, ACT.Exp, scale=1.0 / GLA_TAU)
                        f(bufM, bufB, ACT.Exp, scale=-1.0 / GLA_TAU)
                        f(er[:, 15 * c:15 * c + 15], er[:, 15 * c:15 * c + 15], ACT.Exp, scale=1.0 / GLA_TAU).then_inc(exp_ready, 1)
                    for c in range(4):
                        ps = wait_filled(act, ("ag", c))
                        moved(f(tok2(br3[:, c, :]), ps2(ps), ACT.Silu))
                    act.wait_ge(var_ready, T)
                    f(st[:, 40:45], st[:, 12:22].rearrange("p (t v) -> p t v", v=2)[:, :, 1], ACT.Sqrt, bias=eps).then_inc(std_ready, 1)
                    for c in range(4):
                        ps = wait_filled(act, ("u", c))
                        moved(f(tok2(br3[:, 4 + c, :]), ps2(ps), ACT.Gelu_apprx_tanh))
                    ps = wait_filled(act, ("wsT",))
                    moved(f(wsT[:, :], ps[:, 0:512], ACT.Copy))
                    ps = wait_filled(act, ("kcT",))
                    moved(f(kcT.rearrange("p g t -> p (g t)"), ps[:, 0:512], ACT.Copy))
                    for c in range(4):
                        ps = wait_filled(act, ("ktok", c))
                        if c >= 2:
                            wait_filled(act, ("kv", c - 2))
                        moved(f(ktok[c % 2], ps[:, 0:TOK], ACT.Copy))
                    for p in range(PAIRS):
                        for t in range(T):
                            ps = wait_filled(act, ("o", p, t))
                            moved(f(oT[:, 2 * p:2 * p + 2, P * t:P * (t + 1)], ps.rearrange("p (j t) -> p j t", j=2)[:, :, 0:P], ACT.Copy))
                    def head_square(h):
                        if h >= 2:
                            act.wait_ge(bra_ready, h - 1)
                        f(sq[h % 2], oT[:, h, :], ACT.Square).then_inc(square_ready, 1)

                    def head_roots(heads):
                        for h in heads:
                            ps = wait_filled(act, ("ms", h))
                            step(f(tok2(sq[h % 2]), ps2(ps), ACT.Ln, scale=1.0 / DV, bias=eps))
                        for h in heads:
                            moved(f(sq[h % 2], sq[h % 2], ACT.Exp, scale=-0.5))

                    wait_moved(act, ("o", PAIRS - 1, T - 1))
                    head_square(0)
                    head_square(1)
                    act.wait_ge(kv_out, 16 * 6)
                    for i in range(UNITS + 2):
                        head_roots(heads_beside(i))
                        for head in heads_beside(i + 1):
                            if head >= 2:
                                head_square(head)
                        if i < UNITS:
                            n, h = divmod(i, HEADS)
                            ps = wait_filled(act, ("s", i))
                            act.wait_ge(negmax, i + 1)
                            if i >= 3:
                                wait_filled(act, ("pT", i - 3))
                            nm, rsum, es = (sm[:, 3 * a + i % 3:3 * a + i % 3 + 1] for a in range(3))
                            moved(f(pbuf[i % 3][:, 0:keys_of(n)], ps[:, 0:keys_of(n)], ACT.Exp, scale=HD ** -0.5, bias=nm, accum_out=rsum))
                            f(es, sink[:, h:h + 1], ACT.Exp, bias=nm).then_inc(esink, 1)
                        if i >= 2:
                            u = i - 2
                            n = u // HEADS
                            ps = wait_filled(act, ("pT", u))
                            if u >= 4:
                                wait_filled(act, ("pv", (u - 4) // 2))
                            moved(f(pTbuf[u % 4][:, 0:keys_of(n)], ps[:, 0:keys_of(n)], ACT.Copy))
                    m = 0
                    for half in range(2):
                        for n in range(3):
                            for q in range(4):
                                ps = wait_filled(act, ("gate", half, n, q))
                                if m >= 2:
                                    before = divmod(m - 2, 12)
                                    wait_moved(act, ("proj", before[0], before[1] // 4, before[1] % 4))
                                moved(f(tok2(sig[m % 2]), ps2(ps), ACT.Sigmoid))
                                m += 1
                    def logits_moved(t):
                        ps = wait_filled(act, ("lgT", t))
                        moved(f(lgT[:, P * t:P * (t + 1)], ps[0:LOGITS, 0:P], ACT.Copy))

                    for t in range(T + 2):
                        if t < T:
                            root(t, T)
                        if t >= 2:
                            u = t - 2
                            ps = wait_filled(act, ("h2T", u))
                            moved(f(h3[:, :, P * u:P * (u + 1)], ps.rearrange("p (k t) -> p k t", k=KD), ACT.Copy))
                        if t >= 3:
                            logits_moved(t - 3)
                    logits_moved(T - 1)
                    act.wait_ge(gexp_in, 1)
                    f(R["ge"], R["ge"], ACT.Exp).then_inc(gexp, 1)
                    act.wait_ge(gexp_in, 2)
                    f(R["dq"], R["dq"], ACT.Exp).then_inc(gexp, 1)
                    def silu_of(s, more):
                        ps = wait_filled(act, ("gu", s), more)
                        f(silu, ps[:, 0:FF], ACT.Silu).then_inc(silu_ready, 1)

                    def hidden_moved(s, more):
                        ps = wait_filled(act, ("ht", s), more)
                        moved(f(hidT[s % 2], ps[:, 0:2 * P].rearrange("p (f s) -> p f s", f=2), ACT.Copy))

                    def rows_stored(s, more, stores, tile):
                        ps = wait_filled(act, ("dn", s), more)
                        act.wait_ge(y_stored[s % 2], 16 * stores + 16)
                        moved(f(ys[s % 2], ps, ACT.Copy))
                        wait_moved(act, ("dn", s), moved_more)
                        act.dma_start(rows[bass.ds(P * tile, P), :], ys[s % 2]).then_inc(y_stored[s % 2], 16)

                    for s in range(2):
                        act.sem_inc(y_stored[s], 16)
                    moved_more = 0
                    silu_of(0, 0)
                    hidden_moved(0, 0)
                    silu_of(1, 0)
                    rows_stored(0, 0, 0, 0)
                    hidden_moved(1, 0)
                    pairs = act.value_load(exi[0:1, TILES:TILES + 1], min_val=1, max_val=TILES // 2)
                    with act.Fori(1, TILES // 2) as i:
                        with act.If(i < pairs):
                            more = 2 * PER_TILE * (i - 1)
                            moved_more = 4 * (i - 1)
                            for s in range(2):
                                silu_of(2 + s, more)
                                rows_stored(1 + s, more, i - 1 + s, 2 * i - 1 + s)
                                hidden_moved(2 + s, more)
                    moved_more = 4 * (pairs - 1)
                    rows_stored(1, 2 * PER_TILE * (pairs - 1) - 2, pairs - 1, 2 * pairs - 1)
                    for s in range(2):
                        act.wait_ge(y_stored[s], 16 * pairs + 16)
                    act.sem_inc(experts_done, 1)
                    for t in range(T + 1):
                        if t < T:
                            act.wait_ge(yg_in[t][0], 16)
                            if t >= 2:
                                act.wait_ge(yg_used, t - 1)
                            f(ysum[t % 2], yg[t][0], ACT.Copy, scale=R["w1"][:, t:t + 1]).then_inc(first_scaled, 1)
                        if t:
                            u = t - 1
                            root(u, 2 * T)
                            act.wait_ge(rs_ready, u + 1)
                            f(x3[:, u, :], x3[:, u, :], ACT.Identity, scale=st[:, 50 + u:51 + u], bias=st[:, 56 + u:57 + u])\
                                .then_inc(x_norm, 1)

                @block.vector
                def _(dve):
                    step = Steps(dve, dve_step)
                    V = nc.vector

                    def moved(instruction):
                        instruction.then_inc(dve_moved, 1)

                    def bc(ap, shape):
                        return ap.to_broadcast(shape)

                    def tt(out, a, b, op):
                        return V.tensor_tensor(out, a, b, op)

                    def stats(x, t, width):
                        parts = width // 512
                        for i in range(parts):
                            last = V.bn_stats(st[:, 6 * i:6 * i + 6], x[:, 512 * i:512 * (i + 1)])
                        step(last)
                        V.bn_aggr(st[:, 12 + 2 * t:14 + 2 * t], st[:, 0:6 * parts]).then_inc(var_ready, 1)
                        dve.wait_ge(var_ready, var_before + t + 1)

                    def normalise(x, t):
                        step(V.tensor_scalar(x, x, st[:, 12 + 2 * t:13 + 2 * t], st[:, 50 + t:51 + t], ALU.subtract, ALU.mult))

                    def one_hot(out, x, top, size):
                        o3 = out.rearrange("p (t g) -> p t g", t=T)
                        g3 = R["gx"].rearrange("p (t g) -> p t g", t=T)
                        step(tt(g3, x, bc(top.unsqueeze(2), [P, T, size]), ALU.is_equal))
                        step(tt(g3, g3, bc(cst("first").unsqueeze(1), [P, T, size]), ALU.mult))
                        step(V.tensor_reduce(R["gs"], g3, AXL.X, ALU.max))
                        step(tt(o3, g3, bc(R["gs"].unsqueeze(2), [P, T, size]), ALU.is_equal))

                    def modulation(b):
                        ps = wait_filled(dve, ("mod", b))
                        if b < MOD_FIRST:
                            moved(first_mod(b, ps))
                            return
                        vector, at = b // 4 - 2, 256 * (b % 4)
                        dst = late_rows[vector][:, at:at + 256]
                        if vector == 2:
                            moved(V.tensor_scalar(dst, ps[0:2, 0:256], 1.0, None, ALU.add))
                        else:
                            moved(V.tensor_copy(dst, ps[0:2, 0:256]))

                    for k in range(0, KD, 2):
                        ps = wait_filled(dve, ("hT", k))
                        V.tensor_scalar(h3[:, k, 0:P], ps[:, 0:P], mod3[:, 8 + k, 1:2], mod3[:, k, 1:2], ALU.mult, ALU.add)
                        moved(V.tensor_scalar(h3[:, k, P:TOK], ps[:, P:TOK], mod3[:, 8 + k, 0:1], mod3[:, k, 0:1], ALU.mult, ALU.add))
                    ps = wait_filled(dve, ("vec",))
                    moved(V.tensor_copy(vec[:, :], ps[:, 0:V_ROWS]))
                    wait_moved(dve, ("vec",))
                    for c in range(2):
                        ps = wait_filled(dve, ("ak", c))
                        moved(V.tensor_copy(tok2(aqk[:, 2 + c, :]), ps2(ps)))
                    for c in range(4):
                        d = c // 2
                        ps = wait_filled(dve, ("z", c))
                        dve.wait_ge(abs_done, c + 1)
                        moved(V.tensor_scalar(tok2(bufM), ps2(ps), vec[:, V_GB + c:V_GB + c + 1], 0.0, ALU.add, ALU.min))
                        wait_moved(dve, ("z", c))
                        dve.wait_ge(softplus, c + 1)
                        step(tt(bufM, bufM, bufA, ALU.subtract))
                        if d == 0:
                            step(V.tensor_tensor_scan(bufB, cst("run"), bufM, 0.0, ALU.mult, ALU.add))
                        else:
                            step(V.tensor_tensor_scan(bufB[:, ::-1], cst("run"), bufM[:, ::-1], 0.0, ALU.mult, ALU.add))
                        B3 = bufB.rearrange("p (t s) -> p t s", t=T)
                        e3 = er[:, 15 * c:15 * c + 15].rearrange("p (a t) -> p a t", a=3)
                        end = P - 1 if d == 0 else 0
                        step(V.tensor_copy(e3[:, 0, :], B3[:, :, P // 2]))
                        step(V.tensor_copy(e3[:, 2, :], B3[:, :, end]))
                        step(tt(e3[:, 1, :], e3[:, 2, :], e3[:, 0, :], ALU.subtract))
                        tt(B3, B3, bc(e3[:, 0, :].unsqueeze(2), [P, T, P]), ALU.subtract).then_inc(decay_ready, 1)
                        dve.wait_ge(exp_ready, c + 1)
                        tt(mg3[:, c, :], aqk[:, c % 2, :], bufA, ALU.mult)
                        tt(mg3[:, 4 + c, :], aqk[:, 2 + c % 2, :], bufM, ALU.mult).then_inc(qk_ready, 1)
                    wait_moved(dve, ("vtok", 1, T - 1))
                    var_before = 0
                    for t in range(T):
                        stats(vtok[:, t, :], t, 512)
                    dve.wait_ge(std_ready, 1)
                    step(V.reciprocal(st[:, 50:55], st[:, 40:45]))
                    ones_at = CONST["ones"][0]
                    V.tensor_copy(counting[:, :], const[:, ones_at:ones_at + 2 * P])
                    for t in range(T):
                        normalise(vtok[:, t, :], t)
                    dve.wait_ge(mixer_in, 16 * N_MIXER)
                    V.tensor_scalar(sink[:, HEADS:2 * HEADS], sink[:, 0:HEADS], -1.0, None, ALU.mult)
                    step(tt(vtok, vtok, bc(lng.unsqueeze(1), [P, T, 512]), ALU.mult))
                    tt(vtok, vtok, bc(lnb.unsqueeze(1), [P, T, 512]), ALU.add).then_inc(vn_ready, 1)
                    dve.wait_ge(vn_ready, 1)
                    for c in range(4):
                        ps = wait_filled(dve, ("cq", c))
                        moved(V.tensor_copy(tok2(br3[:, 8 + c, :]), ps2(ps)))
                    for t in range(T):
                        ps = wait_filled(dve, ("ckv", t))
                        moved(V.tensor_copy(kvt[:, t, :], ps[:, 0:256]))
                    for g in range(KV_HEADS):
                        ps = wait_filled(dve, ("kT", g))
                        moved(V.tensor_copy(kT[:, g, :], ps[:, 0:TOK]))
                    def rotated(c):
                        x = br3[:, 8 + c, P:TOK] if c < 4 else kT[:, c - 4, P:TOK]
                        ps = wait_filled(dve, ("rot", c))
                        moved(tt(tmp5[:, 0:4 * P], ps[:, 0:4 * P], cst("sin"), ALU.mult))
                        step(tt(x, x, cst("cos"), ALU.mult))
                        wait_moved(dve, ("rot", c))
                        tt(x, x, tmp5[:, 0:4 * P], ALU.add).then_inc(rope_ready, 1)
                        dve.wait_ge(rope_ready, c + 1)

                    for g in range(4):
                        ps = wait_filled(dve, ("mix", g))
                        bias = bc(bsb[:, P * g:P * (g + 1)].unsqueeze(1), [P, T, P])
                        moved(tt(tmp5.rearrange("p (t s) -> p t s", t=T), ps[:, 0:TOK].rearrange("p (t s) -> p t s", t=T), bias, ALU.add))
                        wait_moved(dve, ("mix", g))
                        wait_moved(dve, ("u", g))
                        tt(br3[:, 4 + g, :], br3[:, 4 + g, :], tmp5, ALU.mult).then_inc(brb_ready, 1)
                        dve.wait_ge(brb_ready, g + 1)
                    for c in range(4):
                        d = c // 2
                        e3 = er[:, 15 * c:15 * c + 15].rearrange("p (a t) -> p a t", a=3)
                        ps = wait_filled(dve, ("kv", c))
                        moved(tt(t1[:, c, :, :], ps[:, 0:TOK].rearrange("p (t v) -> p t v", t=T), bc(e3[:, 1, :].unsqueeze(2), [P, T, P]), ALU.mult))
                        wait_moved(dve, ("kv", c))
                        now, nxt = s0[:, c, :], spare
                        order = [1, 2, 3, 4] if d == 0 else [4, 3, 2, 1]
                        for n, t in enumerate(order):
                            if n < 3:
                                step(V.scalar_tensor_tensor(out=nxt, in0=now, scalar=e3[:, 2, t:t + 1], in1=t1[:, c, t, :],
                                                               op0=ALU.mult, op1=ALU.add))
                            last = V.tensor_scalar(t1[:, c, t, :], now, e3[:, 0, t:t + 1], None, ALU.mult)
                            if n < 3:
                                step(last)
                            now, nxt = nxt, now
                        last.then_inc(states_in, 1)
                        dve.wait_ge(states_in, c + 1)
                    mask = bc(cst("gla_mask").unsqueeze(1), [P, 2, 2 * P])
                    for p in range(PAIRS):
                        for t in range(T):
                            ps = wait_filled(dve, ("gs", p, t))
                            if t >= 2:
                                wait_filled(dve, ("o", p, t - 2))
                            elif p:
                                wait_filled(dve, ("o", p - 1, T - 1))
                            moved(tt(gsb[t % 2].rearrange("p (j c) -> p j c", j=2), ps.rearrange("p (j c) -> p j c", j=2)[:, :, 0:2 * P], mask, ALU.mult))
                            if rot_beside(p, t) is not None:
                                rotated(rot_beside(p, t))
                    def head_gated(h):
                        wait_moved(dve, ("ms", h))
                        wait_moved(dve, ("ag", h))
                        step(V.scalar_tensor_tensor(out=oT[:, h, :], in0=oT[:, h, :], scalar=vec[:, V_NORM + h:V_NORM + h + 1],
                                                       in1=sq[h % 2], op0=ALU.mult, op1=ALU.mult))
                        tt(br3[:, h, :], br3[:, h, :], oT[:, h, :], ALU.mult).then_inc(bra_ready, 1)

                    for i in range(UNITS + 3):
                        if i < UNITS:
                            n, h = divmod(i, HEADS)
                            ps = wait_filled(dve, ("s", i))
                            if i >= 3:
                                dve.wait_ge(esink, i - 2)
                            step(V.tensor_reduce(sm[:, 9 + i % 2:10 + i % 2], ps[:, 0:keys_of(n)], AXL.X, ALU.max))
                            V.tensor_scalar(sm[:, i % 3:i % 3 + 1], sm[:, 9 + i % 2:10 + i % 2], -(HD ** -0.5), sink[:, HEADS + h:HEADS + h + 1],
                                            ALU.mult, ALU.min).then_inc(negmax, 1)
                        if 1 <= i <= UNITS:
                            u = i - 1
                            dve.wait_ge(esink, u + 1)
                            step(tt(sm[:, 11:12], sm[:, 3 + u % 3:4 + u % 3], sm[:, 6 + u % 3:7 + u % 3], ALU.add))
                            step(V.reciprocal(sm[:, 12:13], sm[:, 11:12]))
                            if u >= 3:
                                wait_filled(dve, ("pT", u - 3))
                            V.tensor_scalar(diag[u % 3], ident, sm[:, 12:13], None, ALU.mult).then_inc(p_ready, 1)
                        for head in heads_beside(i - 1):
                            head_gated(head)
                        if i >= 4 and i % 2 == 0:
                            m = (i - 4) // 2
                            n, pair = divmod(m, HEADS // 2)
                            ps = wait_filled(dve, ("pv", m))
                            moved(V.tensor_copy(br3[:, 8 + pair, P * n:P * (n + 1)], ps[:, 0:P]))
                    m = 0
                    for half in range(2):
                        for n in range(3):
                            for q in range(4):
                                b = mod_beside(m)
                                row_sums(step, wait_block(dve, ("ada", b)), acc[b % 2]).then_inc(acc_ready, 1)
                                out = tok2(mg3[:, 4 * half + q, :])
                                ps = wait_filled(dve, ("proj", half, n, q))
                                wait_moved(dve, ("gate", half, n, q))
                                if n == 0:
                                    moved(tt(out, ps2(ps), tok2(sig[m % 2]), ALU.mult))
                                else:
                                    moved(tt(tok2(gtmp), ps2(ps), tok2(sig[m % 2]), ALU.mult))
                                    wait_moved(dve, ("proj", half, n, q))
                                    last = tt(out, out, tok2(gtmp), ALU.add)
                                    if n == 2:
                                        last.then_inc(merged, 1)
                                        dve.wait_ge(merged, 4 * half + q + 1)
                                    else:
                                        step(last)
                                modulation(b)
                                m += 1
                    wait_moved(dve, ("mod", MOD_FIRST - 1))
                    step(V.tensor_scalar(mod[:, 16:32], mod[:, 16:32], 1.0, None, ALU.add))
                    dve.wait_ge(merged, KD)
                    dve.wait_ge(x_back, 16)
                    dve.wait_ge(mod_rows_in, 16 * 6)
                    dve.wait_ge(ln_rows, 16 * 2)
                    var_before = T
                    for t in range(T + 1):
                        if t < T:
                            for cb in range(4):
                                cols = slice(256 * cb, 256 * (cb + 1))
                                ps = wait_filled(dve, ("y", t, cb))
                                moved(tt(ytmp, ps[:, 0:256], bcA[:, 0 if t == 0 else 1, cols], ALU.mult))
                                wait_moved(dve, ("y", t, cb))
                                step(V.scalar_tensor_tensor(out=x3[:, t, cols], in0=x3[:, t, cols], scalar=ALPHA, in1=ytmp,
                                                               op0=ALU.mult, op1=ALU.add))
                            stats(x3[:, t, :], t, D)
                        if t:
                            u = t - 1
                            dve.wait_ge(std_ready, 1 + u + 1)
                            step(V.reciprocal(st[:, 50 + u:51 + u], st[:, 40 + u:41 + u]))
                            normalise(x3[:, u, :], u)
                            step(tt(x3[:, u, :], x3[:, u, :], bcA[:, 2, :], ALU.mult))
                            tt(x3[:, u, :], x3[:, u, :], bcA[:, 3, :], ALU.add).then_inc(x1_done, 1)
                            c = 0 if u == 0 else 1
                            dve.wait_ge(x1_done, u + 1)
                            step(tt(h2[:, u, :], x3[:, u, :], bcB[:, c, :], ALU.mult))
                            tt(h2[:, u, :], h2[:, u, :], bcB[:, 2 + c, :], ALU.add).then_inc(h2_ready, 1)
                    ps = wait_filled(dve, ("logit",))
                    lg = R["lg"].rearrange("p (t c) -> p t c", t=T)
                    moved(tt(lg, ps[:, 0:32 * T].rearrange("p (t c) -> p t c", c=32)[:, :, 0:LOGITS],
                             bc(rb[:, :].unsqueeze(1), [P, T, LOGITS]), ALU.add))
                    wait_moved(dve, ("logit",))
                    ge = R["ge"].rearrange("p (t g) -> p t g", t=T)
                    step(V.tensor_reduce(R["gm"], lg[:, :, 0:NG], AXL.X, ALU.max))
                    tt(ge, lg[:, :, 0:NG], bc(R["gm"].unsqueeze(2), [P, T, NG]), ALU.subtract).then_inc(gexp_in, 1)
                    one_hot(R["G"], lg[:, :, 0:NG], R["gm"], NG)
                    G3 = R["G"].rearrange("p (t g) -> p t g", t=T)
                    big = R["big"].rearrange("p (t g e) -> p t g e", t=T, g=NG)
                    el = lg[:, :, NG:LOGITS].rearrange("p t (g e) -> p t g e", g=NG)
                    step(tt(big, el, bc(G3.unsqueeze(3), [P, T, NG, EG]), ALU.mult))
                    es3, e23 = (R[name].rearrange("p (t e) -> p t e", t=T) for name in ("es", "e2"))
                    step(V.tensor_reduce(es3, big.rearrange("p t g e -> p t e g"), AXL.X, ALU.add))
                    step(V.tensor_reduce(R["m1"], es3, AXL.X, ALU.max))
                    one_hot(R["E1"], es3, R["m1"], EG)
                    step(V.scalar_tensor_tensor(out=R["e2"], in0=R["E1"], scalar=-BIG, in1=R["es"], op0=ALU.mult, op1=ALU.add))
                    step(V.tensor_reduce(R["m2"], e23, AXL.X, ALU.max))
                    tt(R["dq"], R["m2"], R["m1"], ALU.subtract).then_inc(gexp_in, 1)
                    one_hot(R["E2"], e23, R["m2"], EG)
                    step(tt(R["big"][:, 0:T * EG], R["E1"], R["E2"], ALU.add))

                    def in_group(out, one):
                        e4 = one.rearrange("p (t e) -> p t e", t=T).unsqueeze(2)
                        return tt(out.rearrange("p (t g e) -> p t g e", t=T, g=NG), bc(G3.unsqueeze(3), [P, T, NG, EG]),
                                  bc(e4, [P, T, NG, EG]), ALU.mult)

                    in_group(chosen[:, :], R["big"][:, 0:T * EG]).then_inc(masks_ready, 1)
                    in_group(R["M1"], R["E1"])
                    step(in_group(R["M2"], R["E2"]))
                    ps = wait_filled(dve, ("rank",))
                    moved(V.tensor_copy(R["rk"], ps[:, 0:NE * (T + 1)]))
                    wait_moved(dve, ("rank",))
                    cmp3 = R["cmp"].rearrange("p (e j) -> p e j", e=NE)
                    step(tt(cmp3, bc(R["rk"][:, NE * T:NE * (T + 1)].unsqueeze(2), [P, NE, 5]), bc(cst("over").unsqueeze(1), [P, NE, 5]), ALU.is_gt))
                    step(V.tensor_reduce(R["nt"], cmp3, AXL.X, ALU.add))
                    step(V.tensor_tensor_scan(R["end"], cst("ones")[:, 0:NE], R["nt"], 0.0, ALU.mult, ALU.add))
                    step(tt(R["base"], R["end"], R["nt"], ALU.subtract))
                    step(V.tensor_scalar(R["base"], R["base"], float(P), None, ALU.mult))
                    rk3 = R["rk"][:, 0:NE * T].rearrange("p (t e) -> p t e", t=T)
                    step(tt(rk3, rk3, bc(R["base"].unsqueeze(1), [P, T, NE]), ALU.add))
                    pos3 = R["pos"].rearrange("p (t w) -> p t w", w=2)
                    for w, name in enumerate(("M1", "M2")):
                        m3 = R[name].rearrange("p (t e) -> p t e", t=T)
                        step(tt(m3, m3, rk3, ALU.mult))
                        step(V.tensor_reduce(pos3[:, :, w], m3, AXL.X, ALU.add))
                    V.tensor_copy(posi[:, :], R["pos"]).then_inc(places_ready, 1)
                    exc = R["exc"].rearrange("p (j e) -> p j e", j=TILES)
                    step(tt(exc, bc(cst("tile").unsqueeze(2), [P, TILES, NE]), bc(R["end"].unsqueeze(1), [P, TILES, NE]), ALU.is_ge))
                    step(V.tensor_reduce(R["ex"][:, 0:TILES], exc, AXL.X, ALU.add))
                    step(V.tensor_scalar(R["pairs"], cst("tile")[:, 0:TILES // 2], 2.0, R["end"][:, NE - 1:NE], ALU.mult, ALU.is_lt))
                    step(V.tensor_reduce(R["ex"][:, TILES:TILES + 1], R["pairs"], AXL.X, ALU.add))
                    V.tensor_scalar(exi[:, :], R["ex"], float(NE - 1), None, ALU.min).then_inc(route_ready, 1)
                    dve.wait_ge(gexp, 2)
                    step(V.tensor_reduce(R["gs"], ge, AXL.X, ALU.add))
                    step(V.reciprocal(R["gp"], R["gs"]))
                    step(V.tensor_scalar(R["gs"], R["dq"], 1.0, None, ALU.add))
                    step(V.reciprocal(R["gs"], R["gs"]))
                    step(tt(R["w1"], R["gp"], R["gs"], ALU.mult))
                    step(tt(R["w2"], R["w1"], R["dq"], ALU.mult))
                    def rows_moved(s, more):
                        ps = wait_filled(dve, ("xg", s), more)
                        moved(V.tensor_copy(xgT[s % 2], ps.rearrange("p (k s) -> p k s", k=KD)))

                    def hidden(s, more, tile):
                        ps = wait_filled(dve, ("gu", s), more)
                        dve.wait_ge(silu_ready, tile + 1)
                        moved(tt(hid, ps[:, FF:2 * FF], silu, ALU.mult))

                    rows_moved(0, 0)
                    for s in range(2):
                        hidden(s, 0, s)
                        rows_moved(s + 1, 0)
                    pairs = dve.value_load(exi[0:1, TILES:TILES + 1], min_val=1, max_val=TILES // 2)
                    with dve.Fori(1, TILES // 2) as i:
                        with dve.If(i < pairs):
                            more = 2 * PER_TILE * (i - 1)
                            for s in range(2):
                                hidden(2 + s, more, 2 * i + s)
                                rows_moved(3 + s, more)
                    var_before = 2 * T
                    dve.wait_ge(mod_rows_in, 16 * 8)
                    dve.wait_ge(ln_rows, 16 * 4)
                    for t in range(T):
                            x, out = x3[:, t, :], ysum[t % 2]
                            dve.wait_ge(first_scaled, t + 1)
                            dve.wait_ge(yg_in[t][1], 16)
                            step(V.scalar_tensor_tensor(out=out, in0=yg[t][1], scalar=R["w2"][:, t:t + 1], in1=out,
                                                        op0=ALU.mult, op1=ALU.add))
                            step(tt(out, out, bcA[:, 0 if t == 0 else 1, :], ALU.mult))
                            V.scalar_tensor_tensor(out=x, in0=x, scalar=ALPHA, in1=out, op0=ALU.mult, op1=ALU.add).then_inc(yg_used, 1)
                            dve.wait_ge(yg_used, t + 1)
                            stats(x, t, D)
                            dve.wait_ge(std_ready, 1 + T + t + 1)
                            step(V.reciprocal(st[:, 50 + t:51 + t], st[:, 40 + t:41 + t]))
                            V.scalar_tensor_tensor(out=st[:, 56 + t:57 + t], in0=st[:, 12 + 2 * t:13 + 2 * t], scalar=-1.0,
                                                   in1=st[:, 50 + t:51 + t], op0=ALU.mult, op1=ALU.mult).then_inc(rs_ready, 1)
                    dve.wait_ge(x_norm, T)
                    step(tt(x, x, bcA[:, 2, :], ALU.mult))
                    tt(x, x, bcA[:, 3, :], ALU.add).then_inc(x2_last, 1)

            nc.gpsimd.dma_reset()
            for semaphore in per_layer:
                nc.gpsimd.sem_clear(semaphore)
            nc.all_engine_barrier()


def launch_arrays(nc, arrays):
    A = {}
    for name, a in arrays.items():
        A[name] = nc.dram_tensor(f"in_{name}_dram", a.shape, mybir.dt.from_np(a.dtype), kind="ExternalInput").ap()
    for name, shape in _OUTS:
        A[name] = nc.dram_tensor(f"out_{name}_dram", shape, F32, kind="ExternalOutput").ap()
    A["mod_rows"] = nc.dram_tensor("mod_rows", (4, 2, D), F32, kind="Internal").ap()
    A["rows"] = nc.dram_tensor("rows", ((TILES + 1) * P, D), F32, kind="Internal").ap()
    return A




def kernel(**inputs):
    import concourse.bacc as _bacc
    from concourse.bass_utils import run_bass_kernel_spmd as _run

    arrays = {n: np.ascontiguousarray(inputs[n]) for n in _INS[2:]}
    arrays["x"] = np.concatenate([np.asarray(inputs["x_prompt"])[0], np.asarray(inputs["x_sample"])[0]], 0)
    arrays["const"] = const_tile()
    nc = _bacc.Bacc("TRN2", target_bir_lowering=False, num_devices=1)
    build_program(nc, launch_arrays(nc, arrays))
    r = _run(nc, [{f"in_{n}_dram": a for n, a in arrays.items()}], core_ids=[0]).results[0]
    y, state, k, v = (r[f"out_{n}_dram"] for n, _ in _OUTS)
    return (y[None, 0:P], y[None, P:TOK], state[None], k.reshape(1, DEPTH, P, KV_HEADS, HD), v.reshape(1, DEPTH, P, KV_HEADS, HD))
```
